# Optimizing a Trainium2 kernel written in Bass

```python
import math
import jax, jax.numpy as jnp
from jax import lax
import numpy as np

D_MODEL = 1024
BATCH = 1
SEQ = 1024
DEPTH = 2

CHUNK = 64
N_META = 16
S5_WIDTH = D_MODEL // 2
S5_GROUP = 16
S5_GROUPS = S5_WIDTH // S5_GROUP
S5_STATE = 64
S5_DT_MIN = 1e-3
S5_DT_MAX = 1e-1
DA_HEADS = 4
DA_HEAD_DIM = 64
DA_WIDTH = DA_HEADS * 2 * DA_HEAD_DIM
Q_BLOCK = 128
D_RNN = 1280
LRU_BLOCKS = 10
LRU_BLOCK_W = D_RNN // LRU_BLOCKS
CONV_WIDTH = 4
LRU_C = 8.0
N_GROUPS = 4
EXPERTS_PER_GROUP = 8
N_EXPERTS = N_GROUPS * EXPERTS_PER_GROUP
TOP_K_FINE = 2
D_EXPERT = 512
EXPERT_BLOCK = 128
ALPHA = (2 * DEPTH) ** 0.25
BETA = (8 * DEPTH) ** -0.25
LN_EPS = 1e-5
NEG_INF = -1e30

kernel_name = "hybrid_s5_diffattn_rglru_hmoe_block"

F32 = jnp.float32

def _layer_norm(z, g, b):
    zf = z.astype(F32)
    mu = jnp.mean(zf, -1, keepdims=True)
    var = jnp.mean(jnp.square(zf - mu), -1, keepdims=True)
    return (zf - mu) * lax.rsqrt(var + LN_EPS) * g.astype(F32) + b.astype(F32)

def _complex_linear_combine(e1, e2):
    a1r, a1i, b1r, b1i = e1
    a2r, a2i, b2r, b2i = e2
    return (a2r * a1r - a2i * a1i, a2r * a1i + a2i * a1r,
            a2r * b1r - a2i * b1i + b2r, a2r * b1i + a2i * b1r + b2i)

def _real_linear_combine(e1, e2):
    a1, b1 = e1
    a2, b2 = e2
    return (a2 * a1, a2 * b1 + b2)

def _s5(u, lam_re, lam_im, log_dt, b_re, b_im, c_re, c_im, d, w_glu, b_glu):
    bsz, L, _ = u.shape
    ug = u.reshape(bsz, L, S5_GROUPS, S5_GROUP)
    dt = jnp.exp(log_dt.astype(F32))[:, None]
    lr = jnp.minimum(lam_re.astype(F32), -1e-4)
    li = lam_im.astype(F32)
    mag = jnp.exp(lr * dt)
    ar = mag * jnp.cos(li * dt)
    ai = mag * jnp.sin(li * dt)
    den = lr * lr + li * li
    nr, ni = ar - 1.0, ai
    fr = ((nr * lr + ni * li) / den)[..., None]
    fi = ((ni * lr - nr * li) / den)[..., None]
    br, bi = b_re.astype(F32), b_im.astype(F32)
    bbr = fr * br - fi * bi
    bbi = fr * bi + fi * br
    bur = jnp.einsum('blgh,gph->blgp', ug, bbr)
    bui = jnp.einsum('blgh,gph->blgp', ug, bbi)
    a_r = jnp.broadcast_to(ar, (1, L, S5_GROUPS, S5_STATE))
    a_i = jnp.broadcast_to(ai, (1, L, S5_GROUPS, S5_STATE))
    _, _, hr, hi = lax.associative_scan(_complex_linear_combine, (a_r, a_i, bur, bui), axis=1)
    y = (jnp.einsum('blgp,ghp->blgh', hr, c_re.astype(F32))
         - jnp.einsum('blgp,ghp->blgh', hi, c_im.astype(F32)))
    y = y.reshape(bsz, L, S5_WIDTH) + d.astype(F32) * u
    y = jax.nn.gelu(y)
    return y * jax.nn.sigmoid(y @ w_glu.astype(F32) + b_glu.astype(F32))

def _diff_attention(q, k, v, lq1, lk1, lq2, lk2, subln_g, lam_init):
    bsz, L = q.shape[:2]
    Lp = -(-L // Q_BLOCK) * Q_BLOCK
    nqb = Lp // Q_BLOCK
    pad = Lp - L
    padw = lambda t: jnp.pad(t, ((0, 0), (0, pad)) + ((0, 0),) * (t.ndim - 2))
    q, k, v = padw(q), padw(k), padw(v)
    pos = jnp.arange(Lp)
    cid = jnp.where(pos < N_META, 0, 1 + (pos - N_META) // CHUNK)
    cid = jnp.where(pos < L, cid, Lp)
    lam = (jnp.exp(jnp.sum(lq1.astype(F32) * lk1.astype(F32)))
           - jnp.exp(jnp.sum(lq2.astype(F32) * lk2.astype(F32))) + lam_init)
    scale = DA_HEAD_DIM ** -0.5
    qb = q.reshape(bsz, nqb, Q_BLOCK, DA_HEADS, 2, DA_HEAD_DIM).transpose(1, 0, 2, 3, 4, 5)
    cqb = cid.reshape(nqb, Q_BLOCK)

    def block(args):
        q_blk, c_blk = args
        s = jnp.einsum('bqhcd,bkhcd->bchqk', q_blk, k) * scale
        mask = cid[None, :] <= c_blk[:, None]
        p = jax.nn.softmax(jnp.where(mask, s, NEG_INF), axis=-1)
        w = p[:, 0] - lam * p[:, 1]
        return jnp.einsum('bhqk,bkhe->bqhe', w, v)

    o = lax.map(block, (qb, cqb))
    o = o.transpose(1, 0, 2, 3, 4).reshape(bsz, Lp, DA_HEADS, 2 * DA_HEAD_DIM)[:, :L]
    o = o * lax.rsqrt(jnp.mean(o * o, -1, keepdims=True) + LN_EPS) * subln_g.astype(F32)
    return (o * (1.0 - lam_init)).reshape(bsz, L, DA_WIDTH)

def _s5_diffattn_mixer(h, w_in, lam_re, lam_im, log_dt, b_re, b_im, c_re, c_im, d, w_glu, b_glu,
                       lq1, lk1, lq2, lk2, subln_g, w_out, lam_init):
    bsz, L, _ = h.shape
    z = (h @ w_in).astype(F32)
    u = z[..., :S5_WIDTH]
    o = S5_WIDTH
    q = z[..., o:o + DA_WIDTH].reshape(bsz, L, DA_HEADS, 2, DA_HEAD_DIM)
    k = z[..., o + DA_WIDTH:o + 2 * DA_WIDTH].reshape(bsz, L, DA_HEADS, 2, DA_HEAD_DIM)
    v = z[..., o + 2 * DA_WIDTH:].reshape(bsz, L, DA_HEADS, 2 * DA_HEAD_DIM)
    y_s5 = _s5(u, lam_re, lam_im, log_dt, b_re, b_im, c_re, c_im, d, w_glu, b_glu)
    y_da = _diff_attention(q, k, v, lq1, lk1, lq2, lk2, subln_g, lam_init)
    return jnp.concatenate([y_s5, y_da], axis=-1) @ w_out.astype(F32)

def _rglru_mixer(h, w_in, conv_w, conv_b, w_a, b_a, w_x, b_x, lru_lambda, w_out):
    bsz, L, _ = h.shape
    z = (h @ w_in).astype(F32)
    gate_br, rec = z[..., :D_RNN], z[..., D_RNN:]
    rp = jnp.pad(rec, ((0, 0), (CONV_WIDTH - 1, 0), (0, 0)))
    cw = conv_w.astype(F32)
    xc = sum(rp[:, j:j + L] * cw[j] for j in range(CONV_WIDTH)) + conv_b.astype(F32)
    xb = xc.reshape(bsz, L, LRU_BLOCKS, LRU_BLOCK_W)
    r = jax.nn.sigmoid(jnp.einsum('blnd,nde->blne', xb, w_a.astype(F32))
                       + b_a.astype(F32).reshape(LRU_BLOCKS, LRU_BLOCK_W))
    ig = jax.nn.sigmoid(jnp.einsum('blnd,nde->blne', xb, w_x.astype(F32))
                        + b_x.astype(F32).reshape(LRU_BLOCKS, LRU_BLOCK_W))
    log_a = -LRU_C * r * jax.nn.softplus(-lru_lambda.astype(F32).reshape(LRU_BLOCKS, LRU_BLOCK_W))
    a = jnp.exp(log_a)
    bterm = jnp.sqrt(-jnp.expm1(2.0 * log_a)) * (ig * xb)
    _, hs = lax.associative_scan(_real_linear_combine, (a, bterm), axis=1)
    y = jax.nn.gelu(gate_br) * hs.reshape(bsz, L, D_RNN)
    return y @ w_out.astype(F32)

def _hier_moe(h, w_coarse, b_coarse, w_fine, b_fine, w_gate, w_up, w_down):
    bsz, L, d = h.shape
    x2 = h.reshape(-1, d)
    T = x2.shape[0]
    xf = x2.astype(F32)
    coarse = xf @ w_coarse.astype(F32) + b_coarse.astype(F32)
    p_coarse = jax.nn.softmax(coarse, axis=-1)
    grp = jnp.argmax(coarse, axis=-1)
    p_grp = jnp.take_along_axis(p_coarse, grp[:, None], axis=1)
    fine_all = jnp.einsum('td,gde->tge', xf, w_fine.astype(F32)) + b_fine.astype(F32)
    fine = jnp.take_along_axis(fine_all, grp[:, None, None], axis=1)[:, 0]
    top_v, top_i = lax.top_k(fine, TOP_K_FINE)
    gates = p_grp * jax.nn.softmax(top_v, axis=-1)
    experts = grp[:, None] * EXPERTS_PER_GROUP + top_i
    n_assign = T * TOP_K_FINE
    nb = -(-(n_assign + N_EXPERTS * (EXPERT_BLOCK - 1)) // EXPERT_BLOCK)
    e_flat = experts.reshape(-1)
    tok_flat = jnp.repeat(jnp.arange(T), TOP_K_FINE)
    g_flat = gates.reshape(-1)
    order = jnp.argsort(e_flat)
    e_s, tok_s, g_s = e_flat[order], tok_flat[order], g_flat[order]
    counts = jnp.bincount(e_flat, length=N_EXPERTS)
    padded = (counts + EXPERT_BLOCK - 1) // EXPERT_BLOCK * EXPERT_BLOCK
    pad_end = jnp.cumsum(padded)
    pad_start = pad_end - padded
    raw_start = jnp.cumsum(counts) - counts
    dest = pad_start[e_s] + jnp.arange(n_assign) - raw_start[e_s]
    slot_tok = jnp.full((nb * EXPERT_BLOCK,), T, jnp.int32).at[dest].set(tok_s)
    slot_gate = jnp.zeros((nb * EXPERT_BLOCK,), F32).at[dest].set(g_s)
    block_expert = jnp.minimum(
        jnp.searchsorted(pad_end, jnp.arange(nb) * EXPERT_BLOCK, side='right'), N_EXPERTS - 1)
    x_ext = jnp.concatenate([x2, jnp.zeros((1, d), x2.dtype)], axis=0)
    xb = x_ext[slot_tok].reshape(nb, EXPERT_BLOCK, d)

    def expert_block(args):
        xblk, e = args
        hid = jax.nn.silu(xblk @ w_gate[e]) * (xblk @ w_up[e])
        return hid @ w_down[e]

    yb = lax.map(expert_block, (xb, block_expert)).reshape(-1, d)
    y = jnp.zeros((T + 1, d), F32).at[slot_tok].add(yb.astype(F32) * slot_gate[:, None])
    return y[:T].reshape(bsz, L, d)

def setup_inputs(seed: int = 0) -> dict:
    key = jax.random.key(seed)
    keys = iter(jax.random.split(key, 64))
    nrm = lambda shape, scale: jax.random.normal(next(keys), shape, F32) * scale
    p = {}
    p['x'] = nrm((BATCH, SEQ, D_MODEL), 1.0)
    p['meta'] = nrm((N_META, D_MODEL), 1.0)

    def ln(prefix):
        p[prefix + '_g'] = 1.0 + nrm((D_MODEL,), 0.02)
        p[prefix + '_b'] = nrm((D_MODEL,), 0.02)

    def moe(prefix):
        p[prefix + '_w_coarse'] = nrm((D_MODEL, N_GROUPS), D_MODEL ** -0.5)
        p[prefix + '_b_coarse'] = nrm((N_GROUPS,), 0.01)
        p[prefix + '_w_fine'] = nrm((N_GROUPS, D_MODEL, EXPERTS_PER_GROUP), D_MODEL ** -0.5)
        p[prefix + '_b_fine'] = nrm((N_GROUPS, EXPERTS_PER_GROUP), 0.01)
        p[prefix + '_w_gate'] = nrm((N_EXPERTS, D_MODEL, D_EXPERT), D_MODEL ** -0.5)
        p[prefix + '_w_up'] = nrm((N_EXPERTS, D_MODEL, D_EXPERT), D_MODEL ** -0.5)
        p[prefix + '_w_down'] = nrm((N_EXPERTS, D_EXPERT, D_MODEL), D_EXPERT ** -0.5 * BETA)

    ln('l0_ln1')
    p['l0_w_in'] = nrm((D_MODEL, S5_WIDTH + 3 * DA_WIDTH), D_MODEL ** -0.5)
    p['l0_s5_lambda_re'] = -0.5 + nrm((S5_GROUPS, S5_STATE), 0.01)
    p['l0_s5_lambda_im'] = math.pi * jnp.arange(S5_STATE, dtype=F32)[None, :] + nrm((S5_GROUPS, S5_STATE), 0.01)
    p['l0_s5_log_dt'] = jax.random.uniform(next(keys), (S5_GROUPS,), F32, math.log(S5_DT_MIN), math.log(S5_DT_MAX))
    p['l0_s5_b_re'] = nrm((S5_GROUPS, S5_STATE, S5_GROUP), (2 * S5_GROUP) ** -0.5)
    p['l0_s5_b_im'] = nrm((S5_GROUPS, S5_STATE, S5_GROUP), (2 * S5_GROUP) ** -0.5)
    p['l0_s5_c_re'] = nrm((S5_GROUPS, S5_GROUP, S5_STATE), (2 * S5_STATE) ** -0.5)
    p['l0_s5_c_im'] = nrm((S5_GROUPS, S5_GROUP, S5_STATE), (2 * S5_STATE) ** -0.5)
    p['l0_s5_d'] = nrm((S5_WIDTH,), 1.0)
    p['l0_s5_w_glu'] = nrm((S5_WIDTH, S5_WIDTH), S5_WIDTH ** -0.5)
    p['l0_s5_b_glu'] = nrm((S5_WIDTH,), 0.02)
    p['l0_da_lq1'] = nrm((DA_HEAD_DIM,), 0.1)
    p['l0_da_lk1'] = nrm((DA_HEAD_DIM,), 0.1)
    p['l0_da_lq2'] = nrm((DA_HEAD_DIM,), 0.1)
    p['l0_da_lk2'] = nrm((DA_HEAD_DIM,), 0.1)
    p['l0_da_subln_g'] = 1.0 + nrm((2 * DA_HEAD_DIM,), 0.02)
    p['l0_w_out'] = nrm((S5_WIDTH + DA_WIDTH, D_MODEL), (S5_WIDTH + DA_WIDTH) ** -0.5 * BETA)
    ln('l0_ln2')
    moe('l0_moe')
    ln('l1_ln1')
    p['l1_w_in'] = nrm((D_MODEL, 2 * D_RNN), D_MODEL ** -0.5)
    p['l1_conv_w'] = nrm((CONV_WIDTH, D_RNN), CONV_WIDTH ** -0.5)
    p['l1_conv_b'] = nrm((D_RNN,), 0.02)
    p['l1_lru_w_a'] = nrm((LRU_BLOCKS, LRU_BLOCK_W, LRU_BLOCK_W), LRU_BLOCK_W ** -0.5)
    p['l1_lru_b_a'] = nrm((D_RNN,), 0.02)
    p['l1_lru_w_x'] = nrm((LRU_BLOCKS, LRU_BLOCK_W, LRU_BLOCK_W), LRU_BLOCK_W ** -0.5)
    p['l1_lru_b_x'] = nrm((D_RNN,), 0.02)
    a_c = jax.random.uniform(next(keys), (D_RNN,), F32, 0.9, 0.999)
    s = a_c ** (1.0 / LRU_C)
    p['l1_lru_lambda'] = jnp.log(s) - jnp.log1p(-s)
    p['l1_w_out'] = nrm((D_RNN, D_MODEL), D_RNN ** -0.5 * BETA)
    ln('l1_ln2')
    moe('l1_moe')
    return p

def reference(x, meta,
              l0_ln1_g, l0_ln1_b, l0_w_in, l0_s5_lambda_re, l0_s5_lambda_im, l0_s5_log_dt,
              l0_s5_b_re, l0_s5_b_im, l0_s5_c_re, l0_s5_c_im, l0_s5_d, l0_s5_w_glu, l0_s5_b_glu,
              l0_da_lq1, l0_da_lk1, l0_da_lq2, l0_da_lk2, l0_da_subln_g, l0_w_out,
              l0_ln2_g, l0_ln2_b, l0_moe_w_coarse, l0_moe_b_coarse, l0_moe_w_fine, l0_moe_b_fine,
              l0_moe_w_gate, l0_moe_w_up, l0_moe_w_down,
              l1_ln1_g, l1_ln1_b, l1_w_in, l1_conv_w, l1_conv_b, l1_lru_w_a, l1_lru_b_a,
              l1_lru_w_x, l1_lru_b_x, l1_lru_lambda, l1_w_out,
              l1_ln2_g, l1_ln2_b, l1_moe_w_coarse, l1_moe_b_coarse, l1_moe_w_fine, l1_moe_b_fine,
              l1_moe_w_gate, l1_moe_w_up, l1_moe_w_down):
    dt = x.dtype
    bsz = x.shape[0]
    h = jnp.concatenate([jnp.broadcast_to(meta[None].astype(dt), (bsz, N_META, D_MODEL)), x], axis=1)
    mixers = [
        (l0_w_in, l0_s5_lambda_re, l0_s5_lambda_im, l0_s5_log_dt, l0_s5_b_re, l0_s5_b_im,
         l0_s5_c_re, l0_s5_c_im, l0_s5_d, l0_s5_w_glu, l0_s5_b_glu,
         l0_da_lq1, l0_da_lk1, l0_da_lq2, l0_da_lk2, l0_da_subln_g, l0_w_out),
        (l1_w_in, l1_conv_w, l1_conv_b, l1_lru_w_a, l1_lru_b_a, l1_lru_w_x, l1_lru_b_x,
         l1_lru_lambda, l1_w_out),
    ]
    norms = [((l0_ln1_g, l0_ln1_b), (l0_ln2_g, l0_ln2_b)),
             ((l1_ln1_g, l1_ln1_b), (l1_ln2_g, l1_ln2_b))]
    moes = [(l0_moe_w_coarse, l0_moe_b_coarse, l0_moe_w_fine, l0_moe_b_fine,
             l0_moe_w_gate, l0_moe_w_up, l0_moe_w_down),
            (l1_moe_w_coarse, l1_moe_b_coarse, l1_moe_w_fine, l1_moe_b_fine,
             l1_moe_w_gate, l1_moe_w_up, l1_moe_w_down)]
    for i in range(DEPTH):
        if i % 2 == 0:
            lam_init = 0.8 - 0.6 * math.exp(-0.3 * i)
            mix = _s5_diffattn_mixer(h, *mixers[i], lam_init=lam_init)
        else:
            mix = _rglru_mixer(h, *mixers[i])
        h = _layer_norm(ALPHA * h + mix, *norms[i][0]).astype(dt)
        h = _layer_norm(ALPHA * h + _hier_moe(h, *moes[i]), *norms[i][1]).astype(dt)
    return h[:, N_META:]


_drawn_inputs = setup_inputs


def setup_inputs(seed=0):
    import zlib

    import numpy as np

    out = dict(_drawn_inputs(seed))
    spreads = {}
    factors = {'l0_s5_lambda_re': 64.0,
     'l0_s5_lambda_im': 43.312,
     'l0_s5_log_dt': 47.592,
     'l0_s5_b_re': 48.992,
     'l0_s5_b_im': 59.592,
     'l0_s5_c_re': 64.0,
     'l0_s5_c_im': 56.608,
     'l0_s5_b_glu': 200.0,
     'l0_da_lq1': 3.066,
     'l0_da_lk1': 3.877,
     'l0_da_lq2': 3.19,
     'l0_da_lk2': 5.28,
     'l0_da_subln_g': 19.942,
     'l0_moe_b_coarse': 34.636,
     'l0_moe_b_fine': 27.295,
     'l1_lru_b_a': 62.429,
     'l1_lru_b_x': 46.6,
     'l1_ln2_g': 23.993,
     'l1_ln2_b': 23.005,
     'l1_moe_b_coarse': 53.193,
     'l1_moe_b_fine': 22.263,
     'l0_s5_w_glu': 9.636}
    for name, (base, spread) in spreads.items():
        noise = np.random.default_rng([zlib.crc32(name.encode()), seed]).standard_normal(out[name].shape)
        drawn = base * np.exp(spread * noise) if base else spread * noise
        out[name] = __import__('jax').numpy.asarray(drawn.astype(out[name].dtype))
    for name, factor in factors.items():
        out[name] = (out[name] * factor).astype(out[name].dtype)
    return out
```

```python
from contextlib import ExitStack

import numpy as np
import concourse.bass as bass
from concourse import mybir

P = 128
F32 = mybir.dt.float32
I32 = mybir.dt.int32
U32 = mybir.dt.uint32
ALU = mybir.AluOpType
ACT = mybir.ActivationFunctionType
AX_X = mybir.AxisListType.X
ds = bass.ds

D = 1024
KD = D // P
N_META = 16
SEQ = 1024
T = N_META + SEQ
TILES = [(0, N_META)] + [(N_META + P * i, P) for i in range(SEQ // P)]
NT = len(TILES)
DEPTH = 2
ALPHA = (2 * DEPTH) ** 0.25
LN_EPS = 1e-5
S5W = 512
S5_STATES = 64
S5_PAIRS = 16
HEADS = 4
HEAD_DIM = 64
LAM_INIT = 0.2
NEG = -1e30
WIN = 104
NWIN = T // WIN
D_RNN = 1280
NB = D_RNN // P
GROUPS, PER_GROUP = 4, 8
NE = GROUPS * PER_GROUP
F = 512
CHUNKS = [(0, 352), (352, 352), (704, 336)]
TWO_PI = 6.283185307179586
PI_HI = 6.28125
PI_MID = 0.00193500518798828125
PI_LO = TWO_PI - PI_HI - PI_MID
ROUND_MAGIC = 12582912.0


class Place:

    def __init__(self, nc, start):
        self.nc, self.at = nc, start

    def __call__(self, name, shape, dt=F32):
        self.at = (self.at + 31) // 32 * 32
        t = self.nc.alloc_sbuf_tensor_at(name, [P] + shape, dt, offset=self.at)
        self.at += int(np.prod(shape)) * 4
        assert self.at <= self.nc.sbuf_usable_end, (name, self.at)
        return t


class Order:

    def __init__(self, eng, sem):
        self.eng, self.sem, self.base, self.k = eng, sem, 0, 0

    def __call__(self, ins, wait=True):
        self.k += 1
        ins.then_inc(self.sem, 1)
        if wait:
            self.wait()

    def wait(self):
        self.eng.wait_ge(self.sem, self.base + self.k)

    def enter(self, i, per):
        self.outer, self.per = self.base + self.k, per
        self.base, self.k = self.outer + i * per, 0

    def leave(self, count):
        assert self.k == self.per, (self.k, self.per)
        self.base, self.k = self.outer + count * self.per, 0


def bc(ap, n):
    return ap.unsqueeze(2).to_broadcast([ap.shape[0], ap.shape[1], n])


def make_constants(nc, K):
    made = K.sem("identity_made")
    with nc.Block() as block:
        @block.gpsimd
        def _(pool):
            pool.memset(K.ident[:], 0.0).then_inc(made, 1)
            pool.wait_ge(made, 1)
            pool.affine_select(out=K.ident[:], in_=K.ident[:], compare_op=ALU.not_equal, fill=1.0, base=0,
                               pattern=[[-1, P]], channel_multiplier=1).then_inc(made, 1)
            pool.wait_ge(made, 2)


def s5_prepare(nc, K, A):
    at = Place(nc, K.free_zt)
    small = {n: at("s5_" + n, [S5_PAIRS]) for n in (
        "lre", "lim", "dt", "lr", "xr", "ph", "n", "r", "rc", "ai", "ar", "nr", "den", "a", "b", "fr", "fi")}
    S = lambda n: small[n][:]
    b_re, b_im = at("s5_bre", [S5_PAIRS, 16]), at("s5_bim", [S5_PAIRS, 16])
    bd_re, bd_im = at("s5_bdre", [S5_PAIRS, 32]), at("s5_bdim", [S5_PAIRS, 32])
    c_re, c_im = at("s5_cre", [4, P]), at("s5_cim", [4, P])
    t1, t2 = at("s5_t1", [S5_PAIRS, 64]), at("s5_t2", [S5_PAIRS, 64])
    m1, m2 = at("s5_m1", [2, S5_PAIRS]), at("s5_m2", [2, S5_PAIRS])
    zeroed, loaded = K.sem("s5_zeroed"), K.sem("s5_loaded")
    dve_order, act_done = K.sem("s5p_dve_order"), K.sem("s5p_act_done")
    pe_done, ready = K.sem("s5p_pe_done"), K.sem("s5p_ready")
    asked = K.sem("s5p_asked")
    N_LOADS = 5 + 2 + 16
    with nc.psum_tensor("s5p_ps", [P, 4, 512], F32) as ps, nc.Block() as block:
        @block.sync
        def _(sp):
            with nc.allow_non_contiguous_dma(reason="small parameters"):
                sp.dma_start(small["lre"][:], A["l0_s5_lambda_re"].rearrange("(s two) p -> (two p) s", two=2)).then_inc(loaded, 16)
                sp.dma_start(small["lim"][:], A["l0_s5_lambda_im"].rearrange("(s two) p -> (two p) s", two=2)).then_inc(loaded, 16)
                dt = A["l0_s5_log_dt"].rearrange("(s two) -> two s", two=2)
                for two in range(2):
                    sp.dma_start(small["dt"][64 * two:64 * two + 64, :], dt[two:two + 1, :].to_broadcast([64, S5_PAIRS])).then_inc(loaded, 16)
                sp.dma_start(K.s5_d[:], A["l0_s5_d"].rearrange("(t p) -> p t", p=P)).then_inc(loaded, 16)
                sp.dma_start(b_re[:], A["l0_s5_b_re"].rearrange("(s two) p h -> (two p) s h", two=2)).then_inc(loaded, 16)
                sp.dma_start(b_im[:], A["l0_s5_b_im"].rearrange("(s two) p h -> (two p) s h", two=2)).then_inc(loaded, 16)
                sp.wait_ge(zeroed, 4)
                for j in range(8):
                    for c, src in ((c_re, "l0_s5_c_re"), (c_im, "l0_s5_c_im")):
                        sp.dma_start(c[16 * j:16 * j + 16, :, 64 * (j % 2):64 * (j % 2) + 64],
                                     A[src].rearrange("(t j) h p -> j h t p", j=8)[j]).then_inc(loaded, 16)

        @block.gpsimd
        def _(pool):
            for t in (bd_re, bd_im, c_re, c_im, K.b_lhs):
                pool.memset(t[:], 0.0).then_inc(zeroed, 1)

        @block.vector
        def _(dve):
            do = Order(dve, dve_order)
            tt, tsc = dve.tensor_tensor, dve.tensor_scalar
            dve.wait_ge(loaded, 16 * N_LOADS)
            do(tsc(S("lr"), S("lre"), -1e-4, None, ALU.min))
            dve.wait_ge(act_done, 1)
            do(tt(S("xr"), S("lr"), S("dt"), ALU.mult), wait=False)
            do(tt(S("ph"), S("lim"), S("dt"), ALU.mult))
            do(tsc(S("n"), S("ph"), 1.0 / TWO_PI, ROUND_MAGIC, ALU.mult, ALU.add))
            do(tsc(S("n"), S("n"), -ROUND_MAGIC, None, ALU.add))
            do(dve.scalar_tensor_tensor(out=S("r"), in0=S("n"), scalar=-PI_HI, in1=S("ph"), op0=ALU.mult, op1=ALU.add))
            do(dve.scalar_tensor_tensor(out=S("r"), in0=S("n"), scalar=-PI_MID, in1=S("r"), op0=ALU.mult, op1=ALU.add))
            do(dve.scalar_tensor_tensor(out=S("r"), in0=S("n"), scalar=-PI_LO, in1=S("r"), op0=ALU.mult, op1=ALU.add))
            do(tsc(S("r"), S("r"), 3.1415925, -3.1415925, ALU.min, ALU.max))
            do(tsc(S("rc"), S("r"), -1.0, None, ALU.mult))
            do(tt(S("rc"), S("rc"), S("r"), ALU.min))
            do(tsc(S("rc"), S("rc"), TWO_PI / 4, None, ALU.add), wait=False)
            dve.memset(K.cs[:, :, 0:1], 1.0).then_inc(asked, 1)
            dve.memset(K.sn[:, :, 0:1], 0.0).then_inc(asked, 1)
            dve.wait_ge(asked, 2)
            dve.wait_ge(act_done, 4)
            c1, s1 = K.cs[:, :, 1], K.sn[:, :, 1]
            do(tt(S("ar"), K.mag[:], c1, ALU.mult), wait=False)
            do(tt(S("ai"), K.mag[:], s1, ALU.mult))
            do(tsc(S("nr"), S("ar"), -1.0, None, ALU.add), wait=False)
            do(tt(S("a"), S("lr"), S("lr"), ALU.mult), wait=False)
            do(tt(S("b"), S("lim"), S("lim"), ALU.mult))
            do(tt(S("den"), S("a"), S("b"), ALU.add))
            do(dve.reciprocal(S("den"), S("den")), wait=False)
            do(tt(S("a"), S("nr"), S("lr"), ALU.mult), wait=False)
            do(tt(S("b"), S("ai"), S("lim"), ALU.mult))
            do(tt(S("fr"), S("a"), S("b"), ALU.add))
            do(tt(S("a"), S("ai"), S("lr"), ALU.mult), wait=False)
            do(tt(S("b"), S("nr"), S("lim"), ALU.mult), wait=False)
            do(tt(S("fr"), S("fr"), S("den"), ALU.mult))
            do(tt(S("fi"), S("a"), S("b"), ALU.subtract))
            do(tt(S("fi"), S("fi"), S("den"), ALU.mult))
            fr, fi = bc(S("fr"), 16), bc(S("fi"), 16)
            do(tt(t1[:, :, 0:16], fr, b_re[:], ALU.mult), wait=False)
            do(tt(t1[:, :, 16:32], fi, b_im[:], ALU.mult), wait=False)
            do(tt(t1[:, :, 32:48], fr, b_im[:], ALU.mult), wait=False)
            do(tt(t1[:, :, 48:64], fi, b_re[:], ALU.mult))
            dve.wait_ge(zeroed, 4)
            for g in range(2):
                rows = slice(64 * g, 64 * g + 64)
                do(tt(bd_re[rows, :, 16 * g:16 * g + 16], t1[rows, :, 0:16], t1[rows, :, 16:32], ALU.subtract))
                do(tt(bd_im[rows, :, 16 * g:16 * g + 16], t1[rows, :, 32:48], t1[rows, :, 48:64], ALU.add))
            dve.memset(K.s5_zero[:], 0.0).then_inc(ready, 1)
            do(dve.tensor_copy(m1[:, 0, :], c1), wait=False)
            do(dve.tensor_copy(m1[:, 1, :], s1))
            cur, nxt, m, have = m1, m2, 1, 2
            while have < WIN + 1:
                do(tt(t1[:, :, 0], cur[:, 0, :], cur[:, 0, :], ALU.mult), wait=False)
                do(tt(t1[:, :, 1], cur[:, 1, :], cur[:, 1, :], ALU.mult), wait=False)
                do(tt(t1[:, :, 2], cur[:, 0, :], cur[:, 1, :], ALU.mult))
                do(tt(nxt[:, 0, :], t1[:, :, 0], t1[:, :, 1], ALU.subtract), wait=False)
                do(tt(nxt[:, 1, :], t1[:, :, 2], t1[:, :, 2], ALU.add))
                cur, nxt, m = nxt, cur, 2 * m
                n = min(m, WIN + 1 - m)
                cm, sm = bc(cur[:, 0, :], n), bc(cur[:, 1, :], n)
                cj, sj = K.cs[:, :, 0:n], K.sn[:, :, 0:n]
                do(tt(t1[:, :, 0:n], cj, cm, ALU.mult), wait=False)
                do(tt(t2[:, :, 0:n], sj, sm, ALU.mult))
                do(tt(K.cs[:, :, m:m + n], t1[:, :, 0:n], t2[:, :, 0:n], ALU.subtract))
                do(tt(t1[:, :, 0:n], sj, cm, ALU.mult), wait=False)
                do(tt(t2[:, :, 0:n], cj, sm, ALU.mult))
                do(tt(K.sn[:, :, m:m + n], t1[:, :, 0:n], t2[:, :, 0:n], ALU.add))
                have = m + n
            dve.wait_ge(pe_done, 1)
            dve.wait_ge(zeroed, 5)
            for s in range(4):
                rows = slice(32 * s, 32 * s + 32)
                for c in range(2):
                    do(dve.tensor_copy(K.b_lhs[rows, c, :, s, :], ps[rows, c, :].rearrange("p (t c) -> p t c", t=4)), wait=False)
            do(dve.tensor_copy(K.c_lhs[:, 0, :, :], ps[:, 2, :].rearrange("p (t c) -> p t c", t=4)), wait=False)
            do(tsc(K.c_lhs[:, 1, :, :], ps[:, 3, :].rearrange("p (t c) -> p t c", t=4), -1.0, None, ALU.mult))

        @block.scalar
        def _(act):
            act.wait_ge(loaded, 16 * N_LOADS)
            act.activation(S("dt"), S("dt"), ACT.Exp).then_inc(act_done, 1)
            act.wait_ge(dve_order, 3)
            act.activation(K.mag[:], S("xr"), ACT.Exp).then_inc(act_done, 1)
            act.wait_ge(dve_order, 12)
            act.wait_ge(asked, 2)
            act.activation(K.cs[:, :, 1], S("rc"), ACT.Sin).then_inc(act_done, 1)
            act.activation(K.sn[:, :, 1], S("r"), ACT.Sin).then_inc(act_done, 1)

        @block.tensor
        def _(pe):
            pe.wait_ge(ready, 1)
            for c, src in enumerate((bd_re, bd_im)):
                for t in range(4):
                    pe.transpose(ps[:, c, P * t:P * t + P], src[:, 4 * t:4 * t + 4, :].rearrange("p s h -> p (s h)"), K.ident[:])
            pe.wait_ge(loaded, 16 * N_LOADS)
            for c, src in enumerate((c_re, c_im)):
                for t in range(4):
                    last = pe.transpose(ps[:, 2 + c, P * t:P * t + P], src[:, t, :], K.ident[:])
            last.then_inc(pe_done, 1)


def s5_and_projections(nc, K, A):
    at = Place(nc, K.free_loop)
    w_in = at("w_in", [KD, 2048])
    rows_sb = at("h_rows", [D])
    hT = at("hT_window", [KD, WIN])
    uW = at("u_window", [4, WIN])
    q4 = [4, WIN]
    rot = [at(f"s5_rot{i}", q4) for i in range(6)]
    g = [[at(f"s5_g{b}{c}", q4) for c in range(2)] for b in range(2)]
    h = [[at(f"s5_h{b}{c}", q4) for c in range(2)] for b in range(2)]
    pt = [at(f"s5_pt{i}", q4) for i in range(4)]
    init = at("s5_init", [2, S5_PAIRS])
    ca = at("s5_carry", [4, 4])
    yT, zT = K.yT, K.zT
    sem = lambda n: K.sem("s5_" + n)
    w_loaded, rows_loaded, rows_used, hT_ready = [sem(f"w_loaded{c}") for c in range(4)], sem("rows_loaded"), sem("rows_used"), sem("hT_ready")
    u_ready, u_copied, bu_ready, bu_used = sem("u_ready"), sem("u_copied"), sem("bu_ready"), sem("bu_used")
    z_ready, z_copied, g_ready, h_ready = sem("z_ready"), sem("z_copied"), sem("g_ready"), sem("h_ready")
    y_ready, y_used, dve_order, pool_order = sem("y_ready"), sem("y_used"), sem("dve_order"), sem("pool_order")
    x, meta, w = A["x"].rearrange("a b d -> (a b) d"), A["meta"], A["l0_w_in"].rearrange("(k p) c -> p k c", p=P)
    with ExitStack() as ctx:
        psum = lambda n: ctx.enter_context(nc.psum_tensor(n, [P, 512], F32))
        p_u = psum("p_u")
        p_z = [psum(f"p_z{i}") for i in range(2)]
        p_b = [[psum(f"p_b{b}{c}") for c in range(2)] for b in range(2)]
        p_y = psum("p_y")
        v4 = lambda t: t[:, 0:4 * WIN].rearrange("p (s w) -> p s w", s=4)
        block = ctx.enter_context(nc.Block())

        @block.sync
        def _(sp):
            sp.dma_start(rows_sb[0:N_META, :], meta).then_inc(rows_loaded, 16)
            sp.dma_start(rows_sb[N_META:WIN, :], x[0:WIN - N_META, :]).then_inc(rows_loaded, 16)
            for c in range(4):
                sp.dma_start(w_in[:, :, 512 * c:512 * c + 512], w[:, :, 512 * c:512 * c + 512]).then_inc(w_loaded[c], 16)
            with sp.Fori(1, NWIN) as i:
                sp.wait_ge(rows_used, i)
                sp.dma_start(rows_sb[0:WIN, :], x[ds(i * WIN - N_META, WIN), :]).then_inc(rows_loaded, 16)

        def pe_window(pe, w, first):
            pe.wait_ge(rows_loaded, 16 * (w + 2))
            if not first:
                pe.wait_ge(z_copied, 4 * w)
            for k in range(KD):
                last = pe.transpose(p_z[k // 4][:, WIN * (k % 4):WIN * (k % 4) + WIN], rows_sb[0:WIN, P * k:P * k + P], K.ident[0:WIN, 0:WIN])
            last.then_inc(rows_used, 1)
            pe.wait_ge(hT_ready, 2 * (w + 1))
            if first:
                pe.wait_ge(w_loaded[0], 16)
            for t in range(4):
                for k in range(KD):
                    last = pe.matmul(p_u[:, WIN * t:WIN * t + WIN], w_in[:, k, P * t:P * t + P], hT[:, k, :], start=k == 0, stop=k == KD - 1)
            last.then_inc(u_ready, 1)
            for q in range(4):
                step = 4 * w + q
                if not first or q >= 2:
                    pe.wait_ge(z_copied, step - 1)
                for j in range(3):
                    f = S5W + P * (3 * q + j)
                    if first:
                        pe.wait_ge(w_loaded[f // 512], 16)
                    for k in range(KD):
                        last = pe.matmul(p_z[q % 2][:, WIN * j:WIN * j + WIN], w_in[:, k, f:f + P], hT[:, k, :], start=k == 0, stop=k == KD - 1)
                last.then_inc(z_ready, 1)
                if q == 0:
                    pe.wait_ge(u_copied, 2 * (w + 1))
                if not first or q >= 2:
                    pe.wait_ge(bu_used, step - 1)
                for c in range(2):
                    for s in range(4):
                        last = pe.matmul(p_b[q % 2][c][:, WIN * s:WIN * s + WIN], K.b_lhs[:, c, q, s, :], uW[:, q, :], start=True, stop=True)
                last.then_inc(bu_ready, 1)
                if not first or q >= 2:
                    y_product(pe, step - 2, q, not first or q > 2)

        def y_product(pe, step, q, wait):
            pe.wait_ge(h_ready, step + 1)
            if wait:
                pe.wait_ge(y_used, step)
            for s in range(4):
                for c in range(2):
                    last = pe.matmul(p_y[32 * s:32 * s + 32, 0:WIN], K.c_lhs[:, c, (q - 2) % 4, 32 * s:32 * s + 32],
                                     h[q % 2][c][:, s, :], start=c == 0, stop=c == 1)
            last.then_inc(y_ready, 1)

        @block.tensor
        def _(pe):
            pe_window(pe, 0, True)
            with pe.Fori(1, NWIN) as i:
                pe_window(pe, i, False)
            for q in range(2):
                y_product(pe, 4 * NWIN - 2 + q, q, True)

        def act_window(act, w):
            col = ds(w * WIN, WIN)
            act.wait_ge(rows_used, w + 1)
            for i in range(2):
                act.copy(hT[:, 4 * i:4 * i + 4, :], v4(p_z[i])).then_inc(hT_ready, 1)
            act.wait_ge(u_ready, w + 1)
            act.copy(uW[:], v4(p_u)).then_inc(u_copied, 1)
            act.copy(yT[:, :, col], v4(p_u)).then_inc(u_copied, 1)
            for q in range(4):
                act.wait_ge(z_ready, 4 * w + q + 1)
                act.copy(zT[:, 3 * q:3 * q + 3, col], p_z[q % 2][:, 0:3 * WIN].rearrange("p (j w) -> p j w", j=3)).then_inc(z_copied, 1)

        @block.scalar
        def _(act):
            with act.Fori(0, NWIN) as i:
                act_window(act, i)

        def y_add(dve, step, q, w):
            dve.wait_ge(y_ready, step + 1)
            f = (q - 2) % 4
            cols = yT[:, f, ds((w if q >= 2 else w - 1) * WIN, WIN)]
            dve.scalar_tensor_tensor(out=cols, in0=cols, scalar=K.s5_d[:, f:f + 1], in1=p_y[:, 0:WIN],
                                     op0=ALU.mult, op1=ALU.add).then_inc(y_used, 1)

        def dve_window(dve, do, w, first):
            tt = dve.tensor_tensor
            for q in range(4):
                step = 4 * w + q
                cj, sj = K.cs[:, 4 * q:4 * q + 4, 0:WIN], K.sn[:, 4 * q:4 * q + 4, 0:WIN]
                br, bi = v4(p_b[q % 2][0]), v4(p_b[q % 2][1])
                dve.wait_ge(bu_ready, step + 1)
                do(tt(rot[0][:], br, cj, ALU.mult), wait=False)
                do(tt(rot[1][:], bi, sj, ALU.mult), wait=False)
                do(tt(rot[2][:], bi, cj, ALU.mult), wait=False)
                tt(rot[3][:], br, sj, ALU.mult).then_inc(bu_used, 1)
                dve.wait_ge(bu_used, step + 1)
                do(tt(rot[4][:], rot[0][:], rot[1][:], ALU.add), wait=False)
                do(tt(rot[5][:], rot[2][:], rot[3][:], ALU.subtract))
                if not first or q >= 2:
                    dve.wait_ge(h_ready, step - 1)
                for s in range(4):
                    n = 4 * q + s
                    for c in range(2):
                        scan = dve.tensor_tensor_scan(g[q % 2][c][:, s, :], K.mag[:, n:n + 1].to_broadcast([P, WIN]), rot[4 + c][:, s, :],
                                                      K.s5_zero[:] if first else init[:, c, n:n + 1], ALU.mult, ALU.add)
                        if s == 3 and c == 1:
                            scan.then_inc(g_ready, 1)
                        else:
                            do(scan, wait=False)
                dve.wait_ge(g_ready, step + 1)
                ge = [g[q % 2][c][:, :, WIN - 1] for c in range(2)]
                cw, sw = K.cs[:, 4 * q:4 * q + 4, WIN], K.sn[:, 4 * q:4 * q + 4, WIN]
                do(tt(ca[:, 0, :], ge[0], cw, ALU.mult), wait=False)
                do(tt(ca[:, 1, :], ge[1], sw, ALU.mult), wait=False)
                do(tt(ca[:, 2, :], ge[0], sw, ALU.mult), wait=False)
                do(tt(ca[:, 3, :], ge[1], cw, ALU.mult))
                do(tt(init[:, 0, 4 * q:4 * q + 4], ca[:, 0, :], ca[:, 1, :], ALU.subtract), wait=False)
                do(tt(init[:, 1, 4 * q:4 * q + 4], ca[:, 2, :], ca[:, 3, :], ALU.add))
                if not first or q >= 2:
                    y_add(dve, step - 2, q, w)

        @block.vector
        def _(dve):
            do = Order(dve, dve_order)
            dve.wait_ge(u_copied, 2)
            dve_window(dve, do, 0, True)
            per = do.k
            with dve.Fori(1, NWIN) as i:
                do.enter(i - 1, per)
                dve_window(dve, do, i, False)
                do.leave(NWIN - 1)
            for q in range(2):
                y_add(dve, 4 * NWIN - 2 + q, q, NWIN)
            dve.wait_ge(y_used, 4 * NWIN)

        def pool_window(pool, do, w, first):
            tt = pool.tensor_tensor
            for q in range(4):
                step = 4 * w + q
                cj, sj = K.cs[:, 4 * q:4 * q + 4, 0:WIN], K.sn[:, 4 * q:4 * q + 4, 0:WIN]
                gr, gi = g[q % 2][0][:], g[q % 2][1][:]
                if not first or q:
                    pool.wait_ge(h_ready, step)
                pool.wait_ge(g_ready, step + 1)
                do(tt(pt[0][:], gr, cj, ALU.mult), wait=False)
                do(tt(pt[1][:], gi, sj, ALU.mult), wait=False)
                do(tt(pt[2][:], gr, sj, ALU.mult), wait=False)
                do(tt(pt[3][:], gi, cj, ALU.mult))
                if not first or q >= 2:
                    pool.wait_ge(y_ready, step - 1)
                do(tt(h[q % 2][0][:], pt[0][:], pt[1][:], ALU.subtract), wait=False)
                tt(h[q % 2][1][:], pt[2][:], pt[3][:], ALU.add).then_inc(h_ready, 1)

        @block.gpsimd
        def _(pool):
            do = Order(pool, pool_order)
            pool_window(pool, do, 0, True)
            per = do.k
            with pool.Fori(1, NWIN) as i:
                do.enter(i - 1, per)
                pool_window(pool, do, i, False)
                do.leave(NWIN - 1)


def s5_gate(nc, K, A):
    at = Place(nc, K.free_loop)
    gT, w_glu, b_glu, gate = at("glu_g", [4, T]), at("w_glu", [4, S5W]), at("b_glu", [4]), at("glu_gate", [2, T])
    sem = lambda n: K.sem("glu_" + n)
    loaded, gelu_done, lin_ready, gate_ready, out_done = sem("loaded"), sem("gelu_done"), sem("lin_ready"), sem("gate_ready"), sem("out_done")
    yT = K.yT
    with nc.psum_tensor("p_glu", [P, 2, 3, 512], F32) as ps, nc.Block() as block:
        @block.sync
        def _(sp):
            sp.dma_start(w_glu[:], A["l0_s5_w_glu"].rearrange("(k p) c -> p k c", p=P)).then_inc(loaded, 16)
            with nc.allow_non_contiguous_dma(reason="a bias by partition"):
                sp.dma_start(b_glu[:], A["l0_s5_b_glu"].rearrange("(t p) -> p t", p=P)).then_inc(loaded, 16)

        @block.scalar
        def _(act):
            for k in range(4):
                act.activation(gT[:, k, :], yT[:, k, :], ACT.Gelu_apprx_tanh).then_inc(gelu_done, 1)
            act.wait_ge(loaded, 32)
            for f in range(4):
                act.wait_ge(lin_ready, f + 1)
                if f >= 2:
                    act.wait_ge(out_done, f - 1)
                for j, (o, n) in enumerate(CHUNKS):
                    act.activation(gate[:, f % 2, o:o + n], ps[:, f % 2, j, 0:n], ACT.Sigmoid, bias=b_glu[:, f:f + 1]).then_inc(gate_ready, 1)

        @block.tensor
        def _(pe):
            pe.wait_ge(loaded, 32)
            pe.wait_ge(gelu_done, 4)
            for f in range(4):
                if f >= 2:
                    pe.wait_ge(gate_ready, 3 * (f - 1))
                for j, (o, n) in enumerate(CHUNKS):
                    for k in range(4):
                        last = pe.matmul(ps[:, f % 2, j, 0:n], w_glu[:, k, P * f:P * f + P], gT[:, k, o:o + n], start=k == 0, stop=k == 3)
                last.then_inc(lin_ready, 1)

        @block.vector
        def _(dve):
            for f in range(4):
                dve.wait_ge(gate_ready, 3 * (f + 1))
                dve.tensor_tensor(yT[:, f, :], gT[:, f, :], gate[:, f % 2, :], ALU.mult).then_inc(out_done, 1)
            dve.wait_ge(out_done, 4)


def attention(nc, K, A):
    at = Place(nc, K.free_loop)
    K.daT = at("daT", [HEADS, T])
    K.free_da = at.at
    low, top = Place(nc, K.free_s5), Place(nc, K.h_at)
    qh, kh, vh = ([low(f"{x}_head{i}", [T]) for i in range(2)] for x in "qkv")
    v_rows = low("v_rows", [NT, P])
    probs = [[top(f"prob{b}{c}", [T]) for c in range(2)] for b in range(2)]
    w = low("w_rows", [T])
    tail_sb = at("scores_tail_sb", [2, N_META])
    mx2, l2 = at("row_max2", [2]), at("row_sum2", [2, 2])
    wT = at("w_cols", [NT, P])
    hide, ones = at("hide", [P]), at("ones64", [64])
    lq = [at(f"lq{i}", [HEAD_DIM]) for i in range(4)]
    ldot, lexp, nlam = at("ldot", [2]), at("lexp", [2]), at("nlam", [1])
    prod = at("lprod", [HEAD_DIM])
    mx, nb, r, nl = at("row_max", [2]), at("row_bias", [2]), at("row_rec", [2]), at("row_nl", [1])
    sums = [at(f"row_sum{b}", [2]) for b in range(2)]
    assert at.at <= K.w_out0_at and low.at <= K.free_zt
    o_sb, sq = top("o_rows", [NT, 512]), top("o_sq", [2 * P])
    ss, rs, g = top("o_ss", [NT * HEADS]), top("o_rs", [NT * HEADS]), top("subln", [1])
    zT, scale = K.zT, HEAD_DIM ** -0.5
    sem = lambda n: K.sem("da_" + n)
    (loaded, hide_made, lam_ready, staged, s_ready, nb_ready, exp_done, w_ready, tp_ready, tp_copied, o_ready, o_copied,
     dve_order, lexp_done, tp_clear, met, tail_done) = map(sem, (
        "loaded", "hide_made", "lam_ready", "staged", "s_ready", "nb_ready", "exp_done", "w_ready", "tp_ready",
        "tp_copied", "o_ready", "o_copied", "dve_order", "lexp_done", "tp_clear", "met", "tail_done"))
    GRP = [i // 4 + 1 for i in range(NT)]
    TP0 = 3
    TPH = TP0 + sum(GRP)
    WIDE = 1024
    tp_at = lambda qi: TP0 + sum(GRP[:qi])
    with ExitStack() as ctx:
        S = [ctx.enter_context(nc.psum_tensor(f"scores{c}", [P, WIDE], F32)) for c in range(2)]
        tail = ctx.enter_context(nc.psum_tensor("scores_tail", [P, 2, N_META], F32))
        tps = [ctx.enter_context(nc.psum_tensor(f"tp{i}", [P, 4, P], F32)) for i in range(2)]
        po = ctx.enter_context(nc.psum_tensor("po", [P, 512], F32))
        block = ctx.enter_context(nc.Block())

        @block.sync
        def _(sp):
            with nc.allow_non_contiguous_dma(reason="small parameters"):
                for i, n in enumerate(("lq1", "lk1", "lq2", "lk2")):
                    sp.dma_start(lq[i][:], A["l0_da_" + n].rearrange("(a d) -> a d", a=1).to_broadcast([P, HEAD_DIM])).then_inc(loaded, 16)
                sp.dma_start(g[:], A["l0_da_subln_g"].rearrange("(p a) -> p a", a=1)).then_inc(loaded, 16)
            load_w_out(sp, K, 0)

        @block.gpsimd
        def _(pool):
            pool.memset(hide[:], 0.0).then_inc(hide_made, 1)
            pool.memset(ones[:], 1.0).then_inc(hide_made, 1)
            pool.wait_ge(hide_made, 2)
            for c in range(2):
                pool.memset(hide[64 * c:64 * c + 1, 0:64], NEG).then_inc(hide_made, 1)
            pool.wait_ge(hide_made, 4)
            for hd in range(HEADS):
                if hd >= 2:
                    pool.wait_ge(o_ready, (hd - 1) * NT)
                for kind, t in enumerate((qh, kh, vh)):
                    pool.tensor_copy(t[hd % 2][:], zT[:, HEADS * kind + hd, :]).then_inc(staged, 1)

        def scores(pe, hd, par, qi):
            q0, m = TILES[qi]
            n = q0 + m
            cuts = list(range(0, n, 512)) + [n]

            def columns(c, a, b):
                r = slice(64 * c, 64 * c + 64)
                place = lambda a, b: S[c][0:m, a:b] if a < WIDE else tail[0:m, c, a - WIDE:b - WIDE]
                lo = max(a, n - 64) if qi else b
                if lo > a:
                    last = pe.matmul(place(a, min(lo, b)), qh[par][r, q0:q0 + m], kh[par][r, a:min(lo, b)], start=True, stop=True)
                if lo < b:
                    pe.matmul(place(lo, b), qh[par][r, q0:q0 + m], kh[par][r, lo:b], start=True, stop=False)
                    last = pe.matmul(place(lo, b), hide[r, 0:m], ones[r, 0:b - lo], start=False, stop=True)
                return last

            if n > WIDE:
                for c in range(2):
                    columns(c, WIDE, n).then_inc(tail_done, 1)
                    if c == 0:
                        pe.wait_ge(tail_done, 2 * hd + 1)
            for c in range(2):
                if qi == 0:
                    pe.wait_ge(exp_done, 1 + hd * NT * 2)
                    pe.sem_inc(met, 1)
                else:
                    pe.wait_ge(exp_done, 1 + (hd * NT + qi) * 2 + c - 1)
                for a, b in zip(cuts, cuts[1:]):
                    if a < WIDE:
                        last = columns(c, a, b)
                last.then_inc(s_ready, 1)

        def weigh(pe, hd, par, qi):
            q0, m = TILES[qi]
            pe.wait_ge(w_ready, 1 + hd * NT + qi + 1)
            for gq in range(GRP[qi]):
                pe.wait_ge(tp_copied, 1 + hd * TPH + tp_at(qi) + gq - 1)
                tp = tps[(par * TPH + tp_at(qi) + gq) % 2]
                if qi == 0:
                    pe.sem_inc(met, 1)
                for kt in range(4 * gq, min(4 * gq + 4, qi + 1)):
                    k0, kk = TILES[kt]
                    last = pe.transpose(tp[0:kk, kt % 4, 0:m], w[0:m, k0:k0 + kk], K.ident[0:m, 0:m])
                last.then_inc(tp_ready, 1)
            pe.wait_ge(tp_copied, 1 + hd * TPH + tp_at(qi) + GRP[qi])
            pe.wait_ge(o_copied, 1 + hd * NT + qi)
            if qi == 0:
                pe.sem_inc(met, 1)
            for kt in range(qi + 1):
                kk = TILES[kt][1]
                last = pe.matmul(po[0:m, 0:P], wT[0:kk, kt, 0:m], v_rows[0:kk, kt, :], start=kt == 0, stop=kt == qi)
            last.then_inc(o_ready, 1)

        @block.tensor
        def _(pe):
            pe.sem_inc(tp_ready, 1)
            pe.wait_ge(hide_made, 4)
            pe.wait_ge(tp_clear, 2)
            def head(hd, par):
                pe.wait_ge(staged, 3 * hd + 3)
                vs = vh[par]
                for gv in range(TP0):
                    pe.wait_ge(tp_copied, 1 + hd * TPH + gv)
                    tp = tps[(par * TPH + gv) % 2]
                    for kt in range(4 * gv, min(4 * gv + 4, NT)):
                        k0, kk = TILES[kt]
                        last = pe.transpose(tp[0:kk, kt % 4, :], vs[:, k0:k0 + kk], K.ident[:])
                    last.then_inc(tp_ready, 1)
                for qi in range(NT):
                    if qi == 0:
                        scores(pe, hd, par, 0)
                    if qi + 1 < NT:
                        scores(pe, hd, par, qi + 1)
                    weigh(pe, hd, par, qi)

            with pe.Fori(0, HEADS // 2) as i:
                for par in range(2):
                    head(2 * i + par, par)

        def exps(act, hd, qi, c):
            q0, m = TILES[qi]
            n = q0 + m
            if c == 0:
                act.wait_ge(w_ready, 1 + hd * NT + qi - 1)
            act.wait_ge(nb_ready, (hd * NT + qi) * 2 + c + 1)
            prob, kw = probs[qi % 2][c], dict(bias=nb[0:m, c:c + 1], scale=scale)
            if n <= WIDE:
                act.activation(prob[0:m, 0:n], S[c][0:m, 0:n], ACT.Exp, accum_out=sums[qi % 2][0:m, c:c + 1], **kw).then_inc(exp_done, 1)
            else:
                act.activation(prob[0:m, 0:WIDE], S[c][0:m, :], ACT.Exp, accum_out=l2[0:m, c, 0:1], **kw)
                act.activation(prob[0:m, WIDE:n], tail_sb[0:m, c, :], ACT.Exp, accum_out=l2[0:m, c, 1:2], **kw).then_inc(exp_done, 1)

        def copies(act, hd, par, qi):
            m = TILES[qi][1]
            for gq in range(GRP[qi]):
                act.wait_ge(tp_ready, 1 + hd * TPH + tp_at(qi) + gq + 1)
                tp = tps[(par * TPH + tp_at(qi) + gq) % 2]
                n = min(4, qi + 1 - 4 * gq)
                act.copy(wT[:, 4 * gq:4 * gq + n, 0:m], tp[:, 0:n, 0:m]).then_inc(tp_copied, 1)

        @block.scalar
        def _(act):
            act.sem_inc(tp_copied, 1)
            act.sem_inc(exp_done, 1)
            act.wait_ge(lam_ready, 2)
            act.activation(lexp[:], ldot[:], ACT.Exp).then_inc(lexp_done, 1)
            def head(hd, par):
                for gv in range(TP0):
                    act.wait_ge(tp_ready, 1 + hd * TPH + gv + 1)
                    n = min(4, NT - 4 * gv)
                    act.copy(v_rows[:, 4 * gv:4 * gv + n, :], tps[(par * TPH + gv) % 2][:, 0:n, :]).then_inc(tp_copied, 1)
                for qi in range(NT):
                    if qi == 0:
                        exps(act, hd, 0, 0)
                        exps(act, hd, 0, 1)
                    if qi + 1 < NT:
                        exps(act, hd, qi + 1, 0)
                    copies(act, hd, par, qi)
                    if qi + 1 < NT:
                        exps(act, hd, qi + 1, 1)

            with act.Fori(0, HEADS // 2) as i:
                for par in range(2):
                    head(2 * i + par, par)

        def maxima(dve, do, hd, qi):
            q0, m = TILES[qi]
            n = q0 + m
            for c in range(2):
                dve.wait_ge(s_ready, (hd * NT + qi) * 2 + c + 1)
                if n <= WIDE:
                    do(dve.tensor_reduce(mx[0:m, c:c + 1], S[c][0:m, 0:n], AX_X, ALU.max))
                else:
                    if c == 0:
                        do(dve.tensor_copy(tail_sb[0:m, :, :], tail[0:m, :, :]))
                    do(dve.tensor_reduce(mx2[0:m, 0:1], S[c][0:m, :], AX_X, ALU.max), wait=False)
                    do(dve.tensor_reduce(mx2[0:m, 1:2], tail_sb[0:m, c, :], AX_X, ALU.max))
                    do(dve.tensor_reduce(mx[0:m, c:c + 1], mx2[0:m, :], AX_X, ALU.max))
                dve.tensor_scalar(nb[0:m, c:c + 1], mx[0:m, c:c + 1], -scale, None, ALU.mult).then_inc(nb_ready, 1)

        def combine(dve, do, hd, qi):
            q0, m = TILES[qi]
            n = q0 + m
            dve.wait_ge(exp_done, 1 + (hd * NT + qi) * 2 + 2)
            prob, l = probs[qi % 2], sums[qi % 2]
            if n > WIDE:
                do(dve.tensor_reduce(l[0:m, :], l2[0:m, :, :], AX_X, ALU.add))
            do(dve.reciprocal(r[0:m, :], l[0:m, :]))
            do(dve.tensor_tensor(nl[0:m, :], r[0:m, 1:2], nlam[0:m, :], ALU.mult))
            do(dve.tensor_scalar(prob[1][0:m, 0:n], prob[1][0:m, 0:n], nl[0:m, 0:1], None, ALU.mult))
            dve.wait_ge(tp_ready, 1 + hd * TPH + tp_at(qi))
            dve.scalar_tensor_tensor(out=w[0:m, 0:n], in0=prob[0][0:m, 0:n], scalar=r[0:m, 0:1], in1=prob[1][0:m, 0:n],
                                     op0=ALU.mult, op1=ALU.add).then_inc(w_ready, 1)

        def out_copy(dve, hd, qi):
            m = TILES[qi][1]
            dve.wait_ge(o_ready, hd * NT + qi + 1)
            dve.tensor_copy(o_sb[0:m, qi, ds(hd * P, P)], po[0:m, 0:P]).then_inc(o_copied, 1)

        @block.vector
        def _(dve):
            do = Order(dve, dve_order)
            dve.sem_inc(w_ready, 1)
            dve.sem_inc(o_copied, 1)
            for tp in tps:
                dve.memset(tp[:], 0.0).then_inc(tp_clear, 1)
            do(dve.memset(o_sb[:, 0, :], 0.0))
            dve.wait_ge(loaded, 80)
            dve.tensor_tensor_reduce(prod[:], lq[0][:], lq[1][:], 1.0, 0.0, ALU.mult, ALU.add, ldot[:, 0:1]).then_inc(lam_ready, 1)
            dve.wait_ge(lam_ready, 1)
            dve.tensor_tensor_reduce(prod[:], lq[2][:], lq[3][:], 1.0, 0.0, ALU.mult, ALU.add, ldot[:, 1:2]).then_inc(lam_ready, 1)
            dve.wait_ge(lexp_done, 1)
            do(dve.tensor_tensor(nlam[:], lexp[:, 1:2], lexp[:, 0:1], ALU.subtract))
            do(dve.tensor_scalar(nlam[:], nlam[:], -LAM_INIT, None, ALU.add))
            def head(hd):
                for qi in range(NT):
                    if qi == 0:
                        maxima(dve, do, hd, 0)
                    combine(dve, do, hd, qi)
                    if qi:
                        out_copy(dve, hd, qi - 1)
                    if qi + 1 < NT:
                        maxima(dve, do, hd, qi + 1)
                out_copy(dve, hd, NT - 1)

            with dve.Fori(0, HEADS // 2) as i:
                do.enter(i, 2 * (5 * NT + 6))
                for par in range(2):
                    head(2 * i + par)
                do.leave(HEADS // 2)
            dve.wait_ge(o_copied, 1 + HEADS * NT)

    with nc.psum_tensor("p_oT", [P, 2, 4, P], F32) as ps, nc.Block() as block:
        ms_ready, sd_ready, on_ready, oT_ready, oT_copied, g_ready = map(sem, ("ms_ready", "sd_ready", "on_ready", "oT_ready", "oT_copied", "g_ready"))
        order2 = sem("dve_order2")

        @block.vector
        def _(dve):
            do = Order(dve, order2)
            do(dve.tensor_scalar(g[:], g[:], 1.0 - LAM_INIT, None, ALU.mult), wait=False)
            for i in range(NT):
                for h in range(HEADS):
                    o = o_sb[:, i, P * h:P * h + P]
                    do(dve.tensor_tensor_reduce(sq[:, P * ((HEADS * i + h) % 2):P * ((HEADS * i + h) % 2) + P], o, o, 1.0, 0.0, ALU.mult, ALU.add, ss[:, HEADS * i + h:HEADS * i + h + 1]), wait=h == HEADS - 1 or h == 1)
            dve.tensor_scalar(ss[:], ss[:], 1.0 / P, LN_EPS, ALU.mult, ALU.add).then_inc(ms_ready, 1)
            dve.wait_ge(sd_ready, 1)
            do(dve.reciprocal(rs[:], rs[:]))
            ov = o_sb[:].rearrange("p i (h e) -> p (i h) e", h=HEADS)
            for i in range(NT):
                v = ov[:, HEADS * i:HEADS * i + HEADS, :]
                dve.tensor_tensor(v, v, bc(rs[:, HEADS * i:HEADS * i + HEADS], P), ALU.mult).then_inc(on_ready, 1)
            dve.wait_ge(on_ready, NT)

        @block.scalar
        def _(act):
            act.wait_ge(ms_ready, 1)
            act.activation(rs[:], ss[:], ACT.Sqrt).then_inc(sd_ready, 1)
            act.wait_ge(order2, 1)
            for i in range(NT):
                q0, m = TILES[i]
                act.wait_ge(oT_ready, i + 1)
                act.mul(K.daT[:, :, q0:q0 + m], ps[:, i % 2, :, 0:m], g[:, 0:1]).then_inc(oT_copied, 1)

        @block.tensor
        def _(pe):
            for i in range(NT):
                q0, m = TILES[i]
                pe.wait_ge(on_ready, i + 1)
                if i >= 2:
                    pe.wait_ge(oT_copied, i - 1)
                for h in range(HEADS):
                    last = pe.transpose(ps[:, i % 2, h, 0:m], o_sb[0:m, i, P * h:P * h + P], K.ident[0:m, 0:m])
                last.then_inc(oT_ready, 1)


def load_rows(eng, buf, source, i, sem):
    m = TILES[i][1]
    eng.dma_start(buf[0:m, :], source(i)).then_inc(sem, 16)


class Norm:

    def __init__(self, nc, K, name, at):
        self.K, self.nc = K, nc
        self.st, self.mv, self.ve, self.sd, self.rs = (at(f"{name}_{n}", [w]) for n, w in (
            ("stats", 12), ("mean_var", 2), ("var_eps", 1), ("dev", 1), ("rec_dev", 1)))
        self.gain, self.bias = at(name + "_gain", [D]), at(name + "_bias", [D])
        self.var_ready, self.dev_ready, self.xn_ready, self.gained, self.h_ready, self.params = (
            K.sem(f"{name}_{n}") for n in ("var_ready", "dev_ready", "xn_ready", "gained", "h_ready", "params"))

    def load(self, sp, gain, bias):
        for t, src in ((self.gain, gain), (self.bias, bias)):
            sp.dma_start(t[:], src.rearrange("(a d) -> a d", a=1).to_broadcast([P, D])).then_inc(self.params, 16)

    def dve(self, dve, do, i):
        m = TILES[i][1]
        z = self.K.H[0:m, i, :]
        for j in range(2):
            do(dve.bn_stats(self.st[0:m, 6 * j:6 * j + 6], z[:, 512 * j:512 * j + 512]), wait=j == 1)
        do(dve.bn_aggr(self.mv[0:m, :], self.st[0:m, :]))
        dve.tensor_scalar(self.ve[0:m, :], self.mv[0:m, 1:2], LN_EPS, None, ALU.add).then_inc(self.var_ready, 1)
        dve.wait_ge(self.dev_ready, i + 1)
        do(dve.reciprocal(self.rs[0:m, :], self.sd[0:m, :]))
        dve.tensor_scalar(z, z, self.mv[0:m, 0:1], self.rs[0:m, 0:1], ALU.subtract, ALU.mult).then_inc(self.xn_ready, 1)
        dve.wait_ge(self.xn_ready, i + 1)

    def act(self, act, i):
        m = TILES[i][1]
        act.wait_ge(self.var_ready, i + 1)
        act.activation(self.sd[0:m, :], self.ve[0:m, :], ACT.Sqrt).then_inc(self.dev_ready, 1)

    def pool(self, pool, i):
        m = TILES[i][1]
        z = self.K.H[0:m, i, :]
        if i == 0:
            pool.wait_ge(self.params, 32)
        pool.wait_ge(self.xn_ready, i + 1)
        pool.tensor_tensor(z, z, self.gain[0:m, :], ALU.mult).then_inc(self.gained, 1)
        pool.wait_ge(self.gained, i + 1)
        pool.tensor_tensor(z, z, self.bias[0:m, :], ALU.add).then_inc(self.h_ready, 1)


def load_w_out(sp, K, layer):
    w, loaded = K.w_out[layer], K.w_out_loaded[layer]
    src = K.A[f"l{layer}_w_out"].rearrange("(k p) c -> p k c", p=P)
    for c in range(2):
        sp.dma_start(w[:, :, 512 * c:512 * c + 512], src[:, :, 512 * c:512 * c + 512]).then_inc(loaded, 16)


def project_and_norm(nc, K, A, layer, slices, at, residual):
    L = f"l{layer}"
    ns = len(slices)
    res = [at(f"{L}_res{i}", [D]) for i in range(2)]
    hT, wr, rb = at(L + "_h1T", [KD, P]), at(L + "_w_router", [KD, 36]), at(L + "_b_router", [36])
    norm = Norm(nc, K, L + "_ln1", at)
    sem = lambda n: K.sem(f"{L}_out_{n}")
    w_out, w_loaded = K.w_out[layer], K.w_out_loaded[layer]
    r_loaded, res_loaded = sem("r_loaded"), [sem("res_loaded0"), sem("res_loaded1")]
    o_ready, z_done, order, turned, hT_ready, lg_ready, lg_done, stored = map(sem, (
        "o_ready", "z_done", "order", "turned", "hT_ready", "lg_ready", "lg_done", "stored"))
    with ExitStack() as ctx:
        po = [[ctx.enter_context(nc.psum_tensor(f"{L}_po{b}{h}", [P, 512], F32)) for h in range(2)] for b in range(2)]
        pt = [ctx.enter_context(nc.psum_tensor(f"{L}_pt{h}", [P, 4, P], F32)) for h in range(2)]
        pl = ctx.enter_context(nc.psum_tensor(f"{L}_pl", [P, 36], F32))
        block = ctx.enter_context(nc.Block())

        @block.sync
        def _(sp):
            norm.load(sp, A[L + "_ln1_g"], A[L + "_ln1_b"])
            with nc.allow_non_contiguous_dma(reason="router weights"):
                sp.dma_start(wr[:, :, 0:GROUPS], A[L + "_moe_w_coarse"].rearrange("(k p) g -> p k g", p=P)).then_inc(r_loaded, 16)
                for g in range(GROUPS):
                    c = GROUPS + PER_GROUP * g
                    sp.dma_start(wr[:, :, c:c + PER_GROUP], A[L + "_moe_w_fine"][g].rearrange("(k p) e -> p k e", p=P)).then_inc(r_loaded, 16)
                sp.dma_start(rb[:, 0:GROUPS], A[L + "_moe_b_coarse"].rearrange("(a g) -> a g", a=1).to_broadcast([P, GROUPS])).then_inc(r_loaded, 16)
                sp.dma_start(rb[:, GROUPS:36], A[L + "_moe_b_fine"].rearrange("(a g) e -> a (g e)", a=1).to_broadcast([P, NE])).then_inc(r_loaded, 16)
            for i in range(NT):
                if i >= 2:
                    sp.wait_ge(z_done, 2 * (i - 1))
                load_rows(sp, res[i % 2], residual, i, res_loaded[i % 2])
            for i in range(NT):
                t0, m = TILES[i]
                sp.wait_ge(norm.h_ready, i + 1)
                sp.dma_start(K.h1_dram[t0:t0 + m, :], K.H[0:m, i, :]).then_inc(stored, 16)
            sp.wait_ge(stored, 16 * NT)

        @block.tensor
        def _(pe):
            pe.wait_ge(w_loaded, 32)
            for i in range(NT + 1):
                if i < NT:
                    t0, m = TILES[i]
                    if i >= 2:
                        pe.wait_ge(z_done, 2 * (i - 1))
                    for h in range(2):
                        for k, y in enumerate(slices):
                            last = pe.matmul(po[i % 2][h][0:m, :], y[:, t0:t0 + m], w_out[:, k, 512 * h:512 * h + 512], start=k == 0, stop=k == ns - 1)
                        last.then_inc(o_ready, 1)
                if i >= 1:
                    m = TILES[i - 1][1]
                    pe.wait_ge(norm.h_ready, i)
                    for k in range(KD):
                        last = pe.transpose(pt[k // 4][:, k % 4, 0:m], K.H[0:m, i - 1, P * k:P * k + P], K.ident[0:m, 0:m])
                    last.then_inc(turned, 1)
                    if i == 1:
                        pe.wait_ge(r_loaded, 7 * 16)
                    pe.wait_ge(hT_ready, 2 * i)
                    if i >= 2:
                        pe.wait_ge(lg_done, i - 1)
                    for k in range(KD):
                        last = pe.matmul(pl[0:m, :], hT[:, k, 0:m], wr[:, k, :], start=k == 0, stop=k == KD - 1)
                    last.then_inc(lg_ready, 1)

        @block.scalar
        def _(act):
            for i in range(NT + 1):
                if i < NT:
                    norm.act(act, i)
                if i >= 1:
                    m = TILES[i - 1][1]
                    act.wait_ge(turned, i)
                    for h in range(2):
                        act.copy(hT[:, 4 * h:4 * h + 4, 0:m], pt[h][:, :, 0:m]).then_inc(hT_ready, 1)

        @block.vector
        def _(dve):
            do = Order(dve, order)
            do(dve.memset(K.logits[:, 0, :], 0.0))
            for i in range(NT + 1):
                if i < NT:
                    m = TILES[i][1]
                    dve.wait_ge(res_loaded[i % 2], 16 * (i // 2 + 1))
                    for h in range(2):
                        c = slice(512 * h, 512 * h + 512)
                        dve.wait_ge(o_ready, 2 * i + h + 1)
                        dve.scalar_tensor_tensor(out=K.H[0:m, i, c], in0=res[i % 2][0:m, c], scalar=ALPHA, in1=po[i % 2][h][0:m, :],
                                                 op0=ALU.mult, op1=ALU.add).then_inc(z_done, 1)
                    dve.wait_ge(z_done, 2 * i + 2)
                    norm.dve(dve, do, i)
                if i >= 1:
                    m = TILES[i - 1][1]
                    if i == 1:
                        dve.wait_ge(r_loaded, 7 * 16)
                    dve.wait_ge(lg_ready, i)
                    dve.tensor_tensor(K.logits[0:m, i - 1, :], pl[0:m, :], rb[0:m, :], ALU.add).then_inc(lg_done, 1)
            dve.wait_ge(lg_done, NT)

        @block.gpsimd
        def _(pool):
            for i in range(NT):
                norm.pool(pool, i)


NBLK = NE + (2 * T) // P
NOVER = NBLK - NE
EARLY = 2
MAIN = NE + EARLY
MAX_OVER = T // P
NO_ROW = 1.0e6


def expert_buffers(nc, K, layer):
    L = f"l{layer}"
    at = Place(nc, K.base)
    E = K.E = Kept(nc)
    E.wg, E.wu, E.wd = ([at(f"{L}_{x}{i}", [w]) for i in range(2)] for x, w in (("wg", KD * F), ("wu", KD * F), ("wd", 4 * D)))
    E.free = at.at
    E.src = {x: K.A[f"{L}_moe_w_{x}"].rearrange("e (p c) f -> e p (c f)", p=P) for x in ("gate", "up", "down")}
    E.g_loaded, E.u_loaded, E.d_loaded = ([nc.alloc_semaphore(f"{L}_{x}_loaded{i}") for i in range(2)] for x in "gud")


def load_expert(sp, E, e, par, wait_gate=None, wait_down=None):
    if wait_gate is not None:
        sp.wait_ge(*wait_gate)
    sp.dma_start(E.wg[par][:], E.src["gate"][ds(e, 1)].rearrange("a p x -> (a p) x")).then_inc(E.g_loaded[par], 16)
    sp.dma_start(E.wu[par][:], E.src["up"][ds(e, 1)].rearrange("a p x -> (a p) x")).then_inc(E.u_loaded[par], 16)
    if wait_down is not None:
        sp.wait_ge(*wait_down)
    sp.dma_start(E.wd[par][:], E.src["down"][ds(e, 1)].rearrange("a p x -> (a p) x")).then_inc(E.d_loaded[par], 16)


def route(nc, K, layer):
    L = f"l{layer}"
    expert_buffers(nc, K, layer)
    at = Place(nc, K.E.free)
    n = lambda name, shape, dt=F32: at(f"{L}_rt_{name}", shape, dt)
    iota, rev, thr, tok = n("iota", [P]), n("rev", [8]), n("thr", [MAX_OVER]), n("tok", [NT])
    tri, ones, valid = n("tri", [P]), n("ones", [P]), n("valid", [NT])
    cm, vm, dif, G, v4 = n("cm", [NT]), n("vm", [NT]), n("dif", [NT, 4]), n("G", [NT, 4]), n("v4", [NT, 4])
    pg, f48, sel, v8 = n("pg", [NT]), n("f48", [NT, 4, 8]), n("sel", [NT, 8]), n("v8", [NT, 8])
    top = [n("top1", [NT]), n("top2", [NT])]
    O = [n("O1", [NT, 8]), n("O2", [NT, 8])]
    M = [n("M1", [NT, NE]), n("M2", [NT, NE])]
    Ms, pos, tot, run = n("Ms", [NT, NE]), n("pos", [NT, NE]), n("tot", [NT, NE]), n("run", [NT + 1, NE])
    e2, den = n("e2", [NT]), n("den", [NT])
    gt, nover, inc, ob, one32 = n("gt", [NE, MAX_OVER]), n("nover", [NE]), n("inc", [NE]), n("ob", [NE]), n("one32", [NE])
    tmp, q8 = n("tmp", [NT, NE]), n("q8", [NT, MAX_OVER])
    pk, ek, ok, qk, geo, blk, slot = (n(x, [NT]) for x in ("pk", "ek", "ok", "qk", "geo", "blk", "slot"))
    blk, slot = [n("blk1", [NT]), n("blk2", [NT])], [n("slot1", [NT]), n("slot2", [NT])]
    vals = n("vals", [NT, 2, 3])
    Pm, B, R = [n(f"Pm{i}", [P]) for i in range(2)], [n(f"B{i}", [NBLK]) for i in range(2)], [n(f"R{i}", [3, NBLK]) for i in range(2)]
    rowf, isz = n("rowf", [NBLK]), n("isz", [NBLK])
    ind, ind2, ov = n("ind", [NOVER, NE]), n("ind2", [NOVER, NE]), n("ov", [1, NOVER])
    sem = lambda x: K.sem(f"{L}_rt_{x}")
    made, order, exp_in, exp_done, m_ready, cum_ready, oh_ready, tab_used, tab_ready = map(sem, (
        "made", "order", "exp_in", "exp_done", "m_ready", "cum_ready", "oh_ready", "tab_used", "tab_ready"))
    lg = K.logits
    with nc.psum_tensor(L + "_p_cum", [P, 2, 512], F32) as pc, nc.psum_tensor(L + "_p_tab", [P, 3, NBLK], F32) as ptab, nc.Block() as block:
        @block.sync
        def _(sp):
            for par in range(2):
                load_expert(sp, K.E, par, par)

        @block.gpsimd
        def _(pool):
            kw = dict(allow_small_or_imprecise_dtypes=True)
            pool.iota(iota[:], pattern=[[1, P]], base=0, channel_multiplier=0, **kw).then_inc(made, 1)
            pool.iota(rev[:], pattern=[[-1, 8]], base=8, channel_multiplier=0, **kw).then_inc(made, 1)
            pool.iota(thr[:], pattern=[[P, MAX_OVER]], base=P, channel_multiplier=0, **kw).then_inc(made, 1)
            pool.iota(tok[:, 0:1], pattern=[[1, 1]], base=0, channel_multiplier=1, **kw).then_inc(made, 1)
            pool.iota(tok[:, 1:NT], pattern=[[P, NT - 1]], base=N_META, channel_multiplier=1, **kw).then_inc(made, 1)
            pool.memset(ones[:], 1.0).then_inc(made, 1)
            pool.memset(tri[:], 1.0).then_inc(made, 1)
            pool.memset(valid[:], 1.0).then_inc(made, 1)
            pool.wait_ge(made, 8)
            pool.affine_select(out=tri[:], in_=tri[:], compare_op=ALU.is_gt, fill=0.0, base=0, pattern=[[1, P]], channel_multiplier=-1).then_inc(made, 1)
            pool.affine_select(out=valid[:, 0:1], in_=valid[:, 0:1], compare_op=ALU.is_gt, fill=0.0, base=N_META, pattern=[[0, 1]], channel_multiplier=-1).then_inc(made, 1)

        @block.scalar
        def _(act):
            act.wait_ge(exp_in, 1)
            act.activation(dif[:], dif[:], ACT.Exp).then_inc(exp_done, 1)
            act.wait_ge(exp_in, 2)
            act.activation(e2[:], e2[:], ACT.Exp).then_inc(exp_done, 1)

        @block.tensor
        def _(pe):
            pe.wait_ge(made, 10)
            pe.wait_ge(m_ready, 1)
            pe.matmul(pc[:, 0, 0:NT * NE], tri[:], Ms[:].rearrange("p i e -> p (i e)"), start=True, stop=True).then_inc(cum_ready, 1)
            pe.matmul(pc[:, 1, 0:NT * NE], ones[:], Ms[:].rearrange("p i e -> p (i e)"), start=True, stop=True).then_inc(cum_ready, 1)
            for s in range(2 * NT):
                pe.wait_ge(oh_ready, s + 1)
                pe.matmul(ptab[:].rearrange("p a b -> p (a b)"), Pm[s % 2][:], R[s % 2][:].rearrange("p a b -> p (a b)"),
                          start=s == 0, stop=s == 2 * NT - 1).then_inc(tab_used, 1)

        @block.vector
        def _(dve):
            do = Order(dve, order)
            tt, ts, red = dve.tensor_tensor, dve.tensor_scalar, dve.tensor_reduce
            dve.wait_ge(made, 10)
            coarse, fine = lg[:, :, 0:GROUPS], lg[:, :, GROUPS:36].rearrange("p i (g e) -> p i g e", g=GROUPS)

            def first_of_max(values, maxi, v, hot, width):
                do(red(maxi[:], values, AX_X, ALU.max))
                do(tt(v[:], values, bc(maxi[:], width), ALU.is_equal))
                do(tt(v[:], v[:], rev[:, 0:width].unsqueeze(1).to_broadcast([P, NT, width]), ALU.mult))
                do(red(vm[:], v[:], AX_X, ALU.max))
                do(tt(hot[:], v[:], bc(vm[:], width), ALU.is_equal))

            first_of_max(coarse, cm, v4, G, GROUPS)
            tt(dif[:], coarse, bc(cm[:], GROUPS), ALU.subtract).then_inc(exp_in, 1)
            do(tt(f48[:], fine, G[:].unsqueeze(3).to_broadcast([P, NT, GROUPS, PER_GROUP]), ALU.mult))
            do(red(sel[:], f48[:].rearrange("p i g e -> p i e g"), AX_X, ALU.add))
            first_of_max(sel[:], top[0], v8, O[0], PER_GROUP)
            do(ts(v8[:], O[0][:], -3.0e38, None, ALU.mult))
            do(tt(sel[:], sel[:], v8[:], ALU.add))
            first_of_max(sel[:], top[1], v8, O[1], PER_GROUP)
            tt(e2[:], top[1][:], top[0][:], ALU.subtract).then_inc(exp_in, 1)
            for k in range(2):
                do(tt(M[k][:].rearrange("p i (g e) -> p i g e", g=GROUPS), G[:].unsqueeze(3).to_broadcast([P, NT, GROUPS, PER_GROUP]),
                      O[k][:].unsqueeze(2).to_broadcast([P, NT, GROUPS, PER_GROUP]), ALU.mult))
                do(tt(M[k][:], M[k][:], bc(valid[:], NE), ALU.mult))
            tt(Ms[:], M[0][:], M[1][:], ALU.add).then_inc(m_ready, 1)
            dve.wait_ge(exp_done, 2)
            do(red(pg[:], dif[:], AX_X, ALU.add), wait=False)
            do(ts(den[:], e2[:], 1.0, None, ALU.add))
            do(dve.reciprocal(pg[:], pg[:]), wait=False)
            do(dve.reciprocal(den[:], den[:]))
            do(tt(vals[:, :, 0, 2], pg[:], den[:], ALU.mult))
            do(tt(vals[:, :, 1, 2], vals[:, :, 0, 2], e2[:], ALU.mult), wait=False)
            for k in range(2):
                do(dve.tensor_copy(vals[:, :, k, 0], tok[:]), wait=False)
                do(ts(vals[:, :, k, 1], tok[:], float(1 + k * T), None, ALU.add), wait=False)
            dve.wait_ge(cum_ready, 2)
            do(dve.memset(run[:, 0, :], 0.0), wait=False)
            do(dve.tensor_copy(tot[:], pc[:, 1, 0:NT * NE].rearrange("p (i e) -> p i e", i=NT)))
            for i in range(NT):
                do(tt(run[:, i + 1, :], run[:, i, :], tot[:, i, :], ALU.add))
            do(tt(pos[:], pc[:, 0, 0:NT * NE].rearrange("p (i e) -> p i e", i=NT), run[:, 0:NT, :], ALU.add), wait=False)
            do(tt(gt[:], bc(run[:, NT, :], MAX_OVER), thr[:].unsqueeze(1).to_broadcast([P, NE, MAX_OVER]), ALU.is_gt))
            do(red(nover[:], gt[:], AX_X, ALU.add), wait=False)
            do(dve.memset(one32[:], 1.0))
            do(dve.tensor_tensor_scan(inc[:], one32[:], nover[:], 0.0, ALU.mult, ALU.add))
            do(tt(ob[:], inc[:], nover[:], ALU.subtract))
            j = iota[:, 0:NOVER].unsqueeze(2).to_broadcast([P, NOVER, NE])
            do(tt(ind[:], j, ob[:].unsqueeze(1).to_broadcast([P, NOVER, NE]), ALU.is_ge), wait=False)
            do(tt(ind2[:], j, inc[:].unsqueeze(1).to_broadcast([P, NOVER, NE]), ALU.is_lt))
            do(tt(ind[:], ind[:], ind2[:], ALU.mult))
            do(tt(ind2[:], ind[:], iota[:, 0:NE].unsqueeze(1).to_broadcast([P, NOVER, NE]), ALU.mult))
            do(red(ov[:, 0, :], ind2[:], AX_X, ALU.add))
            do(dve.tensor_copy(K.over[:, 0:NOVER], ov[:, 0, :]), wait=False)
            do(dve.tensor_copy(K.over[:, NOVER:NOVER + 1], inc[:, NE - 1:NE]), wait=False)
            for k in range(2):
                for out, per_expert in ((pk, pos[:]), (ek, iota[:, 0:NE].unsqueeze(1).to_broadcast([P, NT, NE])),
                                        (ok, ob[:].unsqueeze(1).to_broadcast([P, NT, NE]))):
                    do(tt(tmp[:], M[k][:], per_expert, ALU.mult))
                    do(red(out[:], tmp[:], AX_X, ALU.add))
                do(tt(q8[:], bc(pk[:], MAX_OVER), thr[:].unsqueeze(1).to_broadcast([P, NT, MAX_OVER]), ALU.is_ge))
                do(red(qk[:], q8[:], AX_X, ALU.add))
                do(ts(geo[:], qk[:], 1.0, None, ALU.min), wait=False)
                do(dve.scalar_tensor_tensor(out=slot[k][:], in0=qk[:], scalar=-float(P), in1=pk[:], op0=ALU.mult, op1=ALU.add), wait=False)
                do(dve.scalar_tensor_tensor(out=blk[k][:], in0=qk[:], scalar=float(NE - 1), in1=ok[:], op0=ALU.add, op1=ALU.add))
                do(tt(blk[k][:], blk[k][:], ek[:], ALU.subtract))
                do(tt(blk[k][:], blk[k][:], geo[:], ALU.mult))
                do(tt(blk[k][:], blk[k][:], ek[:], ALU.add))
            for s in range(2 * NT):
                i, k, b = s // 2, s % 2, s % 2
                if s >= 2:
                    dve.wait_ge(tab_used, s - 1)
                do(ts(Pm[b][:], iota[:], slot[k][:, i:i + 1], None, ALU.is_equal), wait=False)
                do(ts(B[b][:], iota[:, 0:NBLK], blk[k][:, i:i + 1], valid[:, i:i + 1], ALU.is_equal, ALU.mult))
                tt(R[b][:], B[b][:].unsqueeze(1).to_broadcast([P, 3, NBLK]), bc(vals[:, i, k, :], NBLK), ALU.mult).then_inc(oh_ready, 1)
            dve.wait_ge(tab_used, 2 * NT)
            do(dve.tensor_copy(K.tok_idx[:], ptab[:, 0, :]), wait=False)
            do(dve.tensor_copy(K.gates[:], ptab[:, 2, :]), wait=False)
            do(ts(isz[:], ptab[:, 1, :], 0.0, NO_ROW, ALU.is_equal, ALU.mult), wait=False)
            do(ts(rowf[:], ptab[:, 1, :], -1.0, None, ALU.add))
            do(tt(rowf[:], rowf[:], isz[:], ALU.add))
            do(dve.tensor_copy(K.row_idx[:], rowf[:]))


def is_at(b, n):
    return isinstance(b, int) and b == n


def experts(nc, K, A, layer):
    L = f"l{layer}"
    E = K.E
    wg, wu, wd = E.wg, E.wu, E.wd
    at = Place(nc, E.free)
    n = lambda name, shape, dt=F32: at(f"{L}_ex_{name}", shape, dt)
    xb = [n(f"xb{i}", [D]) for i in range(2)]
    xT = [n(f"xT{i}", [KD, P]) for i in range(2)]
    yb = [n(f"yb{i}", [D]) for i in range(2)]
    sil, hid, hT = n("sil", [F]), [n(f"hid{i}", [F]) for i in range(2)], n("hT", [4, P])
    gi, ri, gc = ([n(f"{x}{i}", [1], d) for i in range(2)] for x, d in (("gi", U32), ("ri", U32), ("gc", F32)))
    wv = lambda w: w[:].rearrange("p (c f) -> p c f", f=F)
    dv = lambda w: w[:].rearrange("p (c d) -> p c d", d=D)

    for phase in ("main", "over"):
        main = phase == "main"
        sem = lambda x: K.sem(f"{L}_{phase}_{x}")
        pair = lambda x: [sem(x + "0"), sem(x + "1")]
        g_loaded, u_loaded, d_loaded = E.g_loaded, E.u_loaded, E.d_loaded
        if not main:
            E.g_loaded, E.u_loaded, E.d_loaded = g_loaded, u_loaded, d_loaded = [pair(x) for x in ("g_loaded", "u_loaded", "d_loaded")]
        gathered, scattered = map(pair, ("gathered", "scattered"))
        x_turned, xT_a, xT_v, g_ready, u_ready, silu_done, hid_done, h_turned, hT_ready, y_ready, y_a, y_v, idx_done, row_done, paced = map(sem, (
            "x_turned", "xT_a", "xT_v", "g_ready", "u_ready", "silu_done", "hid_done", "h_turned", "hT_ready", "y_ready",
            "y_a", "y_v", "idx_done", "row_done", "paced"))
        with ExitStack() as ctx:
            psum = lambda x, s: ctx.enter_context(nc.psum_tensor(f"{L}_{phase}_{x}", s, F32))
            pg, pu, ph = psum("pg", [P, 512]), psum("pu", [P, 512]), psum("ph", [P, 4, P])
            px, py = [psum(f"px{i}", [P, 4, P]) for i in range(2)], [psum(f"py{i}", [P, 512]) for i in range(2)]
            block = ctx.enter_context(nc.Block())

            def load(sp, e, i, b, par):
                if is_at(b, 0):
                    load_expert(sp, E, e, par)
                else:
                    load_expert(sp, E, e, par, (u_ready, b - 1), (y_ready, 2 * (b - 1)))

            def gather(pool, col, i, b, par):
                if not (isinstance(b, int) and b < 2):
                    pool.wait_ge(gathered[par], 16 * i)
                    pool.wait_ge(x_turned, b - 1)
                pool.tensor_copy(gi[par][:], K.tok_idx[:, ds(col, 1)]).then_inc(idx_done, 1)
                pool.wait_ge(idx_done, b + 1)
                pool.sem_inc(paced, 1)
                pool.indirect_dma_start(xb[par][:], None, K.h1_dram, bass.IndirectOffsetOnAxis(ap=gi[par][:], axis=0)).then_inc(gathered[par], 16)

            def gate_column(pool, col, b, par):
                if not is_at(b, 0):
                    pool.wait_ge(y_a, b - 1)
                    pool.wait_ge(y_v, b - 1)
                pool.tensor_copy(gc[par][:], K.gates[:, ds(col, 1)]).then_inc(row_done, 1)

            def scatter(pool, col, i, b, par):
                if not is_at(b, 0):
                    pool.wait_ge(scattered[par], 16 * i)
                pool.tensor_copy(ri[par][:], K.row_idx[:, ds(col, 1)]).then_inc(row_done, 1)
                pool.wait_ge(row_done, 2 * b + 2)
                pool.wait_ge(y_a, b + 1)
                pool.wait_ge(y_v, b + 1)
                pool.sem_inc(paced, 1)
                pool.indirect_dma_start(K.y_dram, bass.IndirectOffsetOnAxis(ap=ri[par][:], axis=0), yb[par][:], None,
                                        bounds_check=2 * T - 1, oob_is_err=False).then_inc(scattered[par], 16)

            def turn_x(pe, i, b, par):
                pe.wait_ge(gathered[par], 16 * (i + 1))
                for k in range(KD):
                    last = pe.transpose(px[k // 4][:, k % 4, :], xb[par][:].rearrange("s (p c) -> s c p", c=KD)[:, k, :], K.ident[:])
                last.then_inc(x_turned, 1)

            def gate_up(pe, i, b, par):
                pe.wait_ge(g_loaded[par], 16 * (i + 1))
                pe.wait_ge(xT_a, b + 1)
                pe.wait_ge(xT_v, b + 1)
                pe.wait_ge(silu_done, b)
                for k in range(KD):
                    last = pe.matmul(pg[:], xT[par][:, k, :], wv(wg[par])[:, k, :], start=k == 0, stop=k == KD - 1)
                last.then_inc(g_ready, 1)
                pe.wait_ge(u_loaded[par], 16 * (i + 1))
                pe.wait_ge(hid_done, b)
                for k in range(KD):
                    last = pe.matmul(pu[:], xT[par][:, k, :], wv(wu[par])[:, k, :], start=k == 0, stop=k == KD - 1)
                last.then_inc(u_ready, 1)

            def turn_h(pe, b, par):
                pe.wait_ge(hid_done, b + 1)
                for k in range(4):
                    last = pe.transpose(ph[:, k, :], hid[par][:].rearrange("s (p c) -> s c p", c=4)[:, k, :], K.ident[:])
                last.then_inc(h_turned, 1)

            def down(pe, i, b, par):
                pe.wait_ge(hT_ready, b + 1)
                pe.wait_ge(d_loaded[par], 16 * (i + 1))
                for h, used in enumerate((y_a, y_v)):
                    pe.wait_ge(used, b)
                    for k in range(4):
                        last = pe.matmul(py[h][:], hT[:, k, :], dv(wd[par])[:, k, 512 * h:512 * h + 512], start=k == 0, stop=k == 3)
                    last.then_inc(y_ready, 1)

            def silu(act, b):
                act.wait_ge(g_ready, b + 1)
                act.wait_ge(hid_done, b)
                act.activation(sil[:], pg[:], ACT.Silu).then_inc(silu_done, 1)

            def copy_x(eng, op, half, b, par, done):
                eng.wait_ge(x_turned, b + 1)
                if not is_at(b, 0):
                    eng.wait_ge(u_ready, b - 1)
                op(xT[par][:, 4 * half:4 * half + 4, :], px[half][:]).then_inc(done, 1)

            def hidden(dve, b, par):
                dve.wait_ge(u_ready, b + 1)
                dve.wait_ge(silu_done, b + 1)
                if not is_at(b, 0):
                    dve.wait_ge(h_turned, b - 1)
                dve.tensor_tensor(hid[par][:], sil[:], pu[:], ALU.mult).then_inc(hid_done, 1)

            def copy_h(dve, b):
                dve.wait_ge(h_turned, b + 1)
                dve.tensor_copy(hT[:], ph[:]).then_inc(hT_ready, 1)

            def store_y(eng, half, i, b, par):
                eng.wait_ge(y_ready, 2 * b + half + 1)
                eng.wait_ge(row_done, 2 * b + 1)
                if not is_at(b, 0):
                    eng.wait_ge(scattered[par], 16 * i)
                out = yb[par][:, 512 * half:512 * half + 512]
                if half == 0:
                    eng.mul(out, py[0][:], gc[par][:, 0:1]).then_inc(y_a, 1)
                else:
                    eng.tensor_scalar(out, py[1][:], gc[par][:, 0:1], None, ALU.mult).then_inc(y_v, 1)

            if main:
                def walk(eng, step):
                    for b in range(4):
                        step(b // 2, b, b % 2)
                    with eng.Fori(2, MAIN // 2 - 2) as i:
                        for par in range(2):
                            step(i, 2 * i + par, par)
                    for b in range(MAIN - 4, MAIN):
                        step(b // 2, b, b % 2)
                    step(MAIN // 2, MAIN, 0)

                @block.sync
                def _(sp):
                    with sp.Fori(1, NE // 2) as i:
                        for par in range(2):
                            load(sp, 2 * i + par, i, 2 * i + par, par)
                    for b in range(NE, MAIN):
                        e = sp.value_load(K.over[0:1, b - NE:b - NE + 1], min_val=0, max_val=NE - 1)
                        load(sp, e, b // 2, b, b % 2)

                @block.gpsimd
                def _(pool):
                    def step(i, b, par):
                        if is_at(b, 0):
                            for early in range(3):
                                gather(pool, early, early // 2, early, early % 2)
                        if not (isinstance(b, int) and b > MAIN - 4):
                            gather(pool, b + 3, i + 1 + par, b + 3, 1 - par)
                        if not is_at(b, 0):
                            gate_column(pool, b - 1, b - 1, 1 - par)
                            scatter(pool, b - 1, i - 1 + par, b - 1, 1 - par)
                    walk(pool, step)
                    for par in range(2):
                        pool.wait_ge(scattered[par], 16 * (MAIN // 2))

                @block.tensor
                def _(pe):
                    def step(i, b, par):
                        if is_at(b, 0):
                            turn_x(pe, 0, 0, 0)
                        if not is_at(b, MAIN):
                            gate_up(pe, i, b, par)
                        if not (is_at(b, MAIN - 1) or is_at(b, MAIN)):
                            turn_x(pe, i + par, b + 1, 1 - par)
                        if not is_at(b, 0):
                            turn_h(pe, b - 1, 1 - par)
                            down(pe, i - 1 + par, b - 1, 1 - par)
                    walk(pe, step)

                @block.scalar
                def _(act):
                    def step(i, b, par):
                        if is_at(b, 0):
                            copy_x(act, act.copy, 0, 0, 0, xT_a)
                        if not is_at(b, MAIN):
                            silu(act, b)
                        if not (is_at(b, MAIN - 1) or is_at(b, MAIN)):
                            copy_x(act, act.copy, 0, b + 1, 1 - par, xT_a)
                        if not is_at(b, 0):
                            store_y(act, 0, i - 1 + par, b - 1, 1 - par)
                    walk(act, step)

                @block.vector
                def _(dve):
                    def step(i, b, par):
                        if is_at(b, 0):
                            copy_x(dve, dve.tensor_copy, 1, 0, 0, xT_v)
                        if not is_at(b, MAIN):
                            hidden(dve, b, par)
                        if not (is_at(b, MAIN - 1) or is_at(b, MAIN)):
                            copy_x(dve, dve.tensor_copy, 1, b + 1, 1 - par, xT_v)
                        if not is_at(b, 0):
                            copy_h(dve, b - 1)
                            store_y(dve, 1, i - 1 + par, b - 1, 1 - par)
                    walk(dve, step)
            else:
                def each(eng, step):
                    blocks = eng.value_load(K.over[0:1, NOVER:NOVER + 1], min_val=0, max_val=NOVER)

                    def one(i, par):
                        j = 2 * i + par
                        with eng.If(blocks > j + EARLY):
                            step(i, j, par)
                        with eng.Else():
                            eng.nop()
                    for par in range(2):
                        one(0, par)
                    with eng.Fori(1, (NOVER - EARLY) // 2) as i:
                        for par in range(2):
                            one(i, par)

                @block.sync
                def _(sp):
                    def step(i, j, par):
                        e = sp.value_load(K.over[0:1, ds(j + EARLY, 1)], min_val=0, max_val=NE - 1)
                        load(sp, e, i, j, par)
                    each(sp, step)

                @block.gpsimd
                def _(pool):
                    def step(i, j, par):
                        gather(pool, MAIN + j, i, j, par)
                        gate_column(pool, MAIN + j, j, par)
                        scatter(pool, MAIN + j, i, j, par)
                        pool.wait_ge(scattered[par], 16 * (i + 1))
                        pool.sem_inc(over_done, 1)
                    over_done = sem("over_done")
                    each(pool, step)

                @block.tensor
                def _(pe):
                    def step(i, j, par):
                        turn_x(pe, i, j, par)
                        gate_up(pe, i, j, par)
                        turn_h(pe, j, par)
                        down(pe, i, j, par)
                    each(pe, step)

                @block.scalar
                def _(act):
                    def step(i, j, par):
                        copy_x(act, act.copy, 0, j, par, xT_a)
                        silu(act, j)
                        store_y(act, 0, i, j, par)
                    each(act, step)

                @block.vector
                def _(dve):
                    def step(i, j, par):
                        copy_x(dve, dve.tensor_copy, 1, j, par, xT_v)
                        hidden(dve, j, par)
                        copy_h(dve, j)
                        store_y(dve, 1, i, j, par)
                    each(dve, step)


def combine_and_norm(nc, K, A, layer):
    L, lastl = f"l{layer}", layer == DEPTH - 1
    at = Place(nc, K.base)
    K.hT = None if lastl else at("h2T", [KD, T])
    y0, y1 = [at(f"{L}_y0{i}", [D]) for i in range(2)], [at(f"{L}_y1{i}", [D]) for i in range(2)]
    norm = Norm(nc, K, L + "_ln2", at)
    sem = lambda n: K.sem(f"{L}_cb_{n}")
    y_loaded, z_done, order, turned, hT_ready, stored = [sem("y_loaded0"), sem("y_loaded1")], sem("z_done"), sem("order"), sem("turned"), sem("hT_ready"), sem("stored")
    with ExitStack() as ctx:
        pt = [[ctx.enter_context(nc.psum_tensor(f"{L}_cpt{b}{h}", [P, 4, P], F32)) for h in range(2)] for b in range(2)]
        block = ctx.enter_context(nc.Block())

        @block.sync
        def _(sp):
            norm.load(sp, A[L + "_ln2_g"], A[L + "_ln2_b"])
            for i in range(NT + 2):
                if i < NT:
                    t0, m = TILES[i]
                    if i >= 2:
                        sp.wait_ge(z_done, 2 * (i - 1))
                    for k, y in enumerate((y0, y1)):
                        sp.dma_start(y[i % 2][0:m, :], K.y_dram[k * T + t0:k * T + t0 + m, :]).then_inc(y_loaded[i % 2], 16)
                if i >= 2 and not (lastl and i == 2):
                    t0, m = TILES[i - 2]
                    sp.wait_ge(norm.h_ready, i - 1)
                    out = K.out[t0 - N_META:t0 - N_META + m, :] if lastl else K.h2_dram[t0:t0 + m, :]
                    sp.dma_start(out, K.H[0:m, i - 2, :]).then_inc(stored, 16)
            sp.wait_ge(stored, 16 * (NT - 1 if lastl else NT))

        @block.vector
        def _(dve):
            do = Order(dve, order)
            for i in range(NT):
                m = TILES[i][1]
                z = K.H[0:m, i, :]
                dve.wait_ge(y_loaded[i % 2], 32 * (i // 2 + 1))
                dve.scalar_tensor_tensor(out=z, in0=z, scalar=ALPHA, in1=y0[i % 2][0:m, :], op0=ALU.mult, op1=ALU.add).then_inc(z_done, 1)
                dve.wait_ge(z_done, 2 * i + 1)
                dve.tensor_tensor(z, z, y1[i % 2][0:m, :], ALU.add).then_inc(z_done, 1)
                dve.wait_ge(z_done, 2 * i + 2)
                norm.dve(dve, do, i)

        @block.gpsimd
        def _(pool):
            for i in range(NT):
                norm.pool(pool, i)

        @block.tensor
        def _(pe):
            if not lastl:
                for i in range(NT):
                    m = TILES[i][1]
                    pe.wait_ge(norm.h_ready, i + 1)
                    if i >= 2:
                        pe.wait_ge(hT_ready, 2 * (i - 1))
                    for k in range(KD):
                        last = pe.transpose(pt[i % 2][k // 4][:, k % 4, 0:m], K.H[0:m, i, P * k:P * k + P], K.ident[0:m, 0:m])
                    last.then_inc(turned, 1)

        @block.scalar
        def _(act):
            for i in range(NT + 1):
                if i < NT:
                    norm.act(act, i)
                if i >= 1 and not lastl:
                    t0, m = TILES[i - 1]
                    act.wait_ge(turned, i)
                    for h in range(2):
                        act.copy(K.hT[:, 4 * h:4 * h + 4, t0:t0 + m], pt[(i - 1) % 2][h][:, :, 0:m]).then_inc(hT_ready, 1)


def rglru(nc, K, A):
    at = Place(nc, K.free_hT)
    K.y1T = at("y1T", [NB, T])
    K.free_y1T = at.at
    wide = Place(nc, K.h_at)
    wz = [at(f"lru_wz{i}", [KD, 2, P]) for i in range(2)]
    wax = [at(f"lru_wax{i}", [2, P]) for i in range(2)]
    rec, xc = [at(f"lru_rec{i}", [T + 3]) for i in range(2)], [at(f"lru_xc{i}", [T]) for i in range(2)]
    gg, ra, ii = wide("lru_gg", [T]), wide("lru_r", [T]), wide("lru_i", [T])
    a, t, v, u = wide("lru_a", [T]), wide("lru_t", [T]), wide("lru_v", [T]), wide("lru_u", [T])
    NPR = 9
    prm, pc = at("lru_prm", [NPR, NB]), at("lru_pc", [NPR])
    m0, m1, m2, m3 = (at(f"lru_m{i}", [NB]) for i in range(4))
    assert at.at <= K.w_out1_at
    sem = lambda n: K.sem("lru_" + n)
    loaded, w_loaded = sem("loaded"), [sem("w_loaded0"), sem("w_loaded1")]
    (order, z_exp, z_in, sp_done, prm_ready, rec_ready, rec_copied, gate_ready, gelu_done, xc_ready, ga_ready, sig_done,
     at_done, v_ready, s_done, y_done) = map(sem, (
        "order", "z_exp", "z_in", "sp_done", "prm_ready", "rec_ready", "rec_copied", "gate_ready", "gelu_done", "xc_ready",
        "ga_ready", "sig_done", "at_done", "v_ready", "s_done", "y_done"))
    w = A["l1_w_in"].rearrange("(k p) c -> p k c", p=P)
    NC = len(CHUNKS)
    with ExitStack() as ctx:
        pr = ctx.enter_context(nc.psum_tensor("lru_pr", [P, NC, 512], F32))
        pgt = ctx.enter_context(nc.psum_tensor("lru_pg", [P, NC, 512], F32))
        pa = [ctx.enter_context(nc.psum_tensor(f"lru_pa{i}", [P, 512], F32)) for i in range(2)]
        block = ctx.enter_context(nc.Block())

        def weights(sp, n, par):
            sp.dma_start(wz[par][:, :, 0, :], w[:, :, ds(n * P + D_RNN, P)]).then_inc(w_loaded[par], 16)
            sp.dma_start(wz[par][:, :, 1, :], w[:, :, ds(n * P, P)]).then_inc(w_loaded[par], 16)
            sp.dma_start(wax[par][:, 0, :], A["l1_lru_w_a"][ds(n, 1)].rearrange("a d e -> (a d) e")).then_inc(w_loaded[par], 16)
            sp.dma_start(wax[par][:, 1, :], A["l1_lru_w_x"][ds(n, 1)].rearrange("a d e -> (a d) e")).then_inc(w_loaded[par], 16)

        @block.sync
        def _(sp):
            with nc.allow_non_contiguous_dma(reason="parameters by channel"):
                for par in range(2):
                    weights(sp, par, par)
                load_w_out(sp, K, 1)
                for j in range(4):
                    sp.dma_start(prm[:, j, :], A["l1_conv_w"][j].rearrange("(n p) -> p n", p=P)).then_inc(loaded, 16)
                for j, nm in enumerate(("l1_conv_b", "l1_lru_b_a", "l1_lru_b_x", "l1_lru_lambda")):
                    sp.dma_start(prm[:, 4 + j, :], A[nm].rearrange("(n p) -> p n", p=P)).then_inc(loaded, 16)
                with sp.Fori(1, NB // 2) as i:
                    for par in range(2):
                        sp.wait_ge(ga_ready, (2 * i + par - 1) * 2 * NC)
                        weights(sp, 2 * i + par, par)

        def products(pe, i, n, par):
            pe.wait_ge(w_loaded[par], 64 * (i + 1))
            pe.wait_ge(rec_copied, 1 + NC * n)
            for j, (o, c) in enumerate(CHUNKS):
                for k in range(KD):
                    last = pe.matmul(pr[:, j, 0:c], wz[par][:, k, 0, :], K.hT[:, k, o:o + c], start=k == 0, stop=k == KD - 1)
                last.then_inc(rec_ready, 1)
            pe.wait_ge(gelu_done, 1 + NC * n)
            for j, (o, c) in enumerate(CHUNKS):
                for k in range(KD):
                    last = pe.matmul(pgt[:, j, 0:c], wz[par][:, k, 1, :], K.hT[:, k, o:o + c], start=k == 0, stop=k == KD - 1)
                last.then_inc(gate_ready, 1)
            pe.wait_ge(xc_ready, n + 1)
            for s in range(2 * NC):
                j, g = s // 2, s % 2
                o, c = CHUNKS[j]
                if s < 2:
                    pe.wait_ge(sig_done, 1 + 2 * NC * n)
                else:
                    pe.wait_ge(sig_done, 1 + 2 * NC * n + s - 1)
                pe.matmul(pa[s % 2][:, 0:c], wax[par][:, g, :], xc[par][:, o:o + c], start=True, stop=True).then_inc(ga_ready, 1)

        @block.tensor
        def _(pe):
            with pe.Fori(0, NB // 2) as i:
                for par in range(2):
                    products(pe, i, 2 * i + par, par)

        def acts(act, n, par):
            for j, (o, c) in enumerate(CHUNKS):
                act.wait_ge(rec_ready, NC * n + j + 1)
                act.copy(rec[par][:, 3 + o:3 + o + c], pr[:, j, 0:c]).then_inc(rec_copied, 1)
            act.wait_ge(y_done, 1 + n)
            for j, (o, c) in enumerate(CHUNKS):
                act.wait_ge(gate_ready, NC * n + j + 1)
                act.activation(gg[:, o:o + c], pgt[:, j, 0:c], ACT.Gelu_apprx_tanh).then_inc(gelu_done, 1)
            for s in range(2 * NC):
                j, g = s // 2, s % 2
                o, c = CHUNKS[j]
                act.wait_ge(ga_ready, 2 * NC * n + s + 1)
                act.activation((ra, ii)[g][:, o:o + c], pa[s % 2][:, 0:c], ACT.Sigmoid, bias=pc[:, 5 + g:6 + g]).then_inc(sig_done, 1)
            act.wait_ge(sig_done, 1 + 2 * NC * (n + 1))
            act.activation(t[:], ra[:], ACT.Tanh, scale=pc[:, 8:9]).then_inc(at_done, 1)
            act.activation(a[:], ra[:], ACT.Exp, scale=pc[:, 7:8]).then_inc(at_done, 1)
            act.wait_ge(v_ready, n + 1)
            act.activation(v[:], v[:], ACT.Sqrt).then_inc(s_done, 1)

        @block.scalar
        def _(act):
            for counted in (rec_copied, gelu_done, sig_done):
                act.sem_inc(counted, 1)
            act.wait_ge(z_in, 1)
            act.activation(m1[:], m1[:], ACT.Exp, scale=-1.0).then_inc(z_exp, 1)
            with act.Fori(0, NB // 2) as i:
                for par in range(2):
                    acts(act, 2 * i + par, par)

        def block_dve(dve, do, n, par):
            do(dve.tensor_copy(pc[:], prm[:, :, ds(n, 1)].rearrange("p a b -> p (a b)")))
            x, r = xc[par], rec[par]
            dve.wait_ge(rec_copied, 1 + NC * (n + 1))
            do(dve.tensor_scalar(x[:], r[:, 0:T], pc[:, 0:1], pc[:, 4:5], ALU.mult, ALU.add))
            for j in range(1, 4):
                ins = dve.scalar_tensor_tensor(out=x[:], in0=r[:, j:j + T], scalar=pc[:, j:j + 1], in1=x[:], op0=ALU.mult, op1=ALU.add)
                if j < 3:
                    do(ins)
                else:
                    ins.then_inc(xc_ready, 1)
            dve.wait_ge(sig_done, 1 + 2 * NC * (n + 1))
            dve.wait_ge(xc_ready, n + 1)
            do(dve.tensor_tensor(u[:], ii[:], x[:], ALU.mult), wait=False)
            dve.wait_ge(at_done, 2 * n + 1)
            do(dve.tensor_scalar(v[:], t[:], 1.0, None, ALU.add))
            do(dve.reciprocal(v[:], v[:]))
            dve.scalar_tensor_tensor(out=v[:], in0=t[:], scalar=2.0, in1=v[:], op0=ALU.mult, op1=ALU.mult).then_inc(v_ready, 1)
            dve.wait_ge(s_done, n + 1)
            dve.wait_ge(at_done, 2 * n + 2)
            do(dve.tensor_tensor(u[:], u[:], v[:], ALU.mult))
            do(dve.tensor_tensor_scan(t[:], a[:], u[:], 0.0, ALU.mult, ALU.add))
            dve.tensor_tensor(K.y1T[:, ds(n, 1), :].rearrange("p a t -> p (a t)"), t[:], gg[:], ALU.mult).then_inc(y_done, 1)

        @block.vector
        def _(dve):
            do = Order(dve, order)
            dve.sem_inc(y_done, 1)
            for par in range(2):
                do(dve.memset(rec[par][:, 0:3], 0.0), wait=False)
            dve.wait_ge(loaded, 8 * 16)
            lam = prm[:, 7, :]
            do(dve.tensor_scalar(m0[:], lam, -1.0, None, ALU.mult))
            dve.tensor_tensor(m1[:], m0[:], lam, ALU.max).then_inc(z_in, 1)
            dve.wait_ge(z_exp, 1)
            do(dve.tensor_scalar(m2[:], m1[:], 2.0, None, ALU.add))
            do(dve.reciprocal(m2[:], m2[:]))
            do(dve.tensor_tensor(m1[:], m1[:], m2[:], ALU.mult))
            do(dve.tensor_tensor(m2[:], m1[:], m1[:], ALU.mult))
            do(dve.memset(m3[:], 1.0 / 21))
            for k in range(9, -1, -1):
                do(dve.tensor_tensor(m3[:], m3[:], m2[:], ALU.mult))
                do(dve.tensor_scalar(m3[:], m3[:], 1.0 / (2 * k + 1), None, ALU.add))
            do(dve.tensor_tensor(m3[:], m3[:], m1[:], ALU.mult))
            do(dve.tensor_scalar(m0[:], m0[:], 0.0, None, ALU.max))
            do(dve.scalar_tensor_tensor(out=m3[:], in0=m3[:], scalar=2.0, in1=m0[:], op0=ALU.mult, op1=ALU.add))
            do(dve.tensor_scalar(prm[:, 8, :], m3[:], 8.0, None, ALU.mult), wait=False)
            do(dve.tensor_scalar(prm[:, 7, :], m3[:], -8.0, None, ALU.mult))
            block_per = 9
            with dve.Fori(0, NB // 2) as i:
                do.enter(i, 2 * block_per)
                for par in range(2):
                    block_dve(dve, do, 2 * i + par, par)
                do.leave(NB // 2)
            dve.wait_ge(y_done, 1 + NB)


INPUTS = (
    "x", "meta", "l0_ln1_g", "l0_ln1_b", "l0_w_in", "l0_s5_lambda_re", "l0_s5_lambda_im", "l0_s5_log_dt", "l0_s5_b_re",
    "l0_s5_b_im", "l0_s5_c_re", "l0_s5_c_im", "l0_s5_d", "l0_s5_w_glu", "l0_s5_b_glu", "l0_da_lq1", "l0_da_lk1",
    "l0_da_lq2", "l0_da_lk2", "l0_da_subln_g", "l0_w_out", "l0_ln2_g", "l0_ln2_b", "l0_moe_w_coarse",
    "l0_moe_b_coarse", "l0_moe_w_fine", "l0_moe_b_fine", "l0_moe_w_gate", "l0_moe_w_up", "l0_moe_w_down", "l1_ln1_g",
    "l1_ln1_b", "l1_w_in", "l1_conv_w", "l1_conv_b", "l1_lru_w_a", "l1_lru_b_a", "l1_lru_w_x", "l1_lru_b_x",
    "l1_lru_lambda", "l1_w_out", "l1_ln2_g", "l1_ln2_b", "l1_moe_w_coarse", "l1_moe_b_coarse", "l1_moe_w_fine",
    "l1_moe_b_fine", "l1_moe_w_gate", "l1_moe_w_up", "l1_moe_w_down")


class Kept:

    def __init__(self, nc):
        self.nc, self.sems = nc, []

    def sem(self, name):
        self.sems.append(self.nc.alloc_semaphore(name))
        return self.sems[-1]

    def end_phase(self):
        self.nc.clear_and_free_semaphores(self.sems)
        self.nc.all_engine_barrier()
        self.sems = []


def hybrid_block_kernel(nc, A, out):
    K = Kept(nc)
    K.A = A
    K.out = out.rearrange("a b d -> (a b) d")
    scratch = lambda n, rows: nc.dram_tensor(n, [rows, D], F32, kind="Internal").ap()
    K.h1_dram, K.h2_dram, K.y_dram = scratch("h1_rows", T), scratch("h2_rows", T), scratch("expert_rows", 2 * T)
    at = Place(nc, nc.sbuf_base)
    K.ident, K.logits = at("ident", [P]), at("logits", [NT, 36])
    K.tok_idx, K.row_idx, K.gates = at("tok_idx", [NBLK], U32), at("row_idx", [NBLK], U32), at("gates", [NBLK])
    K.over = at("over", [NOVER + 1], I32)
    K.base = at.at
    H_BYTES = NT * D * 4
    K.h_at = (nc.sbuf_usable_end - H_BYTES) // 32 * 32
    K.H = nc.alloc_sbuf_tensor_at("H", [P, NT, D], F32, offset=K.h_at)
    W_BYTES = [KD * D * 4, NB * D * 4]
    K.w_out0_at, K.w_out1_at = ((K.h_at - w) // 32 * 32 for w in W_BYTES)
    K.w_out = [Place(nc, K.w_out0_at)("w_out0", [KD, D]), Place(nc, K.w_out1_at)("w_out1", [NB, D])]
    K.w_out_loaded = [nc.alloc_semaphore(f"w_out{i}_loaded") for i in range(2)]

    at = Place(nc, K.base)
    K.yT = at("yT", [4, T])
    K.free_s5 = at.at
    K.s5_d, K.mag, K.s5_zero = at("s5_d", [4]), at("mag", [S5_PAIRS]), at("s5_zero", [1])
    K.b_lhs, K.c_lhs = at("b_lhs", [2, 4, 4, P]), at("c_lhs", [2, 4, P])
    K.cs, K.sn = at("cs", [S5_PAIRS, WIN + 1]), at("sn", [S5_PAIRS, WIN + 1])
    K.free_zt = at.at
    K.zT = at("zT", [12, T])
    K.free_loop = at.at
    make_constants(nc, K)
    K.end_phase()
    s5_prepare(nc, K, A)
    K.end_phase()
    s5_and_projections(nc, K, A)
    K.end_phase()
    s5_gate(nc, K, A)
    K.end_phase()
    attention(nc, K, A)
    K.end_phase()
    x, meta = A["x"].rearrange("a b d -> (a b) d"), A["meta"]
    rows0 = lambda i: meta if i == 0 else x[P * (i - 1):P * i, :]
    slices = [K.yT[:, k, :] for k in range(4)] + [K.daT[:, k, :] for k in range(HEADS)]
    project_and_norm(nc, K, A, 0, slices, Place(nc, K.free_zt), rows0)
    K.end_phase()
    route(nc, K, 0)
    K.end_phase()
    experts(nc, K, A, 0)
    K.end_phase()
    combine_and_norm(nc, K, A, 0)
    K.end_phase()

    K.free_hT = K.base + KD * T * 4
    rglru(nc, K, A)
    K.end_phase()
    rows1 = lambda i: K.h2_dram[TILES[i][0]:TILES[i][0] + TILES[i][1], :]
    project_and_norm(nc, K, A, 1, [K.y1T[:, k, :] for k in range(NB)], Place(nc, K.base), rows1)
    K.end_phase()
    route(nc, K, 1)
    K.end_phase()
    experts(nc, K, A, 1)
    K.end_phase()
    combine_and_norm(nc, K, A, 1)


def kernel(**inputs):
    import concourse.bacc as bacc
    from concourse.bass_utils import run_bass_kernel_spmd

    nc = bacc.Bacc("TRN2", target_bir_lowering=False, num_devices=1)
    arrays, A = {}, {}
    for name in INPUTS:
        a = np.ascontiguousarray(inputs[name])
        arrays[f"in_{name}"] = a
        A[name] = nc.dram_tensor(f"in_{name}", a.shape, mybir.dt.from_np(a.dtype), kind="ExternalInput").ap()
    out = nc.dram_tensor("out", (1, SEQ, D), F32, kind="ExternalOutput").ap()
    hybrid_block_kernel(nc, A, out)
    r = run_bass_kernel_spmd(nc, [arrays], core_ids=[0])
    return r.results[0]["out"]
```

```python
from contextlib import ExitStack

import numpy as np
import concourse.bass as bass
from concourse import mybir

P = 128
F32 = mybir.dt.float32
I32 = mybir.dt.int32
U32 = mybir.dt.uint32
ALU = mybir.AluOpType
ACT = mybir.ActivationFunctionType
AX_X = mybir.AxisListType.X
ds = bass.ds

D = 1024
KD = D // P
N_META = 16
SEQ = 1024
T = N_META + SEQ
TILES = [(0, N_META)] + [(N_META + P * i, P) for i in range(SEQ // P)]
NT = len(TILES)
DEPTH = 2
ALPHA = (2 * DEPTH) ** 0.25
LN_EPS = 1e-5
S5W = 512
S5_STATES = 64
S5_PAIRS = 16
HEADS = 4
HEAD_DIM = 64
LAM_INIT = 0.2
NEG = -1e30
WIN = 116
NWIN = -(-T // WIN)
LAST = T - (NWIN - 1) * WIN
D_RNN = 1280
NB = D_RNN // P
GROUPS, PER_GROUP = 4, 8
NE = GROUPS * PER_GROUP
F = 512
CHUNKS = [(0, 352), (352, 352), (704, 336)]
TWO_PI = 6.283185307179586
PI_HI = 6.28125
PI_MID = 0.00193500518798828125
PI_LO = TWO_PI - PI_HI - PI_MID
ROUND_MAGIC = 12582912.0


class Place:

    def __init__(self, nc, start):
        self.nc, self.at = nc, start

    def __call__(self, name, shape, dt=F32):
        self.at = (self.at + 31) // 32 * 32
        t = self.nc.alloc_sbuf_tensor_at(name, [P] + shape, dt, offset=self.at)
        self.at += int(np.prod(shape)) * 4
        assert self.at <= self.nc.sbuf_usable_end, (name, self.at)
        return t


class Order:

    def __init__(self, eng, sem):
        self.eng, self.sem, self.base, self.k = eng, sem, 0, 0

    def __call__(self, ins, wait=True):
        self.k += 1
        ins.then_inc(self.sem, 1)
        if wait:
            self.wait()

    def wait(self):
        self.eng.wait_ge(self.sem, self.base + self.k)

    def enter(self, i, per):
        self.outer, self.per = self.base + self.k, per
        self.base, self.k = self.outer + i * per, 0

    def leave(self, count):
        assert self.k == self.per, (self.k, self.per)
        self.base, self.k = self.outer + count * self.per, 0


def bc(ap, n):
    return ap.unsqueeze(2).to_broadcast([ap.shape[0], ap.shape[1], n])


def make_constants(nc, K):
    made = K.sem("identity_made")
    with nc.Block() as block:
        @block.gpsimd
        def _(pool):
            pool.memset(K.ident[:], 0.0).then_inc(made, 1)
            pool.wait_ge(made, 1)
            pool.affine_select(out=K.ident[:], in_=K.ident[:], compare_op=ALU.not_equal, fill=1.0, base=0,
                               pattern=[[-1, P]], channel_multiplier=1).then_inc(made, 1)
            pool.wait_ge(made, 2)


def s5_prepare(nc, K, A):
    at = Place(nc, K.free_zt)
    small = {n: at("s5_" + n, [S5_PAIRS]) for n in (
        "lre", "lim", "dt", "lr", "xr", "ph", "n", "r", "rc", "ai", "ar", "nr", "den", "a", "b", "fr", "fi")}
    S = lambda n: small[n][:]
    b_re, b_im = at("s5_bre", [S5_PAIRS, 16]), at("s5_bim", [S5_PAIRS, 16])
    bd_re, bd_im = at("s5_bdre", [S5_PAIRS, 32]), at("s5_bdim", [S5_PAIRS, 32])
    c_re, c_im = at("s5_cre", [4, P]), at("s5_cim", [4, P])
    t1, t2 = at("s5_t1", [S5_PAIRS, 64]), at("s5_t2", [S5_PAIRS, 64])
    m1, m2 = at("s5_m1", [2, S5_PAIRS]), at("s5_m2", [2, S5_PAIRS])
    zeroed, loaded = K.sem("s5_zeroed"), K.sem("s5_loaded")
    dve_order, act_done = K.sem("s5p_dve_order"), K.sem("s5p_act_done")
    pe_done, ready = K.sem("s5p_pe_done"), K.sem("s5p_ready")
    asked = K.sem("s5p_asked")
    assert at.at <= K.free_loop
    N_LOADS = 5 + 2 + 16
    with nc.psum_tensor("s5p_ps", [P, 4, 512], F32) as ps, nc.Block() as block:
        @block.sync
        def _(sp):
            with nc.allow_non_contiguous_dma(reason="small parameters"):
                sp.dma_start(small["lre"][:], A["l0_s5_lambda_re"].rearrange("(s two) p -> (two p) s", two=2)).then_inc(loaded, 16)
                sp.dma_start(small["lim"][:], A["l0_s5_lambda_im"].rearrange("(s two) p -> (two p) s", two=2)).then_inc(loaded, 16)
                dt = A["l0_s5_log_dt"].rearrange("(s two) -> two s", two=2)
                for two in range(2):
                    sp.dma_start(small["dt"][64 * two:64 * two + 64, :], dt[two:two + 1, :].to_broadcast([64, S5_PAIRS])).then_inc(loaded, 16)
                sp.dma_start(K.s5_d[:], A["l0_s5_d"].rearrange("(t p) -> p t", p=P)).then_inc(loaded, 16)
                sp.dma_start(b_re[:], A["l0_s5_b_re"].rearrange("(s two) p h -> (two p) s h", two=2)).then_inc(loaded, 16)
                sp.dma_start(b_im[:], A["l0_s5_b_im"].rearrange("(s two) p h -> (two p) s h", two=2)).then_inc(loaded, 16)
                sp.wait_ge(zeroed, 4)
                for j in range(8):
                    for c, src in ((c_re, "l0_s5_c_re"), (c_im, "l0_s5_c_im")):
                        sp.dma_start(c[16 * j:16 * j + 16, :, 64 * (j % 2):64 * (j % 2) + 64],
                                     A[src].rearrange("(t j) h p -> j h t p", j=8)[j]).then_inc(loaded, 16)
            w = A["l0_w_in"].rearrange("(k p) c -> p k c", p=P)
            for c in range(4):
                sp.dma_start(K.w_in[:, :, 512 * c:512 * c + 512], w[:, :, 512 * c:512 * c + 512]).then_inc(K.w_in_loaded[c], 16)

        @block.gpsimd
        def _(pool):
            for t in (bd_re, bd_im, c_re, c_im, K.b_lhs):
                pool.memset(t[:], 0.0).then_inc(zeroed, 1)

        @block.vector
        def _(dve):
            do = Order(dve, dve_order)
            tt, tsc = dve.tensor_tensor, dve.tensor_scalar
            dve.wait_ge(loaded, 16 * N_LOADS)
            do(tsc(S("lr"), S("lre"), -1e-4, None, ALU.min))
            dve.wait_ge(act_done, 1)
            do(tt(S("xr"), S("lr"), S("dt"), ALU.mult), wait=False)
            do(tt(S("ph"), S("lim"), S("dt"), ALU.mult))
            do(tsc(S("n"), S("ph"), 1.0 / TWO_PI, ROUND_MAGIC, ALU.mult, ALU.add))
            do(tsc(S("n"), S("n"), -ROUND_MAGIC, None, ALU.add))
            do(dve.scalar_tensor_tensor(out=S("r"), in0=S("n"), scalar=-PI_HI, in1=S("ph"), op0=ALU.mult, op1=ALU.add))
            do(dve.scalar_tensor_tensor(out=S("r"), in0=S("n"), scalar=-PI_MID, in1=S("r"), op0=ALU.mult, op1=ALU.add))
            do(dve.scalar_tensor_tensor(out=S("r"), in0=S("n"), scalar=-PI_LO, in1=S("r"), op0=ALU.mult, op1=ALU.add))
            do(tsc(S("r"), S("r"), 3.1415925, -3.1415925, ALU.min, ALU.max))
            do(tsc(S("rc"), S("r"), -1.0, None, ALU.mult))
            do(tt(S("rc"), S("rc"), S("r"), ALU.min))
            do(tsc(S("rc"), S("rc"), TWO_PI / 4, None, ALU.add), wait=False)
            dve.memset(K.cs[:, :, 0:1], 1.0).then_inc(asked, 1)
            dve.memset(K.sn[:, :, 0:1], 0.0).then_inc(asked, 1)
            dve.wait_ge(asked, 2)
            dve.wait_ge(act_done, 4)
            c1, s1 = K.cs[:, :, 1], K.sn[:, :, 1]
            do(tt(S("ar"), K.mag[:], c1, ALU.mult), wait=False)
            do(tt(S("ai"), K.mag[:], s1, ALU.mult))
            do(tsc(S("nr"), S("ar"), -1.0, None, ALU.add), wait=False)
            do(tt(S("a"), S("lr"), S("lr"), ALU.mult), wait=False)
            do(tt(S("b"), S("lim"), S("lim"), ALU.mult))
            do(tt(S("den"), S("a"), S("b"), ALU.add))
            do(dve.reciprocal(S("den"), S("den")), wait=False)
            do(tt(S("a"), S("nr"), S("lr"), ALU.mult), wait=False)
            do(tt(S("b"), S("ai"), S("lim"), ALU.mult))
            do(tt(S("fr"), S("a"), S("b"), ALU.add))
            do(tt(S("a"), S("ai"), S("lr"), ALU.mult), wait=False)
            do(tt(S("b"), S("nr"), S("lim"), ALU.mult), wait=False)
            do(tt(S("fr"), S("fr"), S("den"), ALU.mult))
            do(tt(S("fi"), S("a"), S("b"), ALU.subtract))
            do(tt(S("fi"), S("fi"), S("den"), ALU.mult))
            fr, fi = bc(S("fr"), 16), bc(S("fi"), 16)
            do(tt(t1[:, :, 0:16], fr, b_re[:], ALU.mult), wait=False)
            do(tt(t1[:, :, 16:32], fi, b_im[:], ALU.mult), wait=False)
            do(tt(t1[:, :, 32:48], fr, b_im[:], ALU.mult), wait=False)
            do(tt(t1[:, :, 48:64], fi, b_re[:], ALU.mult))
            dve.wait_ge(zeroed, 4)
            for g in range(2):
                rows = slice(64 * g, 64 * g + 64)
                do(tt(bd_re[rows, :, 16 * g:16 * g + 16], t1[rows, :, 0:16], t1[rows, :, 16:32], ALU.subtract))
                do(tt(bd_im[rows, :, 16 * g:16 * g + 16], t1[rows, :, 32:48], t1[rows, :, 48:64], ALU.add))
            dve.memset(K.s5_zero[:], 0.0).then_inc(ready, 1)
            do(dve.tensor_copy(m1[:, 0, :], c1), wait=False)
            do(dve.tensor_copy(m1[:, 1, :], s1))
            cur, nxt, m, have = m1, m2, 1, 2
            while have < WIN + 1:
                do(tt(t1[:, :, 0], cur[:, 0, :], cur[:, 0, :], ALU.mult), wait=False)
                do(tt(t1[:, :, 1], cur[:, 1, :], cur[:, 1, :], ALU.mult), wait=False)
                do(tt(t1[:, :, 2], cur[:, 0, :], cur[:, 1, :], ALU.mult))
                do(tt(nxt[:, 0, :], t1[:, :, 0], t1[:, :, 1], ALU.subtract), wait=False)
                do(tt(nxt[:, 1, :], t1[:, :, 2], t1[:, :, 2], ALU.add))
                cur, nxt, m = nxt, cur, 2 * m
                n = min(m, WIN + 1 - m)
                cm, sm = bc(cur[:, 0, :], n), bc(cur[:, 1, :], n)
                cj, sj = K.cs[:, :, 0:n], K.sn[:, :, 0:n]
                do(tt(t1[:, :, 0:n], cj, cm, ALU.mult), wait=False)
                do(tt(t2[:, :, 0:n], sj, sm, ALU.mult))
                do(tt(K.cs[:, :, m:m + n], t1[:, :, 0:n], t2[:, :, 0:n], ALU.subtract))
                do(tt(t1[:, :, 0:n], sj, cm, ALU.mult), wait=False)
                do(tt(t2[:, :, 0:n], cj, sm, ALU.mult))
                do(tt(K.sn[:, :, m:m + n], t1[:, :, 0:n], t2[:, :, 0:n], ALU.add))
                have = m + n
            dve.wait_ge(pe_done, 1)
            dve.wait_ge(zeroed, 5)
            for s in range(4):
                rows = slice(32 * s, 32 * s + 32)
                do(dve.tensor_copy(K.b_lhs[rows, 0, :, s, :], ps[rows, 0, :].rearrange("p (t c) -> p t c", t=4)), wait=False)
            do(tsc(K.c_lhs[:, 1, :, :], ps[:, 3, :].rearrange("p (t c) -> p t c", t=4), -1.0, None, ALU.mult))

        @block.scalar
        def _(act):
            act.wait_ge(loaded, 16 * N_LOADS)
            act.activation(S("dt"), S("dt"), ACT.Exp).then_inc(act_done, 1)
            act.wait_ge(dve_order, 3)
            act.activation(K.mag[:], S("xr"), ACT.Exp).then_inc(act_done, 1)
            act.wait_ge(dve_order, 12)
            act.wait_ge(asked, 2)
            act.activation(K.cs[:, :, 1], S("rc"), ACT.Sin).then_inc(act_done, 1)
            act.activation(K.sn[:, :, 1], S("r"), ACT.Sin).then_inc(act_done, 1)
            act.wait_ge(pe_done, 1)
            act.wait_ge(zeroed, 5)
            for s in range(4):
                rows = slice(32 * s, 32 * s + 32)
                act.copy(K.b_lhs[rows, 1, :, s, :], ps[rows, 1, :].rearrange("p (t c) -> p t c", t=4)).then_inc(act_done, 1)
            act.copy(K.c_lhs[:, 0, :, :], ps[:, 2, :].rearrange("p (t c) -> p t c", t=4)).then_inc(act_done, 1)
            act.wait_ge(act_done, 9)

        @block.tensor
        def _(pe):
            pe.wait_ge(ready, 1)
            for c, src in enumerate((bd_re, bd_im)):
                for t in range(4):
                    pe.transpose(ps[:, c, P * t:P * t + P], src[:, 4 * t:4 * t + 4, :].rearrange("p s h -> p (s h)"), K.ident[:])
            pe.wait_ge(loaded, 16 * N_LOADS)
            for c, src in enumerate((c_re, c_im)):
                for t in range(4):
                    last = pe.transpose(ps[:, 2 + c, P * t:P * t + P], src[:, t, :], K.ident[:])
            last.then_inc(pe_done, 1)


def s5_and_projections(nc, K, A):
    at = Place(nc, K.free_w_in)
    w_in, w_loaded = K.w_in, K.w_in_loaded
    rows_sb = at("h_rows", [D])
    hT = at("hT_window", [KD, WIN])
    uW = at("u_window", [4, WIN])
    q4 = [4, WIN]
    rot = [at(f"s5_rot{i}", q4) for i in range(4)]
    g = [[at(f"s5_g{b}{c}", q4) for c in range(2)] for b in range(2)]
    h = [[at(f"s5_h{b}{c}", q4) for c in range(2)] for b in range(2)]
    pt = [at(f"s5_pt{i}", q4) for i in range(4)]
    init = at("s5_init", [2, S5_PAIRS])
    ca = at("s5_carry", [4, 4])
    yT, zT = K.yT, K.zT
    sem = lambda n: K.sem("s5_" + n)
    rows_loaded, rows_used, hT_ready = sem("rows_loaded"), sem("rows_used"), sem("hT_ready")
    u_ready, u_copied, bu_ready, bu_used = sem("u_ready"), sem("u_copied"), sem("bu_ready"), sem("bu_used")
    z_ready, z_copied, g_ready, h_ready = sem("z_ready"), sem("z_copied"), sem("g_ready"), sem("h_ready")
    y_ready, y_used, dve_order, pool_order = sem("y_ready"), sem("y_used"), sem("dve_order"), sem("pool_order")
    x, meta = A["x"].rearrange("a b d -> (a b) d"), A["meta"]
    with ExitStack() as ctx:
        psum = lambda n: ctx.enter_context(nc.psum_tensor(n, [P, 512], F32))
        p_u = psum("p_u")
        p_z = [psum(f"p_z{i}") for i in range(2)]
        p_b = [[psum(f"p_b{b}{c}") for c in range(2)] for b in range(2)]
        p_y = psum("p_y")
        v4 = lambda t: t[:, 0:4 * WIN].rearrange("p (s w) -> p s w", s=4)
        block = ctx.enter_context(nc.Block())

        @block.sync
        def _(sp):
            sp.dma_start(rows_sb[0:N_META, :], meta).then_inc(rows_loaded, 16)
            sp.dma_start(rows_sb[N_META:WIN, :], x[0:WIN - N_META, :]).then_inc(rows_loaded, 16)
            with sp.Fori(1, NWIN - 1) as i:
                sp.wait_ge(rows_used, i)
                sp.dma_start(rows_sb[0:WIN, :], x[ds(i * WIN - N_META, WIN), :]).then_inc(rows_loaded, 16)
            sp.wait_ge(rows_used, NWIN - 1)
            sp.dma_start(rows_sb[0:LAST, :], x[SEQ - LAST:SEQ, :]).then_inc(rows_loaded, 16)

        def turn_rows(pe, half, n=WIN):
            for k in range(4 * half, 4 * half + 4):
                last = pe.transpose(p_z[half][:, WIN * (k % 4):WIN * (k % 4) + n], rows_sb[0:n, P * k:P * k + P], K.ident[0:n, 0:n])
            return last

        def pe_window(pe, w, first=False, final=False, n_next=WIN):
            if first:
                pe.wait_ge(rows_loaded, 32)
                turn_rows(pe, 0)
                turn_rows(pe, 1).then_inc(rows_used, 1)
            pe.wait_ge(hT_ready, 2 * (w + 1))
            if first:
                pe.wait_ge(w_loaded[0], 16)
            for t in range(4):
                for k in range(KD):
                    last = pe.matmul(p_u[:, WIN * t:WIN * t + WIN], w_in[:, k, P * t:P * t + P], hT[:, k, :], start=k == 0, stop=k == KD - 1)
            last.then_inc(u_ready, 1)
            for q in range(4):
                step = 4 * w + q
                if not first or q >= 2:
                    pe.wait_ge(z_copied, step - 1)
                for j in range(3):
                    f = S5W + P * (3 * q + j)
                    if first:
                        pe.wait_ge(w_loaded[f // 512], 16)
                    for k in range(KD):
                        last = pe.matmul(p_z[q % 2][:, WIN * j:WIN * j + WIN], w_in[:, k, f:f + P], hT[:, k, :], start=k == 0, stop=k == KD - 1)
                last.then_inc(z_ready, 1)
                if q == 3 and not final:
                    pe.wait_ge(rows_loaded, 16 * (w + 3))
                    pe.wait_ge(z_copied, 4 * w + 3)
                    turn_rows(pe, 0, n_next)
                if q == 0:
                    pe.wait_ge(u_copied, 2 * (w + 1))
                if not first or q >= 2:
                    pe.wait_ge(bu_used, step - 1)
                for c in range(2):
                    for s in range(4):
                        last = pe.matmul(p_b[q % 2][c][:, WIN * s:WIN * s + WIN], K.b_lhs[:, c, q, s, :], uW[:, q, :], start=True, stop=True)
                last.then_inc(bu_ready, 1)
                if q == 3 and not final:
                    pe.wait_ge(z_copied, 4 * w + 4)
                    turn_rows(pe, 1, n_next).then_inc(rows_used, 1)
                if not first or q >= 2:
                    y_product(pe, step - 2, q, not first or q > 2)

        def y_product(pe, step, q, wait):
            pe.wait_ge(h_ready, step + 1)
            if wait:
                pe.wait_ge(y_used, step)
            for s in range(4):
                for c in range(2):
                    last = pe.matmul(p_y[32 * s:32 * s + 32, 0:WIN], K.c_lhs[:, c, (q - 2) % 4, 32 * s:32 * s + 32],
                                     h[q % 2][c][:, s, :], start=c == 0, stop=c == 1)
            last.then_inc(y_ready, 1)

        @block.tensor
        def _(pe):
            pe_window(pe, 0, first=True)
            with pe.Fori(1, NWIN - 2) as i:
                pe_window(pe, i)
            pe_window(pe, NWIN - 2, n_next=LAST)
            pe_window(pe, NWIN - 1, final=True)
            for q in range(2):
                y_product(pe, 4 * NWIN - 2 + q, q, True)

        def act_window(act, w, n=WIN):
            col = ds(w * WIN, n)
            act.wait_ge(rows_used, w + 1)
            for i in range(2):
                act.copy(hT[:, 4 * i:4 * i + 4, :], v4(p_z[i])).then_inc(hT_ready, 1)
            act.wait_ge(u_ready, w + 1)
            act.copy(uW[:], v4(p_u)).then_inc(u_copied, 1)
            act.copy(yT[:, :, col], v4(p_u)[:, :, 0:n]).then_inc(u_copied, 1)
            for q in range(4):
                act.wait_ge(z_ready, 4 * w + q + 1)
                act.copy(zT[:, 3 * q:3 * q + 3, col], p_z[q % 2][:, 0:3 * WIN].rearrange("p (j w) -> p j w", j=3)[:, :, 0:n]).then_inc(z_copied, 1)

        @block.scalar
        def _(act):
            with act.Fori(0, NWIN - 1) as i:
                act_window(act, i)
            act_window(act, NWIN - 1, LAST)

        def y_add(dve, step, q, w, n=WIN):
            dve.wait_ge(y_ready, step + 1)
            f = (q - 2) % 4
            cols = yT[:, f, ds((w if q >= 2 else w - 1) * WIN, n)]
            dve.scalar_tensor_tensor(out=cols, in0=cols, scalar=K.s5_d[:, f:f + 1], in1=p_y[:, 0:n],
                                     op0=ALU.mult, op1=ALU.add).then_inc(y_used, 1)

        def dve_window(dve, do, w, first, n_out=WIN):
            tt = dve.tensor_tensor
            for q in range(4):
                step = 4 * w + q
                cj, sj = K.cs[:, 4 * q:4 * q + 4, 0:WIN], K.sn[:, 4 * q:4 * q + 4, 0:WIN]
                br, bi = v4(p_b[q % 2][0]), v4(p_b[q % 2][1])
                dve.wait_ge(bu_ready, step + 1)
                do(tt(rot[0][:], br, cj, ALU.mult), wait=False)
                do(tt(rot[1][:], bi, sj, ALU.mult), wait=False)
                do(tt(rot[2][:], bi, cj, ALU.mult), wait=False)
                tt(rot[3][:], br, sj, ALU.mult).then_inc(bu_used, 1)
                dve.wait_ge(bu_used, step + 1)
                do(tt(rot[0][:], rot[0][:], rot[1][:], ALU.add), wait=False)
                do(tt(rot[2][:], rot[2][:], rot[3][:], ALU.subtract))
                if not first or q >= 2:
                    dve.wait_ge(h_ready, step - 1)
                for s in range(4):
                    n = 4 * q + s
                    for c in range(2):
                        scan = dve.tensor_tensor_scan(g[q % 2][c][:, s, :], K.mag[:, n:n + 1].to_broadcast([P, WIN]), rot[2 * c][:, s, :],
                                                      K.s5_zero[:] if first else init[:, c, n:n + 1], ALU.mult, ALU.add)
                        if s == 3 and c == 1:
                            scan.then_inc(g_ready, 1)
                        else:
                            do(scan, wait=False)
                dve.wait_ge(g_ready, step + 1)
                ge = [g[q % 2][c][:, :, WIN - 1] for c in range(2)]
                cw, sw = K.cs[:, 4 * q:4 * q + 4, WIN], K.sn[:, 4 * q:4 * q + 4, WIN]
                do(tt(ca[:, 0, :], ge[0], cw, ALU.mult), wait=False)
                do(tt(ca[:, 1, :], ge[1], sw, ALU.mult), wait=False)
                do(tt(ca[:, 2, :], ge[0], sw, ALU.mult), wait=False)
                do(tt(ca[:, 3, :], ge[1], cw, ALU.mult))
                do(tt(init[:, 0, 4 * q:4 * q + 4], ca[:, 0, :], ca[:, 1, :], ALU.subtract), wait=False)
                do(tt(init[:, 1, 4 * q:4 * q + 4], ca[:, 2, :], ca[:, 3, :], ALU.add))
                if not first or q >= 2:
                    y_add(dve, step - 2, q, w, n_out if q >= 2 else WIN)

        @block.vector
        def _(dve):
            do = Order(dve, dve_order)
            dve.wait_ge(u_copied, 2)
            dve_window(dve, do, 0, True)
            per = do.k
            with dve.Fori(1, NWIN - 1) as i:
                do.enter(i - 1, per)
                dve_window(dve, do, i, False)
                do.leave(NWIN - 2)
            dve_window(dve, do, NWIN - 1, False, LAST)
            for q in range(2):
                y_add(dve, 4 * NWIN - 2 + q, q, NWIN, LAST)
            dve.wait_ge(y_used, 4 * NWIN)

        def pool_window(pool, do, w, first):
            tt = pool.tensor_tensor
            for q in range(4):
                step = 4 * w + q
                cj, sj = K.cs[:, 4 * q:4 * q + 4, 0:WIN], K.sn[:, 4 * q:4 * q + 4, 0:WIN]
                gr, gi = g[q % 2][0][:], g[q % 2][1][:]
                if not first or q:
                    pool.wait_ge(h_ready, step)
                pool.wait_ge(g_ready, step + 1)
                do(tt(pt[0][:], gr, cj, ALU.mult), wait=False)
                do(tt(pt[1][:], gi, sj, ALU.mult), wait=False)
                do(tt(pt[2][:], gr, sj, ALU.mult), wait=False)
                do(tt(pt[3][:], gi, cj, ALU.mult))
                if not first or q >= 2:
                    pool.wait_ge(y_ready, step - 1)
                do(tt(h[q % 2][0][:], pt[0][:], pt[1][:], ALU.subtract), wait=False)
                tt(h[q % 2][1][:], pt[2][:], pt[3][:], ALU.add).then_inc(h_ready, 1)

        @block.gpsimd
        def _(pool):
            do = Order(pool, pool_order)
            pool_window(pool, do, 0, True)
            per = do.k
            with pool.Fori(1, NWIN) as i:
                do.enter(i - 1, per)
                pool_window(pool, do, i, False)
                do.leave(NWIN - 1)


def s5_gate(nc, K, A):
    at = Place(nc, K.free_loop)
    gT, w_glu, b_glu, gate = at("glu_g", [4, T]), at("w_glu", [4, S5W]), at("b_glu", [4]), at("glu_gate", [2, T])
    sem = lambda n: K.sem("glu_" + n)
    loaded, gelu_done, lin_ready, gate_ready, out_done = sem("loaded"), sem("gelu_done"), sem("lin_ready"), sem("gate_ready"), sem("out_done")
    yT = K.yT
    with nc.psum_tensor("p_glu", [P, 2, 3, 512], F32) as ps, nc.Block() as block:
        @block.sync
        def _(sp):
            sp.dma_start(w_glu[:], A["l0_s5_w_glu"].rearrange("(k p) c -> p k c", p=P)).then_inc(loaded, 16)
            with nc.allow_non_contiguous_dma(reason="a bias by partition"):
                sp.dma_start(b_glu[:], A["l0_s5_b_glu"].rearrange("(t p) -> p t", p=P)).then_inc(loaded, 16)

        @block.scalar
        def _(act):
            for k in range(4):
                act.activation(gT[:, k, :], yT[:, k, :], ACT.Gelu_apprx_tanh).then_inc(gelu_done, 1)
            act.wait_ge(loaded, 32)
            for f in range(4):
                act.wait_ge(lin_ready, f + 1)
                if f >= 2:
                    act.wait_ge(out_done, f - 1)
                for j, (o, n) in enumerate(CHUNKS):
                    act.activation(gate[:, f % 2, o:o + n], ps[:, f % 2, j, 0:n], ACT.Sigmoid, bias=b_glu[:, f:f + 1]).then_inc(gate_ready, 1)

        @block.tensor
        def _(pe):
            pe.wait_ge(loaded, 32)
            pe.wait_ge(gelu_done, 4)
            for f in range(4):
                if f >= 2:
                    pe.wait_ge(gate_ready, 3 * (f - 1))
                for j, (o, n) in enumerate(CHUNKS):
                    for k in range(4):
                        last = pe.matmul(ps[:, f % 2, j, 0:n], w_glu[:, k, P * f:P * f + P], gT[:, k, o:o + n], start=k == 0, stop=k == 3)
                last.then_inc(lin_ready, 1)

        @block.vector
        def _(dve):
            for f in range(4):
                dve.wait_ge(gate_ready, 3 * (f + 1))
                dve.tensor_tensor(yT[:, f, :], gT[:, f, :], gate[:, f % 2, :], ALU.mult).then_inc(out_done, 1)
            dve.wait_ge(out_done, 4)


def attention(nc, K, A):
    at = Place(nc, K.free_loop)
    K.daT = at("daT", [HEADS, T])
    K.free_da = at.at
    low, top = Place(nc, K.free_s5), Place(nc, K.h_at)
    qh, kh, vh = ([low(f"{x}_head{i}", [T]) for i in range(2)] for x in "qkv")
    v_rows = low("v_rows", [NT, P])
    probs = [[top(f"prob{b}{c}", [T]) for c in range(2)] for b in range(2)]
    w = low("w_rows", [T])
    tail_sb = at("scores_tail_sb", [2, N_META])
    mx2, l2 = at("row_max2", [2]), at("row_sum2", [2, 2])
    wT = at("w_cols", [NT, P])
    hide, ones = at("hide", [P]), at("ones64", [64])
    lq = [at(f"lq{i}", [HEAD_DIM]) for i in range(4)]
    ldot, lexp, nlam = at("ldot", [2]), at("lexp", [2]), at("nlam", [1])
    prod = at("lprod", [HEAD_DIM])
    mx, nb, r, nl = at("row_max", [2]), at("row_bias", [2]), at("row_rec", [2]), at("row_nl", [1])
    sums = [at(f"row_sum{b}", [2]) for b in range(2)]
    assert at.at <= K.w_out0_at and low.at <= K.free_zt
    o_sb, sq = top("o_rows", [NT, 512]), top("o_sq", [2 * P])
    ss, rs, g = top("o_ss", [NT * HEADS]), top("o_rs", [NT * HEADS]), top("subln", [1])
    zT, scale = K.zT, HEAD_DIM ** -0.5
    sem = lambda n: K.sem("da_" + n)
    (loaded, hide_made, lam_ready, staged, s_ready, nb_ready, exp_done, w_ready, tp_ready, tp_copied, o_ready, o_copied,
     dve_order, lexp_done, tp_clear, met, tail_done) = map(sem, (
        "loaded", "hide_made", "lam_ready", "staged", "s_ready", "nb_ready", "exp_done", "w_ready", "tp_ready",
        "tp_copied", "o_ready", "o_copied", "dve_order", "lexp_done", "tp_clear", "met", "tail_done"))
    GRP = [i // 4 + 1 for i in range(NT)]
    TP0 = 3
    TPH = TP0 + sum(GRP)
    WIDE = 1024
    tp_at = lambda qi: TP0 + sum(GRP[:qi])
    with ExitStack() as ctx:
        S = [ctx.enter_context(nc.psum_tensor(f"scores{c}", [P, WIDE], F32)) for c in range(2)]
        tail = ctx.enter_context(nc.psum_tensor("scores_tail", [P, 2, N_META], F32))
        tps = [ctx.enter_context(nc.psum_tensor(f"tp{i}", [P, 4, P], F32)) for i in range(2)]
        po = ctx.enter_context(nc.psum_tensor("po", [P, 512], F32))
        block = ctx.enter_context(nc.Block())

        @block.sync
        def _(sp):
            with nc.allow_non_contiguous_dma(reason="small parameters"):
                for i, n in enumerate(("lq1", "lk1", "lq2", "lk2")):
                    sp.dma_start(lq[i][:], A["l0_da_" + n].rearrange("(a d) -> a d", a=1).to_broadcast([P, HEAD_DIM])).then_inc(loaded, 16)
                sp.dma_start(g[:], A["l0_da_subln_g"].rearrange("(p a) -> p a", a=1)).then_inc(loaded, 16)
            load_w_out(sp, K, 0)

        @block.gpsimd
        def _(pool):
            pool.memset(hide[:], 0.0).then_inc(hide_made, 1)
            pool.memset(ones[:], 1.0).then_inc(hide_made, 1)
            pool.wait_ge(hide_made, 2)
            for c in range(2):
                pool.memset(hide[64 * c:64 * c + 1, 0:64], NEG).then_inc(hide_made, 1)
            pool.wait_ge(hide_made, 4)
            pool.wait_ge(staged, 3)
            for hd in range(1, HEADS):
                if hd >= 2:
                    pool.wait_ge(o_ready, (hd - 1) * NT)
                for kind, t in enumerate((qh, kh, vh)):
                    pool.tensor_copy(t[hd % 2][:], zT[:, HEADS * kind + hd, :]).then_inc(staged, 1)

        def scores(pe, hd, par, qi):
            q0, m = TILES[qi]
            n = q0 + m
            cuts = list(range(0, n, 512)) + [n]

            def columns(c, a, b):
                r = slice(64 * c, 64 * c + 64)
                place = lambda a, b: S[c][0:m, a:b] if a < WIDE else tail[0:m, c, a - WIDE:b - WIDE]
                lo = max(a, n - 64) if qi else b
                if lo > a:
                    last = pe.matmul(place(a, min(lo, b)), qh[par][r, q0:q0 + m], kh[par][r, a:min(lo, b)], start=True, stop=True)
                if lo < b:
                    pe.matmul(place(lo, b), qh[par][r, q0:q0 + m], kh[par][r, lo:b], start=True, stop=False)
                    last = pe.matmul(place(lo, b), hide[r, 0:m], ones[r, 0:b - lo], start=False, stop=True)
                return last

            if n > WIDE:
                for c in range(2):
                    columns(c, WIDE, n).then_inc(tail_done, 1)
                    if c == 0:
                        pe.wait_ge(tail_done, 2 * hd + 1)
            for c in range(2):
                if qi == 0:
                    pe.wait_ge(exp_done, 1 + hd * NT * 2)
                    pe.sem_inc(met, 1)
                else:
                    pe.wait_ge(exp_done, 1 + (hd * NT + qi) * 2 + c - 1)
                for a, b in zip(cuts, cuts[1:]):
                    if a < WIDE:
                        last = columns(c, a, b)
                last.then_inc(s_ready, 1)

        def turn_w(pe, hd, par, qi):
            q0, m = TILES[qi]
            pe.wait_ge(w_ready, 1 + hd * NT + qi + 1)
            for gq in range(GRP[qi]):
                pe.wait_ge(tp_copied, 1 + hd * TPH + tp_at(qi) + gq - 1)
                tp = tps[(par * TPH + tp_at(qi) + gq) % 2]
                if qi == 0:
                    pe.sem_inc(met, 1)
                for kt in range(4 * gq, min(4 * gq + 4, qi + 1)):
                    k0, kk = TILES[kt]
                    last = pe.transpose(tp[0:kk, kt % 4, 0:m], w[0:m, k0:k0 + kk], K.ident[0:m, 0:m])
                last.then_inc(tp_ready, 1)

        def weigh(pe, hd, par, qi):
            q0, m = TILES[qi]
            pe.wait_ge(tp_copied, 1 + hd * TPH + tp_at(qi) + GRP[qi])
            pe.wait_ge(o_copied, 1 + hd * NT + qi)
            if qi == 0:
                pe.sem_inc(met, 1)
            for kt in range(qi + 1):
                kk = TILES[kt][1]
                last = pe.matmul(po[0:m, 0:P], wT[0:kk, kt, 0:m], v_rows[0:kk, kt, :], start=kt == 0, stop=kt == qi)
            last.then_inc(o_ready, 1)

        @block.tensor
        def _(pe):
            pe.sem_inc(tp_ready, 1)
            pe.wait_ge(hide_made, 4)
            pe.wait_ge(tp_clear, 2)
            def head(hd, par):
                pe.wait_ge(staged, 3 * hd + 3)
                vs = vh[par]
                for gv in range(TP0):
                    pe.wait_ge(tp_copied, 1 + hd * TPH + gv)
                    tp = tps[(par * TPH + gv) % 2]
                    for kt in range(4 * gv, min(4 * gv + 4, NT)):
                        k0, kk = TILES[kt]
                        last = pe.transpose(tp[0:kk, kt % 4, :], vs[:, k0:k0 + kk], K.ident[:])
                    last.then_inc(tp_ready, 1)
                for qi in range(NT):
                    if qi == 0:
                        scores(pe, hd, par, 0)
                    if qi + 1 < NT:
                        scores(pe, hd, par, qi + 1)
                    if qi:
                        weigh(pe, hd, par, qi - 1)
                    turn_w(pe, hd, par, qi)
                weigh(pe, hd, par, NT - 1)

            with pe.Fori(0, HEADS // 2) as i:
                for par in range(2):
                    head(2 * i + par, par)

        def exps(act, hd, qi, c):
            q0, m = TILES[qi]
            n = q0 + m
            if c == 0:
                act.wait_ge(w_ready, 1 + hd * NT + qi - 1)
            act.wait_ge(nb_ready, (hd * NT + qi) * 2 + c + 1)
            prob, kw = probs[qi % 2][c], dict(bias=nb[0:m, c:c + 1], scale=scale)
            if n <= WIDE:
                act.activation(prob[0:m, 0:n], S[c][0:m, 0:n], ACT.Exp, accum_out=sums[qi % 2][0:m, c:c + 1], **kw).then_inc(exp_done, 1)
            else:
                act.activation(prob[0:m, 0:WIDE], S[c][0:m, :], ACT.Exp, accum_out=l2[0:m, c, 0:1], **kw)
                act.activation(prob[0:m, WIDE:n], tail_sb[0:m, c, :], ACT.Exp, accum_out=l2[0:m, c, 1:2], **kw).then_inc(exp_done, 1)

        def copies(act, hd, par, qi):
            m = TILES[qi][1]
            for gq in range(GRP[qi]):
                act.wait_ge(tp_ready, 1 + hd * TPH + tp_at(qi) + gq + 1)
                tp = tps[(par * TPH + tp_at(qi) + gq) % 2]
                n = min(4, qi + 1 - 4 * gq)
                act.copy(wT[:, 4 * gq:4 * gq + n, 0:m], tp[:, 0:n, 0:m]).then_inc(tp_copied, 1)

        @block.scalar
        def _(act):
            act.sem_inc(tp_copied, 1)
            act.sem_inc(exp_done, 1)
            act.copy(vh[0][:], zT[:, 2 * HEADS, :]).then_inc(staged, 1)
            act.wait_ge(lam_ready, 2)
            act.activation(lexp[:], ldot[:], ACT.Exp).then_inc(lexp_done, 1)
            def head(hd, par):
                for gv in range(TP0):
                    act.wait_ge(tp_ready, 1 + hd * TPH + gv + 1)
                    n = min(4, NT - 4 * gv)
                    act.copy(v_rows[:, 4 * gv:4 * gv + n, :], tps[(par * TPH + gv) % 2][:, 0:n, :]).then_inc(tp_copied, 1)
                for qi in range(NT):
                    if qi == 0:
                        exps(act, hd, 0, 0)
                        exps(act, hd, 0, 1)
                    if qi + 1 < NT:
                        exps(act, hd, qi + 1, 0)
                    copies(act, hd, par, qi)
                    if qi + 1 < NT:
                        exps(act, hd, qi + 1, 1)

            with act.Fori(0, HEADS // 2) as i:
                for par in range(2):
                    head(2 * i + par, par)

        def maxima(dve, do, hd, qi):
            q0, m = TILES[qi]
            n = q0 + m
            for c in range(2):
                dve.wait_ge(s_ready, (hd * NT + qi) * 2 + c + 1)
                if n <= WIDE:
                    do(dve.tensor_reduce(mx[0:m, c:c + 1], S[c][0:m, 0:n], AX_X, ALU.max))
                else:
                    if c == 0:
                        do(dve.tensor_copy(tail_sb[0:m, :, :], tail[0:m, :, :]))
                    do(dve.tensor_reduce(mx2[0:m, 0:1], S[c][0:m, :], AX_X, ALU.max), wait=False)
                    do(dve.tensor_reduce(mx2[0:m, 1:2], tail_sb[0:m, c, :], AX_X, ALU.max))
                    do(dve.tensor_reduce(mx[0:m, c:c + 1], mx2[0:m, :], AX_X, ALU.max))
                dve.tensor_scalar(nb[0:m, c:c + 1], mx[0:m, c:c + 1], -scale, None, ALU.mult).then_inc(nb_ready, 1)

        def combine(dve, do, hd, qi):
            q0, m = TILES[qi]
            n = q0 + m
            dve.wait_ge(exp_done, 1 + (hd * NT + qi) * 2 + 2)
            prob, l = probs[qi % 2], sums[qi % 2]
            if n > WIDE:
                do(dve.tensor_reduce(l[0:m, :], l2[0:m, :, :], AX_X, ALU.add))
            do(dve.reciprocal(r[0:m, :], l[0:m, :]))
            do(dve.tensor_tensor(nl[0:m, :], r[0:m, 1:2], nlam[0:m, :], ALU.mult))
            do(dve.tensor_scalar(prob[1][0:m, 0:n], prob[1][0:m, 0:n], nl[0:m, 0:1], None, ALU.mult))
            dve.wait_ge(tp_ready, 1 + hd * TPH + tp_at(qi))
            dve.scalar_tensor_tensor(out=w[0:m, 0:n], in0=prob[0][0:m, 0:n], scalar=r[0:m, 0:1], in1=prob[1][0:m, 0:n],
                                     op0=ALU.mult, op1=ALU.add).then_inc(w_ready, 1)

        def out_copy(dve, hd, qi):
            m = TILES[qi][1]
            dve.wait_ge(o_ready, hd * NT + qi + 1)
            dve.tensor_copy(o_sb[0:m, qi, ds(hd * P, P)], po[0:m, 0:P]).then_inc(o_copied, 1)

        @block.vector
        def _(dve):
            do = Order(dve, dve_order)
            dve.sem_inc(w_ready, 1)
            dve.sem_inc(o_copied, 1)
            for kind, t in enumerate((qh, kh)):
                dve.tensor_copy(t[0][:], zT[:, HEADS * kind, :]).then_inc(staged, 1)
            for tp in tps:
                dve.memset(tp[:], 0.0).then_inc(tp_clear, 1)
            do(dve.memset(o_sb[:, 0, :], 0.0))
            dve.wait_ge(loaded, 80)
            dve.tensor_tensor_reduce(prod[:], lq[0][:], lq[1][:], 1.0, 0.0, ALU.mult, ALU.add, ldot[:, 0:1]).then_inc(lam_ready, 1)
            dve.wait_ge(lam_ready, 1)
            dve.tensor_tensor_reduce(prod[:], lq[2][:], lq[3][:], 1.0, 0.0, ALU.mult, ALU.add, ldot[:, 1:2]).then_inc(lam_ready, 1)
            dve.wait_ge(lexp_done, 1)
            do(dve.tensor_tensor(nlam[:], lexp[:, 1:2], lexp[:, 0:1], ALU.subtract))
            do(dve.tensor_scalar(nlam[:], nlam[:], -LAM_INIT, None, ALU.add))
            def head(hd):
                for qi in range(NT):
                    if qi == 0:
                        maxima(dve, do, hd, 0)
                    combine(dve, do, hd, qi)
                    if qi + 1 < NT:
                        maxima(dve, do, hd, qi + 1)
                    if qi:
                        out_copy(dve, hd, qi - 1)
                out_copy(dve, hd, NT - 1)

            with dve.Fori(0, HEADS // 2) as i:
                do.enter(i, 2 * (5 * NT + 6))
                for par in range(2):
                    head(2 * i + par)
                do.leave(HEADS // 2)
            dve.wait_ge(o_copied, 1 + HEADS * NT)

    with nc.psum_tensor("p_oT", [P, 2, 4, P], F32) as ps, nc.Block() as block:
        ms_ready, sd_ready, on_ready, oT_ready, oT_copied, g_ready = map(sem, ("ms_ready", "sd_ready", "on_ready", "oT_ready", "oT_copied", "g_ready"))
        order2, squared = sem("dve_order2"), sem("squared")
        sq_a = probs[0][0]
        BY_ACT = NT // 2

        @block.vector
        def _(dve):
            do = Order(dve, order2)
            do(dve.tensor_scalar(g[:], g[:], 1.0 - LAM_INIT, None, ALU.mult), wait=False)
            for i in range(BY_ACT, NT):
                for h in range(HEADS):
                    o = o_sb[:, i, P * h:P * h + P]
                    do(dve.tensor_tensor_reduce(sq[:, P * ((HEADS * i + h) % 2):P * ((HEADS * i + h) % 2) + P], o, o, 1.0, 0.0, ALU.mult, ALU.add, ss[:, HEADS * i + h:HEADS * i + h + 1]), wait=h == HEADS - 1 or h == 1)
            dve.wait_ge(squared, HEADS * BY_ACT)
            dve.tensor_scalar(ss[:], ss[:], 1.0 / P, LN_EPS, ALU.mult, ALU.add).then_inc(ms_ready, 1)
            dve.wait_ge(sd_ready, 1)
            do(dve.reciprocal(rs[:], rs[:]))
            ov = o_sb[:].rearrange("p i (h e) -> p (i h) e", h=HEADS)
            for i in range(NT):
                v = ov[:, HEADS * i:HEADS * i + HEADS, :]
                dve.tensor_tensor(v, v, bc(rs[:, HEADS * i:HEADS * i + HEADS], P), ALU.mult).then_inc(on_ready, 1)
            dve.wait_ge(on_ready, NT)

        @block.scalar
        def _(act):
            for n in range(HEADS * BY_ACT):
                i, h = n // HEADS, n % HEADS
                if n >= 2:
                    act.wait_ge(squared, n - 1)
                act.activation(sq_a[:, P * (n % 2):P * (n % 2) + P], o_sb[:, i, P * h:P * h + P], ACT.Square,
                               accum_out=ss[:, n:n + 1]).then_inc(squared, 1)
            act.wait_ge(ms_ready, 1)
            act.activation(rs[:], ss[:], ACT.Sqrt).then_inc(sd_ready, 1)
            act.wait_ge(order2, 1)
            for i in range(NT):
                q0, m = TILES[i]
                act.wait_ge(oT_ready, i + 1)
                act.mul(K.daT[:, :, q0:q0 + m], ps[:, i % 2, :, 0:m], g[:, 0:1]).then_inc(oT_copied, 1)

        @block.tensor
        def _(pe):
            for i in range(NT):
                q0, m = TILES[i]
                pe.wait_ge(on_ready, i + 1)
                if i >= 2:
                    pe.wait_ge(oT_copied, i - 1)
                for h in range(HEADS):
                    last = pe.transpose(ps[:, i % 2, h, 0:m], o_sb[0:m, i, P * h:P * h + P], K.ident[0:m, 0:m])
                last.then_inc(oT_ready, 1)


def load_rows(eng, buf, source, i, sem):
    m = TILES[i][1]
    eng.dma_start(buf[0:m, :], source(i)).then_inc(sem, 16)


class Norm:

    def __init__(self, nc, K, name, at):
        self.K, self.nc = K, nc
        self.st, self.mv, self.ve, self.sd = (at(f"{name}_{n}", [w]) for n, w in (
            ("stats", 12), ("mean_var", 2), ("var_eps", 1), ("dev", 1)))
        self.rs, self.nm = at(name + "_rec_dev", [2]), at(name + "_neg_mean", [2])
        self.gain, self.bias = at(name + "_gain", [D]), at(name + "_bias", [D])
        self.var_ready, self.dev_ready, self.scales_ready, self.xn_ready, self.gained, self.h_ready, self.params = (
            K.sem(f"{name}_{n}") for n in ("var_ready", "dev_ready", "scales_ready", "xn_ready", "gained", "h_ready", "params"))

    def load(self, sp, gain, bias):
        for t, src in ((self.gain, gain), (self.bias, bias)):
            sp.dma_start(t[:], src.rearrange("(a d) -> a d", a=1).to_broadcast([P, D])).then_inc(self.params, 16)

    def statistics(self, dve, do, i):
        m = TILES[i][1]
        z = self.K.H[0:m, i, :]
        for j in range(2):
            do(dve.bn_stats(self.st[0:m, 6 * j:6 * j + 6], z[:, 512 * j:512 * j + 512]), wait=j == 1)
        do(dve.bn_aggr(self.mv[0:m, :], self.st[0:m, :]))
        dve.tensor_scalar(self.ve[0:m, :], self.mv[0:m, 1:2], LN_EPS, None, ALU.add).then_inc(self.var_ready, 1)

    def scales(self, dve, do, i):
        m, b = TILES[i][1], i % 2
        if i >= 2:
            dve.wait_ge(self.xn_ready, i - 1)
        dve.wait_ge(self.dev_ready, i + 1)
        do(dve.reciprocal(self.rs[0:m, b:b + 1], self.sd[0:m, :]))
        dve.tensor_scalar(self.nm[0:m, b:b + 1], self.mv[0:m, 0:1], self.rs[0:m, b:b + 1], -1.0, ALU.mult, ALU.mult).then_inc(self.scales_ready, 1)
        dve.wait_ge(self.scales_ready, i + 1)

    def act(self, act, i):
        m, b = TILES[i][1], i % 2
        z = self.K.H[0:m, i, :]
        act.wait_ge(self.var_ready, i + 1)
        act.activation(self.sd[0:m, :], self.ve[0:m, :], ACT.Sqrt).then_inc(self.dev_ready, 1)
        act.wait_ge(self.scales_ready, i + 1)
        act.activation(z, z, ACT.Identity, scale=self.rs[0:m, b:b + 1], bias=self.nm[0:m, b:b + 1]).then_inc(self.xn_ready, 1)

    def apply_gain(self, dve, i):
        m = TILES[i][1]
        z = self.K.H[0:m, i, :]
        if i == 0:
            dve.wait_ge(self.params, 32)
        dve.wait_ge(self.xn_ready, i + 1)
        dve.tensor_tensor(z, z, self.gain[0:m, :], ALU.mult).then_inc(self.gained, 1)
        if i == NT - 1:
            dve.wait_ge(self.gained, NT)
            dve.wait_ge(self.h_ready, NT - 1)
            dve.tensor_tensor(z, z, self.bias[0:m, :], ALU.add).then_inc(self.h_ready, 1)

    def add_bias(self, pool, i):
        m = TILES[i][1]
        z = self.K.H[0:m, i, :]
        if i == 0:
            pool.wait_ge(self.params, 32)
        pool.wait_ge(self.gained, i + 1)
        pool.tensor_tensor(z, z, self.bias[0:m, :], ALU.add).then_inc(self.h_ready, 1)


def load_w_out(sp, K, layer):
    w, loaded = K.w_out[layer], K.w_out_loaded[layer]
    src = K.A[f"l{layer}_w_out"].rearrange("(k p) c -> p k c", p=P)
    for c in range(2):
        sp.dma_start(w[:, :, 512 * c:512 * c + 512], src[:, :, 512 * c:512 * c + 512]).then_inc(loaded, 16)


def project_and_norm(nc, K, A, layer, slices, at, residual):
    L = f"l{layer}"
    ns = len(slices)
    res = [at(f"{L}_res{i}", [D]) for i in range(2)]
    hT, wr, rb = at(L + "_h1T", [KD, P]), at(L + "_w_router", [KD, 36]), at(L + "_b_router", [36])
    norm = Norm(nc, K, L + "_ln1", at)
    sem = lambda n: K.sem(f"{L}_out_{n}")
    w_out, w_loaded = K.w_out[layer], K.w_out_loaded[layer]
    r_loaded, res_loaded = sem("r_loaded"), [sem("res_loaded0"), sem("res_loaded1")]
    o_ready, z_done, order, turned, hT_ready, lg_ready, lg_done, stored = map(sem, (
        "o_ready", "z_done", "order", "turned", "hT_ready", "lg_ready", "lg_done", "stored"))
    with ExitStack() as ctx:
        po = [[ctx.enter_context(nc.psum_tensor(f"{L}_po{b}{h}", [P, 512], F32)) for h in range(2)] for b in range(2)]
        pt = [ctx.enter_context(nc.psum_tensor(f"{L}_pt{h}", [P, 4, P], F32)) for h in range(2)]
        pl = ctx.enter_context(nc.psum_tensor(f"{L}_pl", [P, 36], F32))
        block = ctx.enter_context(nc.Block())

        @block.sync
        def _(sp):
            norm.load(sp, A[L + "_ln1_g"], A[L + "_ln1_b"])
            with nc.allow_non_contiguous_dma(reason="router weights"):
                sp.dma_start(wr[:, :, 0:GROUPS], A[L + "_moe_w_coarse"].rearrange("(k p) g -> p k g", p=P)).then_inc(r_loaded, 16)
                for g in range(GROUPS):
                    c = GROUPS + PER_GROUP * g
                    sp.dma_start(wr[:, :, c:c + PER_GROUP], A[L + "_moe_w_fine"][g].rearrange("(k p) e -> p k e", p=P)).then_inc(r_loaded, 16)
                sp.dma_start(rb[:, 0:GROUPS], A[L + "_moe_b_coarse"].rearrange("(a g) -> a g", a=1).to_broadcast([P, GROUPS])).then_inc(r_loaded, 16)
                sp.dma_start(rb[:, GROUPS:36], A[L + "_moe_b_fine"].rearrange("(a g) e -> a (g e)", a=1).to_broadcast([P, NE])).then_inc(r_loaded, 16)
            for i in range(NT):
                if i >= 2:
                    sp.wait_ge(z_done, 2 * (i - 1))
                load_rows(sp, res[i % 2], residual, i, res_loaded[i % 2])
            for i in range(NT):
                t0, m = TILES[i]
                sp.wait_ge(norm.h_ready, i + 1)
                sp.dma_start(K.h1_dram[t0:t0 + m, :], K.H[0:m, i, :]).then_inc(stored, 16)
            sp.wait_ge(stored, 16 * NT)

        @block.tensor
        def _(pe):
            pe.wait_ge(w_loaded, 32)
            def output(i, h):
                t0, m = TILES[i]
                for k, y in enumerate(slices):
                    last = pe.matmul(po[i % 2][h][0:m, :], y[:, t0:t0 + m], w_out[:, k, 512 * h:512 * h + 512], start=k == 0, stop=k == ns - 1)
                last.then_inc(o_ready, 1)

            def turn(i):
                m = TILES[i][1]
                pe.wait_ge(norm.h_ready, i + 1)
                for k in range(KD):
                    last = pe.transpose(pt[k // 4][:, k % 4, 0:m], K.H[0:m, i, P * k:P * k + P], K.ident[0:m, 0:m])
                last.then_inc(turned, 1)

            def router(i):
                m = TILES[i][1]
                if i == 0:
                    pe.wait_ge(r_loaded, 7 * 16)
                pe.wait_ge(hT_ready, 2 * (i + 1))
                if i >= 1:
                    pe.wait_ge(lg_done, i)
                for k in range(KD):
                    last = pe.matmul(pl[0:m, :], hT[:, k, 0:m], wr[:, k, :], start=k == 0, stop=k == KD - 1)
                last.then_inc(lg_ready, 1)

            for i in range(NT + 2):
                if i < NT:
                    if i >= 2:
                        pe.wait_ge(z_done, 2 * (i - 1))
                    output(i, 0)
                if i >= 2:
                    router(i - 2)
                if i < NT:
                    output(i, 1)
                if 1 <= i <= NT:
                    turn(i - 1)

        @block.scalar
        def _(act):
            for i in range(NT + 1):
                if i >= 1:
                    m = TILES[i - 1][1]
                    act.wait_ge(turned, i)
                    for h in range(2):
                        act.copy(hT[:, 4 * h:4 * h + 4, 0:m], pt[h][:, :, 0:m]).then_inc(hT_ready, 1)
                if i < NT:
                    norm.act(act, i)

        @block.vector
        def _(dve):
            do = Order(dve, order)
            do(dve.memset(K.logits[:, 0, :], 0.0))
            for i in range(NT + 2):
                if i < NT:
                    m = TILES[i][1]
                    dve.wait_ge(res_loaded[i % 2], 16 * (i // 2 + 1))
                    for h in range(2):
                        c = slice(512 * h, 512 * h + 512)
                        dve.wait_ge(o_ready, 2 * i + h + 1)
                        dve.scalar_tensor_tensor(out=K.H[0:m, i, c], in0=res[i % 2][0:m, c], scalar=ALPHA, in1=po[i % 2][h][0:m, :],
                                                 op0=ALU.mult, op1=ALU.add).then_inc(z_done, 1)
                    dve.wait_ge(z_done, 2 * i + 2)
                    norm.statistics(dve, do, i)
                    norm.scales(dve, do, i)
                    norm.apply_gain(dve, i)
                if i >= 2:
                    m = TILES[i - 2][1]
                    if i == 2:
                        dve.wait_ge(r_loaded, 7 * 16)
                    dve.wait_ge(lg_ready, i - 1)
                    dve.tensor_tensor(K.logits[0:m, i - 2, :], pl[0:m, :], rb[0:m, :], ALU.add).then_inc(lg_done, 1)
            dve.wait_ge(lg_done, NT)

        @block.gpsimd
        def _(pool):
            for i in range(NT - 1):
                norm.add_bias(pool, i)


NBLK = NE + (2 * T) // P
NOVER = NBLK - NE
EARLY = 2
MAIN = NE + EARLY
MAX_OVER = T // P
NO_ROW = 1.0e6


def expert_buffers(nc, K, layer):
    L = f"l{layer}"
    at = Place(nc, K.base)
    E = K.E = Kept(nc)
    E.wg, E.wu, E.wd = ([at(f"{L}_{x}{i}", [w]) for i in range(2)] for x, w in (("wg", KD * F), ("wu", KD * F), ("wd", 4 * D)))
    E.free = at.at
    E.src = {x: K.A[f"{L}_moe_w_{x}"].rearrange("e (p c) f -> e p (c f)", p=P) for x in ("gate", "up", "down")}
    E.g_loaded, E.u_loaded, E.d_loaded = ([nc.alloc_semaphore(f"{L}_{x}_loaded{i}") for i in range(2)] for x in "gud")


def load_expert(sp, E, e, par, wait_gate=None, wait_down=None):
    if wait_gate is not None:
        sp.wait_ge(*wait_gate)
    sp.dma_start(E.wg[par][:], E.src["gate"][ds(e, 1)].rearrange("a p x -> (a p) x")).then_inc(E.g_loaded[par], 16)
    sp.dma_start(E.wu[par][:], E.src["up"][ds(e, 1)].rearrange("a p x -> (a p) x")).then_inc(E.u_loaded[par], 16)
    if wait_down is not None:
        sp.wait_ge(*wait_down)
    sp.dma_start(E.wd[par][:], E.src["down"][ds(e, 1)].rearrange("a p x -> (a p) x")).then_inc(E.d_loaded[par], 16)


def route(nc, K, layer):
    L = f"l{layer}"
    expert_buffers(nc, K, layer)
    at = Place(nc, K.E.free)
    n = lambda name, shape, dt=F32: at(f"{L}_rt_{name}", shape, dt)
    iota, rev, thr, tok = n("iota", [P]), n("rev", [8]), n("thr", [MAX_OVER]), n("tok", [NT])
    tri, ones, valid = n("tri", [P]), n("ones", [P]), n("valid", [NT])
    cm, vm, dif, G, v4 = n("cm", [NT]), n("vm", [NT]), n("dif", [NT, 4]), n("G", [NT, 4]), n("v4", [NT, 4])
    pg, f48, sel, v8 = n("pg", [NT]), n("f48", [NT, 4, 8]), n("sel", [NT, 8]), n("v8", [NT, 8])
    top = [n("top1", [NT]), n("top2", [NT])]
    O = [n("O1", [NT, 8]), n("O2", [NT, 8])]
    M = [n("M1", [NT, NE]), n("M2", [NT, NE])]
    Ms, pos, tot, run = n("Ms", [NT, NE]), n("pos", [NT, NE]), n("tot", [NT, NE]), n("run", [NT + 1, NE])
    e2, den = n("e2", [NT]), n("den", [NT])
    gt, nover, inc, ob, one32 = n("gt", [NE, MAX_OVER]), n("nover", [NE]), n("inc", [NE]), n("ob", [NE]), n("one32", [NE])
    tmp, q8 = n("tmp", [NT, NE]), n("q8", [NT, MAX_OVER])
    pk, ok, qk, geo, blk = (n(x, [NT]) for x in ("pk", "ok", "qk", "geo", "blk"))
    ek, slot = [n("ek1", [NT]), n("ek2", [NT])], [n("slot1", [NT]), n("slot2", [NT])]
    vals = n("vals", [NT, 2, 3])
    Pm, B, R = [n(f"Pm{k}", [NT, P]) for k in range(2)], n("B", [NT, NBLK]), [n(f"R{k}", [NT, 3, NBLK]) for k in range(2)]
    rowf, isz = n("rowf", [NBLK]), n("isz", [NBLK])
    ind, ind2, ov = n("ind", [NOVER, NE]), n("ind2", [NOVER, NE]), n("ov", [1, NOVER])
    sem = lambda x: K.sem(f"{L}_rt_{x}")
    made, order, exp_in, exp_done, m_ready, cum_ready, slot_ready, places_ready, r_ready, tab_ready = map(sem, (
        "made", "order", "exp_in", "exp_done", "m_ready", "cum_ready", "slot_ready", "places_ready", "r_ready", "tab_ready"))
    lg = K.logits
    with nc.psum_tensor(L + "_p_cum", [P, 2, 512], F32) as pc, nc.psum_tensor(L + "_p_tab", [P, 3, NBLK], F32) as ptab, nc.Block() as block:
        @block.sync
        def _(sp):
            for par in range(2):
                load_expert(sp, K.E, par, par)

        @block.gpsimd
        def _(pool):
            kw = dict(allow_small_or_imprecise_dtypes=True)
            pool.iota(iota[:], pattern=[[1, P]], base=0, channel_multiplier=0, **kw).then_inc(made, 1)
            pool.iota(rev[:], pattern=[[-1, 8]], base=8, channel_multiplier=0, **kw).then_inc(made, 1)
            pool.iota(thr[:], pattern=[[P, MAX_OVER]], base=P, channel_multiplier=0, **kw).then_inc(made, 1)
            pool.iota(tok[:, 0:1], pattern=[[1, 1]], base=0, channel_multiplier=1, **kw).then_inc(made, 1)
            pool.iota(tok[:, 1:NT], pattern=[[P, NT - 1]], base=N_META, channel_multiplier=1, **kw).then_inc(made, 1)
            pool.memset(ones[:], 1.0).then_inc(made, 1)
            pool.memset(tri[:], 1.0).then_inc(made, 1)
            pool.memset(valid[:], 1.0).then_inc(made, 1)
            pool.wait_ge(made, 8)
            pool.affine_select(out=tri[:], in_=tri[:], compare_op=ALU.is_gt, fill=0.0, base=0, pattern=[[1, P]], channel_multiplier=-1).then_inc(made, 1)
            pool.affine_select(out=valid[:, 0:1], in_=valid[:, 0:1], compare_op=ALU.is_gt, fill=0.0, base=N_META, pattern=[[0, 1]], channel_multiplier=-1).then_inc(made, 1)
            for k in range(2):
                pool.wait_ge(slot_ready, k + 1)
                for i in range(NT):
                    pool.tensor_scalar(Pm[k][:, i, :], iota[:], slot[k][:, i:i + 1], None, ALU.is_equal).then_inc(places_ready, 1)

        @block.scalar
        def _(act):
            act.wait_ge(exp_in, 1)
            act.activation(dif[:], dif[:], ACT.Exp).then_inc(exp_done, 1)
            act.wait_ge(exp_in, 2)
            act.activation(e2[:], e2[:], ACT.Exp).then_inc(exp_done, 1)

        @block.tensor
        def _(pe):
            pe.wait_ge(made, 10)
            pe.wait_ge(m_ready, 1)
            pe.matmul(pc[:, 0, 0:NT * NE], tri[:], Ms[:].rearrange("p i e -> p (i e)"), start=True, stop=True).then_inc(cum_ready, 1)
            pe.matmul(pc[:, 1, 0:NT * NE], ones[:], Ms[:].rearrange("p i e -> p (i e)"), start=True, stop=True).then_inc(cum_ready, 1)
            for k in range(2):
                pe.wait_ge(r_ready, k + 1)
                for i in range(NT):
                    pe.wait_ge(places_ready, k * NT + i + 1)
                    last = pe.matmul(ptab[:].rearrange("p a b -> p (a b)"), Pm[k][:, i, :], R[k][:, i, :, :].rearrange("p a b -> p (a b)"),
                                     start=k == 0 and i == 0, stop=k == 1 and i == NT - 1)
            last.then_inc(tab_ready, 1)

        @block.vector
        def _(dve):
            do = Order(dve, order)
            tt, ts, red = dve.tensor_tensor, dve.tensor_scalar, dve.tensor_reduce
            dve.wait_ge(made, 10)
            coarse, fine = lg[:, :, 0:GROUPS], lg[:, :, GROUPS:36].rearrange("p i (g e) -> p i g e", g=GROUPS)

            def first_of_max(values, maxi, v, hot, width):
                do(red(maxi[:], values, AX_X, ALU.max))
                do(tt(v[:], values, bc(maxi[:], width), ALU.is_equal))
                do(tt(v[:], v[:], rev[:, 0:width].unsqueeze(1).to_broadcast([P, NT, width]), ALU.mult))
                do(red(vm[:], v[:], AX_X, ALU.max))
                do(tt(hot[:], v[:], bc(vm[:], width), ALU.is_equal))

            first_of_max(coarse, cm, v4, G, GROUPS)
            tt(dif[:], coarse, bc(cm[:], GROUPS), ALU.subtract).then_inc(exp_in, 1)
            do(tt(f48[:], fine, G[:].unsqueeze(3).to_broadcast([P, NT, GROUPS, PER_GROUP]), ALU.mult))
            do(red(sel[:], f48[:].rearrange("p i g e -> p i e g"), AX_X, ALU.add))
            first_of_max(sel[:], top[0], v8, O[0], PER_GROUP)
            do(ts(v8[:], O[0][:], -3.0e38, None, ALU.mult))
            do(tt(sel[:], sel[:], v8[:], ALU.add))
            first_of_max(sel[:], top[1], v8, O[1], PER_GROUP)
            tt(e2[:], top[1][:], top[0][:], ALU.subtract).then_inc(exp_in, 1)
            for k in range(2):
                do(tt(M[k][:].rearrange("p i (g e) -> p i g e", g=GROUPS), G[:].unsqueeze(3).to_broadcast([P, NT, GROUPS, PER_GROUP]),
                      O[k][:].unsqueeze(2).to_broadcast([P, NT, GROUPS, PER_GROUP]), ALU.mult))
                do(tt(M[k][:], M[k][:], bc(valid[:], NE), ALU.mult))
            tt(Ms[:], M[0][:], M[1][:], ALU.add).then_inc(m_ready, 1)
            dve.wait_ge(exp_done, 2)
            do(red(pg[:], dif[:], AX_X, ALU.add), wait=False)
            do(ts(den[:], e2[:], 1.0, None, ALU.add))
            do(dve.reciprocal(pg[:], pg[:]), wait=False)
            do(dve.reciprocal(den[:], den[:]))
            do(tt(vals[:, :, 0, 2], pg[:], den[:], ALU.mult))
            do(tt(vals[:, :, 1, 2], vals[:, :, 0, 2], e2[:], ALU.mult), wait=False)
            for k in range(2):
                do(dve.tensor_copy(vals[:, :, k, 0], tok[:]), wait=False)
                do(ts(vals[:, :, k, 1], tok[:], float(1 + k * T), None, ALU.add))
            do(tt(vals[:].rearrange("p i k c -> p i (k c)"), vals[:].rearrange("p i k c -> p i (k c)"), bc(valid[:], 6), ALU.mult), wait=False)
            experts_iota = iota[:, 0:NE].unsqueeze(1).to_broadcast([P, NT, NE])
            for k in range(2):
                do(tt(tmp[:], M[k][:], experts_iota, ALU.mult))
                do(red(ek[k][:], tmp[:], AX_X, ALU.add))
            dve.wait_ge(cum_ready, 2)
            do(dve.memset(run[:, 0, :], 0.0), wait=False)
            do(dve.tensor_copy(tot[:], pc[:, 1, 0:NT * NE].rearrange("p (i e) -> p i e", i=NT)))
            for i in range(NT):
                do(tt(run[:, i + 1, :], run[:, i, :], tot[:, i, :], ALU.add))
            do(tt(pos[:], pc[:, 0, 0:NT * NE].rearrange("p (i e) -> p i e", i=NT), run[:, 0:NT, :], ALU.add), wait=False)
            do(tt(gt[:], bc(run[:, NT, :], MAX_OVER), thr[:].unsqueeze(1).to_broadcast([P, NE, MAX_OVER]), ALU.is_gt))
            do(red(nover[:], gt[:], AX_X, ALU.add), wait=False)
            do(dve.memset(one32[:], 1.0))
            do(dve.tensor_tensor_scan(inc[:], one32[:], nover[:], 0.0, ALU.mult, ALU.add))
            do(tt(ob[:], inc[:], nover[:], ALU.subtract))
            for k in range(2):
                for out, per_expert in ((pk, pos[:]), (ok, ob[:].unsqueeze(1).to_broadcast([P, NT, NE]))):
                    do(tt(tmp[:], M[k][:], per_expert, ALU.mult))
                    do(red(out[:], tmp[:], AX_X, ALU.add))
                do(tt(q8[:], bc(pk[:], MAX_OVER), thr[:].unsqueeze(1).to_broadcast([P, NT, MAX_OVER]), ALU.is_ge))
                do(red(qk[:], q8[:], AX_X, ALU.add))
                dve.scalar_tensor_tensor(out=slot[k][:], in0=qk[:], scalar=-float(P), in1=pk[:], op0=ALU.mult, op1=ALU.add).then_inc(slot_ready, 1)
                do(ts(geo[:], qk[:], 1.0, None, ALU.min), wait=False)
                do(dve.scalar_tensor_tensor(out=blk[:], in0=qk[:], scalar=float(NE - 1), in1=ok[:], op0=ALU.add, op1=ALU.add))
                do(tt(blk[:], blk[:], ek[k][:], ALU.subtract))
                do(tt(blk[:], blk[:], geo[:], ALU.mult))
                do(tt(blk[:], blk[:], ek[k][:], ALU.add))
                do(tt(B[:], iota[:, 0:NBLK].unsqueeze(1).to_broadcast([P, NT, NBLK]), bc(blk[:], NBLK), ALU.is_equal))
                tt(R[k][:], B[:].unsqueeze(2).to_broadcast([P, NT, 3, NBLK]),
                   vals[:, :, k, :].unsqueeze(3).to_broadcast([P, NT, 3, NBLK]), ALU.mult).then_inc(r_ready, 1)
                dve.wait_ge(r_ready, k + 1)
            j = iota[:, 0:NOVER].unsqueeze(2).to_broadcast([P, NOVER, NE])
            do(tt(ind[:], j, ob[:].unsqueeze(1).to_broadcast([P, NOVER, NE]), ALU.is_ge), wait=False)
            do(tt(ind2[:], j, inc[:].unsqueeze(1).to_broadcast([P, NOVER, NE]), ALU.is_lt))
            do(tt(ind[:], ind[:], ind2[:], ALU.mult))
            do(tt(ind2[:], ind[:], iota[:, 0:NE].unsqueeze(1).to_broadcast([P, NOVER, NE]), ALU.mult))
            do(red(ov[:, 0, :], ind2[:], AX_X, ALU.add))
            do(dve.tensor_copy(K.over[:, 0:NOVER], ov[:, 0, :]), wait=False)
            do(dve.tensor_copy(K.over[:, NOVER:NOVER + 1], inc[:, NE - 1:NE]), wait=False)
            dve.wait_ge(tab_ready, 1)
            do(dve.tensor_copy(K.tok_idx[:], ptab[:, 0, :]), wait=False)
            do(dve.tensor_copy(K.gates[:], ptab[:, 2, :]), wait=False)
            do(ts(isz[:], ptab[:, 1, :], 0.0, NO_ROW, ALU.is_equal, ALU.mult), wait=False)
            do(ts(rowf[:], ptab[:, 1, :], -1.0, None, ALU.add))
            do(tt(rowf[:], rowf[:], isz[:], ALU.add))
            do(dve.tensor_copy(K.row_idx[:], rowf[:]))


def is_at(b, n):
    return isinstance(b, int) and b == n


def experts(nc, K, A, layer):
    L = f"l{layer}"
    E = K.E
    wg, wu, wd = E.wg, E.wu, E.wd
    at = Place(nc, E.free)
    n = lambda name, shape, dt=F32: at(f"{L}_ex_{name}", shape, dt)
    xb = [n(f"xb{i}", [D]) for i in range(2)]
    xT = [n(f"xT{i}", [KD, P]) for i in range(2)]
    yb = [n(f"yb{i}", [D]) for i in range(2)]
    sil, hid, hT = n("sil", [F]), [n(f"hid{i}", [F]) for i in range(2)], n("hT", [4, P])
    gi, ri, gc = ([n(f"{x}{i}", [1], d) for i in range(2)] for x, d in (("gi", U32), ("ri", U32), ("gc", F32)))
    wv = lambda w: w[:].rearrange("p (c f) -> p c f", f=F)
    dv = lambda w: w[:].rearrange("p (c d) -> p c d", d=D)

    for phase in ("main", "over"):
        main = phase == "main"
        sem = lambda x: K.sem(f"{L}_{phase}_{x}")
        pair = lambda x: [sem(x + "0"), sem(x + "1")]
        g_loaded, u_loaded, d_loaded = E.g_loaded, E.u_loaded, E.d_loaded
        if not main:
            early_loads = [g_loaded[0], u_loaded[0], d_loaded[0]]
            E.g_loaded, E.u_loaded, E.d_loaded = g_loaded, u_loaded, d_loaded = [pair(x) for x in ("g_loaded", "u_loaded", "d_loaded")]
        gathered, scattered = map(pair, ("gathered", "scattered"))
        x_turned, xT_a, xT_v, g_ready, u_ready, silu_done, hid_done, h_turned, hT_ready, y_ready, y_a, y_v, idx_done, row_done, paced = map(sem, (
            "x_turned", "xT_a", "xT_v", "g_ready", "u_ready", "silu_done", "hid_done", "h_turned", "hT_ready", "y_ready",
            "y_a", "y_v", "idx_done", "row_done", "paced"))
        with ExitStack() as ctx:
            psum = lambda x, s: ctx.enter_context(nc.psum_tensor(f"{L}_{phase}_{x}", s, F32))
            pg, pu, ph = psum("pg", [P, 512]), psum("pu", [P, 512]), psum("ph", [P, 4, P])
            px, py = [psum(f"px{i}", [P, 4, P]) for i in range(2)], [psum(f"py{i}", [P, 512]) for i in range(2)]
            block = ctx.enter_context(nc.Block())

            def load(sp, e, i, b, par):
                if is_at(b, 0):
                    load_expert(sp, E, e, par)
                else:
                    load_expert(sp, E, e, par, (u_ready, b - 1), (y_ready, 2 * (b - 1)))

            def gather(pool, col, i, b, par):
                if not (isinstance(b, int) and b < 2):
                    pool.wait_ge(gathered[par], 16 * i)
                    pool.wait_ge(x_turned, b - 1)
                pool.tensor_copy(gi[par][:], K.tok_idx[:, ds(col, 1)]).then_inc(idx_done, 1)
                pool.wait_ge(idx_done, b + 1)
                pool.sem_inc(paced, 1)
                pool.indirect_dma_start(xb[par][:], None, K.h1_dram, bass.IndirectOffsetOnAxis(ap=gi[par][:], axis=0)).then_inc(gathered[par], 16)

            def gate_column(pool, col, b, par):
                if not is_at(b, 0):
                    pool.wait_ge(y_a, b - 1)
                    pool.wait_ge(y_v, b - 1)
                pool.tensor_copy(gc[par][:], K.gates[:, ds(col, 1)]).then_inc(row_done, 1)

            def scatter(pool, col, i, b, par):
                if not is_at(b, 0):
                    pool.wait_ge(scattered[par], 16 * i)
                pool.tensor_copy(ri[par][:], K.row_idx[:, ds(col, 1)]).then_inc(row_done, 1)
                pool.wait_ge(row_done, 2 * b + 2)
                pool.wait_ge(y_a, b + 1)
                pool.wait_ge(y_v, b + 1)
                pool.sem_inc(paced, 1)
                pool.indirect_dma_start(K.y_dram, bass.IndirectOffsetOnAxis(ap=ri[par][:], axis=0), yb[par][:], None,
                                        bounds_check=2 * T - 1, oob_is_err=False).then_inc(scattered[par], 16)

            def turn_x(pe, i, b, par):
                pe.wait_ge(gathered[par], 16 * (i + 1))
                for k in range(KD):
                    last = pe.transpose(px[k // 4][:, k % 4, :], xb[par][:].rearrange("s (p c) -> s c p", c=KD)[:, k, :], K.ident[:])
                last.then_inc(x_turned, 1)

            def gate(pe, i, b, par):
                pe.wait_ge(g_loaded[par], 16 * (i + 1))
                pe.wait_ge(xT_a, b + 1)
                pe.wait_ge(xT_v, b + 1)
                pe.wait_ge(silu_done, b)
                for k in range(KD):
                    last = pe.matmul(pg[:], xT[par][:, k, :], wv(wg[par])[:, k, :], start=k == 0, stop=k == KD - 1)
                last.then_inc(g_ready, 1)

            def up(pe, i, b, par):
                pe.wait_ge(u_loaded[par], 16 * (i + 1))
                pe.wait_ge(hid_done, b)
                for k in range(KD):
                    last = pe.matmul(pu[:], xT[par][:, k, :], wv(wu[par])[:, k, :], start=k == 0, stop=k == KD - 1)
                last.then_inc(u_ready, 1)

            def turn_h(pe, b, par):
                pe.wait_ge(hid_done, b + 1)
                for k in range(4):
                    last = pe.transpose(ph[:, k, :], hid[par][:].rearrange("s (p c) -> s c p", c=4)[:, k, :], K.ident[:])
                last.then_inc(h_turned, 1)

            def down(pe, i, b, par):
                pe.wait_ge(hT_ready, b + 1)
                pe.wait_ge(d_loaded[par], 16 * (i + 1))
                for h, used in enumerate((y_a, y_v)):
                    pe.wait_ge(used, b)
                    for k in range(4):
                        last = pe.matmul(py[h][:], hT[:, k, :], dv(wd[par])[:, k, 512 * h:512 * h + 512], start=k == 0, stop=k == 3)
                    last.then_inc(y_ready, 1)

            def silu(act, b):
                act.wait_ge(g_ready, b + 1)
                act.wait_ge(hid_done, b)
                act.activation(sil[:], pg[:], ACT.Silu).then_inc(silu_done, 1)

            def copy_x(eng, op, half, b, par, done):
                eng.wait_ge(x_turned, b + 1)
                if not is_at(b, 0):
                    eng.wait_ge(u_ready, b - 1)
                op(xT[par][:, 4 * half:4 * half + 4, :], px[half][:]).then_inc(done, 1)

            def hidden(dve, b, par):
                dve.wait_ge(u_ready, b + 1)
                dve.wait_ge(silu_done, b + 1)
                if not is_at(b, 0):
                    dve.wait_ge(h_turned, b - 1)
                dve.tensor_tensor(hid[par][:], sil[:], pu[:], ALU.mult).then_inc(hid_done, 1)

            def copy_h(dve, b):
                dve.wait_ge(h_turned, b + 1)
                dve.tensor_copy(hT[:], ph[:]).then_inc(hT_ready, 1)

            def store_y(eng, half, i, b, par):
                eng.wait_ge(y_ready, 2 * b + half + 1)
                eng.wait_ge(row_done, 2 * b + 1)
                if not is_at(b, 0):
                    eng.wait_ge(scattered[par], 16 * i)
                out = yb[par][:, 512 * half:512 * half + 512]
                if half == 0:
                    eng.mul(out, py[0][:], gc[par][:, 0:1]).then_inc(y_a, 1)
                else:
                    eng.tensor_scalar(out, py[1][:], gc[par][:, 0:1], None, ALU.mult).then_inc(y_v, 1)

            if main:
                def walk(eng, step):
                    for b in range(4):
                        step(b // 2, b, b % 2)
                    with eng.Fori(2, MAIN // 2 - 2) as i:
                        for par in range(2):
                            step(i, 2 * i + par, par)
                    for b in range(MAIN - 4, MAIN):
                        step(b // 2, b, b % 2)
                    step(MAIN // 2, MAIN, 0)

                @block.sync
                def _(sp):
                    with sp.Fori(1, NE // 2) as i:
                        for par in range(2):
                            load(sp, 2 * i + par, i, 2 * i + par, par)
                    for b in range(NE, MAIN + 1):
                        e = sp.value_load(K.over[0:1, b - NE:b - NE + 1], min_val=0, max_val=NE - 1)
                        load(sp, e, b // 2, b, b % 2)

                @block.gpsimd
                def _(pool):
                    def step(i, b, par):
                        if is_at(b, 0):
                            for early in range(3):
                                gather(pool, early, early // 2, early, early % 2)
                        if not (isinstance(b, int) and b > MAIN - 4):
                            gather(pool, b + 3, i + 1 + par, b + 3, 1 - par)
                        if not is_at(b, 0):
                            gate_column(pool, b - 1, b - 1, 1 - par)
                            scatter(pool, b - 1, i - 1 + par, b - 1, 1 - par)
                    walk(pool, step)
                    for par in range(2):
                        pool.wait_ge(scattered[par], 16 * (MAIN // 2))

                @block.tensor
                def _(pe):
                    def step(i, b, par):
                        if is_at(b, 0):
                            turn_x(pe, 0, 0, 0)
                        if not is_at(b, MAIN):
                            gate(pe, i, b, par)
                        if not is_at(b, 0):
                            turn_h(pe, b - 1, 1 - par)
                        if not is_at(b, MAIN):
                            up(pe, i, b, par)
                        if not (is_at(b, MAIN - 1) or is_at(b, MAIN)):
                            turn_x(pe, i + par, b + 1, 1 - par)
                        if not is_at(b, 0):
                            down(pe, i - 1 + par, b - 1, 1 - par)
                    walk(pe, step)

                @block.scalar
                def _(act):
                    def step(i, b, par):
                        if is_at(b, 0):
                            copy_x(act, act.copy, 0, 0, 0, xT_a)
                        if not is_at(b, MAIN):
                            silu(act, b)
                        if not (is_at(b, MAIN - 1) or is_at(b, MAIN)):
                            copy_x(act, act.copy, 0, b + 1, 1 - par, xT_a)
                        if not is_at(b, 0):
                            store_y(act, 0, i - 1 + par, b - 1, 1 - par)
                    walk(act, step)

                @block.vector
                def _(dve):
                    def step(i, b, par):
                        if is_at(b, 0):
                            copy_x(dve, dve.tensor_copy, 1, 0, 0, xT_v)
                        if not is_at(b, 0):
                            copy_h(dve, b - 1)
                        if not is_at(b, MAIN):
                            hidden(dve, b, par)
                        if not (is_at(b, MAIN - 1) or is_at(b, MAIN)):
                            copy_x(dve, dve.tensor_copy, 1, b + 1, 1 - par, xT_v)
                        if not is_at(b, 0):
                            store_y(dve, 1, i - 1 + par, b - 1, 1 - par)
                    walk(dve, step)
            else:
                def each(eng, step):
                    blocks = eng.value_load(K.over[0:1, NOVER:NOVER + 1], min_val=0, max_val=NOVER)

                    def one(i, par):
                        j = 2 * i + par
                        with eng.If(blocks > j + EARLY):
                            step(i, j, par)
                        with eng.Else():
                            eng.nop()
                    for par in range(2):
                        one(0, par)
                    with eng.If(blocks > 2 + EARLY):
                        with eng.Fori(1, (NOVER - EARLY) // 2) as i:
                            for par in range(2):
                                one(i, par)
                    with eng.Else():
                        eng.nop()

                @block.sync
                def _(sp):
                    def step(i, j, par):
                        if is_at(j, 0):
                            sp.nop()
                            return
                        e = sp.value_load(K.over[0:1, ds(j + EARLY, 1)], min_val=0, max_val=NE - 1)
                        load(sp, e, i, j, par)
                    for early, here in zip(early_loads, (g_loaded[0], u_loaded[0], d_loaded[0])):
                        sp.wait_ge(early, 16 * (MAIN // 2 + 1))
                        sp.sem_inc(here, 16)
                    each(sp, step)

                @block.gpsimd
                def _(pool):
                    def step(i, j, par):
                        gather(pool, MAIN + j, i, j, par)
                        gate_column(pool, MAIN + j, j, par)
                        scatter(pool, MAIN + j, i, j, par)
                        pool.wait_ge(scattered[par], 16 * (i + 1))
                        pool.sem_inc(over_done, 1)
                    over_done = sem("over_done")
                    each(pool, step)

                @block.tensor
                def _(pe):
                    def step(i, j, par):
                        turn_x(pe, i, j, par)
                        gate(pe, i, j, par)
                        up(pe, i, j, par)
                        turn_h(pe, j, par)
                        down(pe, i, j, par)
                    each(pe, step)

                @block.scalar
                def _(act):
                    def step(i, j, par):
                        copy_x(act, act.copy, 0, j, par, xT_a)
                        silu(act, j)
                        store_y(act, 0, i, j, par)
                    each(act, step)

                @block.vector
                def _(dve):
                    def step(i, j, par):
                        copy_x(dve, dve.tensor_copy, 1, j, par, xT_v)
                        hidden(dve, j, par)
                        copy_h(dve, j)
                        store_y(dve, 1, i, j, par)
                    each(dve, step)


def combine_and_norm(nc, K, A, layer):
    L, lastl = f"l{layer}", layer == DEPTH - 1
    at = Place(nc, K.base)
    K.hT = None if lastl else at("h2T", [KD, T])
    YB = 4
    y0, y1 = [at(f"{L}_y0{i}", [D]) for i in range(YB)], [at(f"{L}_y1{i}", [D]) for i in range(YB)]
    norm = Norm(nc, K, L + "_ln2", at)
    sem = lambda n: K.sem(f"{L}_cb_{n}")
    y_loaded = [sem(f"y_loaded{i}") for i in range(YB)]
    y_summed, z_done, order, turned, hT_ready, stored = map(sem, ("y_summed", "z_done", "order", "turned", "hT_ready", "stored"))
    with ExitStack() as ctx:
        pt = [[ctx.enter_context(nc.psum_tensor(f"{L}_cpt{b}{h}", [P, 4, P], F32)) for h in range(2)] for b in range(2)]
        block = ctx.enter_context(nc.Block())

        @block.sync
        def _(sp):
            norm.load(sp, A[L + "_ln2_g"], A[L + "_ln2_b"])
            for i in range(1 if lastl else 0, NT):
                t0, m = TILES[i]
                sp.wait_ge(norm.h_ready, i + 1)
                out = K.out[t0 - N_META:t0 - N_META + m, :] if lastl else K.h2_dram[t0:t0 + m, :]
                sp.dma_start(out, K.H[0:m, i, :]).then_inc(stored, 16)
            sp.wait_ge(stored, 16 * (NT - 1 if lastl else NT))

        @block.vector
        def _(dve):
            do = Order(dve, order)
            for i in range(NT + 1):
                if i == NT:
                    norm.apply_gain(dve, i - 1)
                    break
                m = TILES[i][1]
                z = K.H[0:m, i, :]
                dve.wait_ge(y_summed, i + 1)
                dve.scalar_tensor_tensor(out=z, in0=z, scalar=ALPHA, in1=y0[i % YB][0:m, :], op0=ALU.mult, op1=ALU.add).then_inc(z_done, 1)
                dve.wait_ge(z_done, i + 1)
                norm.statistics(dve, do, i)
                if i:
                    norm.apply_gain(dve, i - 1)
                norm.scales(dve, do, i)

        @block.gpsimd
        def _(pool):
            def y_sum(i):
                m = TILES[i][1]
                pool.wait_ge(y_loaded[i % YB], 32 * (i // YB + 1))
                pool.tensor_tensor(y0[i % YB][0:m, :], y0[i % YB][0:m, :], y1[i % YB][0:m, :], ALU.add).then_inc(y_summed, 1)
            for i in range(3):
                y_sum(i)
            for i in range(NT - 1):
                norm.add_bias(pool, i)
                if i + 3 < NT:
                    y_sum(i + 3)

        @block.tensor
        def _(pe):
            if not lastl:
                for i in range(NT):
                    m = TILES[i][1]
                    pe.wait_ge(norm.h_ready, i + 1)
                    if i >= 2:
                        pe.wait_ge(hT_ready, 2 * (i - 1))
                    for k in range(KD):
                        last = pe.transpose(pt[i % 2][k // 4][:, k % 4, 0:m], K.H[0:m, i, P * k:P * k + P], K.ident[0:m, 0:m])
                    last.then_inc(turned, 1)

        @block.scalar
        def _(act):
            def load_y(i):
                t0, m = TILES[i]
                if i >= YB:
                    act.wait_ge(z_done, i - YB + 1)
                for k, y in enumerate((y0, y1)):
                    act.dma_start(y[i % YB][0:m, :], K.y_dram[k * T + t0:k * T + t0 + m, :]).then_inc(y_loaded[i % YB], 16)
            for i in range(YB):
                load_y(i)
            for i in range(NT + 2):
                if i < NT:
                    norm.act(act, i)
                if i + YB < NT:
                    load_y(i + YB)
                if i >= 2 and not lastl:
                    t0, m = TILES[i - 2]
                    act.wait_ge(turned, i - 1)
                    for h in range(2):
                        act.copy(K.hT[:, 4 * h:4 * h + 4, t0:t0 + m], pt[i % 2][h][:, :, 0:m]).then_inc(hT_ready, 1)


def rglru(nc, K, A):
    at = Place(nc, K.free_hT)
    K.y1T = at("y1T", [NB, T])
    K.free_y1T = at.at
    wide = Place(nc, K.h_at)
    wz = [at(f"lru_wz{i}", [KD, 2, P]) for i in range(2)]
    wax = [at(f"lru_wax{i}", [2, P]) for i in range(2)]
    rec, xc = [at(f"lru_rec{i}", [T + 3]) for i in range(2)], [at(f"lru_xc{i}", [T]) for i in range(2)]
    gg, ra, ii = wide("lru_gg", [T]), wide("lru_r", [T]), wide("lru_i", [T])
    a, t, v, u = wide("lru_a", [T]), wide("lru_t", [T]), wide("lru_v", [T]), wide("lru_u", [T])
    NPR = 9
    prm, pc = at("lru_prm", [NPR, NB]), at("lru_pc", [NPR])
    m0, m1, m2, m3 = (at(f"lru_m{i}", [NB]) for i in range(4))
    assert at.at <= K.w_out1_at
    sem = lambda n: K.sem("lru_" + n)
    loaded, w_loaded = sem("loaded"), [sem("w_loaded0"), sem("w_loaded1")]
    (order, z_exp, z_in, sp_done, prm_ready, rec_ready, rec_copied, gate_ready, gelu_done, xc_ready, ga_ready, sig_done,
     at_done, v_ready, s_done, y_done) = map(sem, (
        "order", "z_exp", "z_in", "sp_done", "prm_ready", "rec_ready", "rec_copied", "gate_ready", "gelu_done", "xc_ready",
        "ga_ready", "sig_done", "at_done", "v_ready", "s_done", "y_done"))
    w = A["l1_w_in"].rearrange("(k p) c -> p k c", p=P)
    NC = len(CHUNKS)
    with ExitStack() as ctx:
        pr = ctx.enter_context(nc.psum_tensor("lru_pr", [P, NC, 512], F32))
        pgt = ctx.enter_context(nc.psum_tensor("lru_pg", [P, NC, 512], F32))
        pa = [ctx.enter_context(nc.psum_tensor(f"lru_pa{i}", [P, 512], F32)) for i in range(2)]
        block = ctx.enter_context(nc.Block())

        def weights(sp, n, par):
            sp.dma_start(wz[par][:, :, 0, :], w[:, :, ds(n * P + D_RNN, P)]).then_inc(w_loaded[par], 16)
            sp.dma_start(wz[par][:, :, 1, :], w[:, :, ds(n * P, P)]).then_inc(w_loaded[par], 16)
            sp.dma_start(wax[par][:, 0, :], A["l1_lru_w_a"][ds(n, 1)].rearrange("a d e -> (a d) e")).then_inc(w_loaded[par], 16)
            sp.dma_start(wax[par][:, 1, :], A["l1_lru_w_x"][ds(n, 1)].rearrange("a d e -> (a d) e")).then_inc(w_loaded[par], 16)

        @block.sync
        def _(sp):
            with nc.allow_non_contiguous_dma(reason="parameters by channel"):
                for par in range(2):
                    weights(sp, par, par)
                load_w_out(sp, K, 1)
                for j in range(4):
                    sp.dma_start(prm[:, j, :], A["l1_conv_w"][j].rearrange("(n p) -> p n", p=P)).then_inc(loaded, 16)
                for j, nm in enumerate(("l1_conv_b", "l1_lru_b_a", "l1_lru_b_x", "l1_lru_lambda")):
                    sp.dma_start(prm[:, 4 + j, :], A[nm].rearrange("(n p) -> p n", p=P)).then_inc(loaded, 16)
                with sp.Fori(1, NB // 2) as i:
                    for par in range(2):
                        sp.wait_ge(ga_ready, (2 * i + par - 1) * 2 * NC)
                        weights(sp, 2 * i + par, par)

        def products(pe, i, n, par):
            pe.wait_ge(w_loaded[par], 64 * (i + 1))
            pe.wait_ge(rec_copied, 1 + NC * n)
            for j, (o, c) in enumerate(CHUNKS):
                for k in range(KD):
                    last = pe.matmul(pr[:, j, 0:c], wz[par][:, k, 0, :], K.hT[:, k, o:o + c], start=k == 0, stop=k == KD - 1)
                last.then_inc(rec_ready, 1)
            pe.wait_ge(gelu_done, 1 + NC * n)
            for j, (o, c) in enumerate(CHUNKS):
                for k in range(KD):
                    last = pe.matmul(pgt[:, j, 0:c], wz[par][:, k, 1, :], K.hT[:, k, o:o + c], start=k == 0, stop=k == KD - 1)
                last.then_inc(gate_ready, 1)
            pe.wait_ge(xc_ready, n + 1)
            for s in range(2 * NC):
                j, g = s // 2, s % 2
                o, c = CHUNKS[j]
                if s < 2:
                    pe.wait_ge(sig_done, 1 + 2 * NC * n)
                else:
                    pe.wait_ge(sig_done, 1 + 2 * NC * n + s - 1)
                pe.matmul(pa[s % 2][:, 0:c], wax[par][:, g, :], xc[par][:, o:o + c], start=True, stop=True).then_inc(ga_ready, 1)

        @block.tensor
        def _(pe):
            with pe.Fori(0, NB // 2) as i:
                for par in range(2):
                    products(pe, i, 2 * i + par, par)

        def acts(act, n, par):
            for j, (o, c) in enumerate(CHUNKS):
                act.wait_ge(rec_ready, NC * n + j + 1)
                act.copy(rec[par][:, 3 + o:3 + o + c], pr[:, j, 0:c]).then_inc(rec_copied, 1)
            act.wait_ge(y_done, 1 + n)
            for j, (o, c) in enumerate(CHUNKS):
                act.wait_ge(gate_ready, NC * n + j + 1)
                act.activation(gg[:, o:o + c], pgt[:, j, 0:c], ACT.Gelu_apprx_tanh).then_inc(gelu_done, 1)
            for s in range(2 * NC):
                j, g = s // 2, s % 2
                o, c = CHUNKS[j]
                act.wait_ge(ga_ready, 2 * NC * n + s + 1)
                act.activation((ra, ii)[g][:, o:o + c], pa[s % 2][:, 0:c], ACT.Sigmoid, bias=pc[:, 5 + g:6 + g]).then_inc(sig_done, 1)
            act.wait_ge(sig_done, 1 + 2 * NC * (n + 1))
            act.activation(t[:], ra[:], ACT.Tanh, scale=pc[:, 8:9]).then_inc(at_done, 1)
            act.activation(a[:], ra[:], ACT.Exp, scale=pc[:, 7:8]).then_inc(at_done, 1)
            act.wait_ge(v_ready, n + 1)
            act.activation(v[:], v[:], ACT.Sqrt).then_inc(s_done, 1)

        @block.scalar
        def _(act):
            for counted in (rec_copied, gelu_done, sig_done):
                act.sem_inc(counted, 1)
            act.wait_ge(z_in, 1)
            act.activation(m1[:], m1[:], ACT.Exp, scale=-1.0).then_inc(z_exp, 1)
            with act.Fori(0, NB // 2) as i:
                for par in range(2):
                    acts(act, 2 * i + par, par)

        def block_dve(dve, do, n, par):
            do(dve.tensor_copy(pc[:], prm[:, :, ds(n, 1)].rearrange("p a b -> p (a b)")))
            x, r = xc[par], rec[par]
            dve.wait_ge(rec_copied, 1 + NC * (n + 1))
            do(dve.tensor_scalar(x[:], r[:, 0:T], pc[:, 0:1], pc[:, 4:5], ALU.mult, ALU.add))
            for j in range(1, 4):
                ins = dve.scalar_tensor_tensor(out=x[:], in0=r[:, j:j + T], scalar=pc[:, j:j + 1], in1=x[:], op0=ALU.mult, op1=ALU.add)
                if j < 3:
                    do(ins)
                else:
                    ins.then_inc(xc_ready, 1)
            dve.wait_ge(sig_done, 1 + 2 * NC * (n + 1))
            dve.wait_ge(xc_ready, n + 1)
            do(dve.tensor_tensor(u[:], ii[:], x[:], ALU.mult), wait=False)
            dve.wait_ge(at_done, 2 * n + 1)
            do(dve.tensor_scalar(v[:], t[:], 1.0, None, ALU.add))
            do(dve.reciprocal(v[:], v[:]))
            dve.scalar_tensor_tensor(out=v[:], in0=t[:], scalar=2.0, in1=v[:], op0=ALU.mult, op1=ALU.mult).then_inc(v_ready, 1)
            dve.wait_ge(s_done, n + 1)
            dve.wait_ge(at_done, 2 * n + 2)
            do(dve.tensor_tensor(u[:], u[:], v[:], ALU.mult))
            do(dve.tensor_tensor_scan(t[:], a[:], u[:], 0.0, ALU.mult, ALU.add))
            dve.tensor_tensor(K.y1T[:, ds(n, 1), :].rearrange("p a t -> p (a t)"), t[:], gg[:], ALU.mult).then_inc(y_done, 1)

        @block.vector
        def _(dve):
            do = Order(dve, order)
            dve.sem_inc(y_done, 1)
            for par in range(2):
                do(dve.memset(rec[par][:, 0:3], 0.0), wait=False)
            dve.wait_ge(loaded, 8 * 16)
            lam = prm[:, 7, :]
            do(dve.tensor_scalar(m0[:], lam, -1.0, None, ALU.mult))
            dve.tensor_tensor(m1[:], m0[:], lam, ALU.max).then_inc(z_in, 1)
            dve.wait_ge(z_exp, 1)
            do(dve.tensor_scalar(m2[:], m1[:], 2.0, None, ALU.add))
            do(dve.reciprocal(m2[:], m2[:]))
            do(dve.tensor_tensor(m1[:], m1[:], m2[:], ALU.mult))
            do(dve.tensor_tensor(m2[:], m1[:], m1[:], ALU.mult))
            do(dve.memset(m3[:], 1.0 / 21))
            for k in range(9, -1, -1):
                do(dve.tensor_tensor(m3[:], m3[:], m2[:], ALU.mult))
                do(dve.tensor_scalar(m3[:], m3[:], 1.0 / (2 * k + 1), None, ALU.add))
            do(dve.tensor_tensor(m3[:], m3[:], m1[:], ALU.mult))
            do(dve.tensor_scalar(m0[:], m0[:], 0.0, None, ALU.max))
            do(dve.scalar_tensor_tensor(out=m3[:], in0=m3[:], scalar=2.0, in1=m0[:], op0=ALU.mult, op1=ALU.add))
            do(dve.tensor_scalar(prm[:, 8, :], m3[:], 8.0, None, ALU.mult), wait=False)
            do(dve.tensor_scalar(prm[:, 7, :], m3[:], -8.0, None, ALU.mult))
            block_per = 9
            with dve.Fori(0, NB // 2) as i:
                do.enter(i, 2 * block_per)
                for par in range(2):
                    block_dve(dve, do, 2 * i + par, par)
                do.leave(NB // 2)
            dve.wait_ge(y_done, 1 + NB)


INPUTS = (
    "x", "meta", "l0_ln1_g", "l0_ln1_b", "l0_w_in", "l0_s5_lambda_re", "l0_s5_lambda_im", "l0_s5_log_dt", "l0_s5_b_re",
    "l0_s5_b_im", "l0_s5_c_re", "l0_s5_c_im", "l0_s5_d", "l0_s5_w_glu", "l0_s5_b_glu", "l0_da_lq1", "l0_da_lk1",
    "l0_da_lq2", "l0_da_lk2", "l0_da_subln_g", "l0_w_out", "l0_ln2_g", "l0_ln2_b", "l0_moe_w_coarse",
    "l0_moe_b_coarse", "l0_moe_w_fine", "l0_moe_b_fine", "l0_moe_w_gate", "l0_moe_w_up", "l0_moe_w_down", "l1_ln1_g",
    "l1_ln1_b", "l1_w_in", "l1_conv_w", "l1_conv_b", "l1_lru_w_a", "l1_lru_b_a", "l1_lru_w_x", "l1_lru_b_x",
    "l1_lru_lambda", "l1_w_out", "l1_ln2_g", "l1_ln2_b", "l1_moe_w_coarse", "l1_moe_b_coarse", "l1_moe_w_fine",
    "l1_moe_b_fine", "l1_moe_w_gate", "l1_moe_w_up", "l1_moe_w_down")


class Kept:

    def __init__(self, nc):
        self.nc, self.sems = nc, []

    def sem(self, name):
        self.sems.append(self.nc.alloc_semaphore(name))
        return self.sems[-1]

    def end_phase(self):
        self.nc.clear_and_free_semaphores(self.sems)
        self.nc.all_engine_barrier()
        self.sems = []


def hybrid_block_kernel(nc, A, out):
    K = Kept(nc)
    K.A = A
    K.out = out.rearrange("a b d -> (a b) d")
    scratch = lambda n, rows: nc.dram_tensor(n, [rows, D], F32, kind="Internal").ap()
    K.h1_dram, K.h2_dram, K.y_dram = scratch("h1_rows", T), scratch("h2_rows", T), scratch("expert_rows", 2 * T)
    at = Place(nc, nc.sbuf_base)
    K.ident, K.logits = at("ident", [P]), at("logits", [NT, 36])
    K.tok_idx, K.row_idx, K.gates = at("tok_idx", [NBLK], U32), at("row_idx", [NBLK], U32), at("gates", [NBLK])
    K.over = at("over", [NOVER + 1], I32)
    K.base = at.at
    H_BYTES = NT * D * 4
    K.h_at = (nc.sbuf_usable_end - H_BYTES) // 32 * 32
    K.H = nc.alloc_sbuf_tensor_at("H", [P, NT, D], F32, offset=K.h_at)
    W_BYTES = [KD * D * 4, NB * D * 4]
    K.w_out0_at, K.w_out1_at = ((K.h_at - w) // 32 * 32 for w in W_BYTES)
    K.w_out = [Place(nc, K.w_out0_at)("w_out0", [KD, D]), Place(nc, K.w_out1_at)("w_out1", [NB, D])]
    K.w_out_loaded = [nc.alloc_semaphore(f"w_out{i}_loaded") for i in range(2)]

    at = Place(nc, K.base)
    K.yT = at("yT", [4, T])
    K.free_s5 = at.at
    K.s5_d, K.mag, K.s5_zero = at("s5_d", [4]), at("mag", [S5_PAIRS]), at("s5_zero", [1])
    K.b_lhs, K.c_lhs = at("b_lhs", [2, 4, 4, P]), at("c_lhs", [2, 4, P])
    K.cs, K.sn = at("cs", [S5_PAIRS, WIN + 1]), at("sn", [S5_PAIRS, WIN + 1])
    K.free_zt = at.at
    K.zT = at("zT", [12, T])
    K.free_loop = at.at
    K.w_in = at("w_in", [KD, 2048])
    K.w_in_loaded = [nc.alloc_semaphore(f"w_in_loaded{c}") for c in range(4)]
    K.free_w_in = at.at
    make_constants(nc, K)
    K.end_phase()
    s5_prepare(nc, K, A)
    K.end_phase()
    s5_and_projections(nc, K, A)
    K.end_phase()
    s5_gate(nc, K, A)
    K.end_phase()
    attention(nc, K, A)
    K.end_phase()
    x, meta = A["x"].rearrange("a b d -> (a b) d"), A["meta"]
    rows0 = lambda i: meta if i == 0 else x[P * (i - 1):P * i, :]
    slices = [K.yT[:, k, :] for k in range(4)] + [K.daT[:, k, :] for k in range(HEADS)]
    project_and_norm(nc, K, A, 0, slices, Place(nc, K.free_zt), rows0)
    K.end_phase()
    route(nc, K, 0)
    K.end_phase()
    experts(nc, K, A, 0)
    K.end_phase()
    combine_and_norm(nc, K, A, 0)
    K.end_phase()

    K.free_hT = K.base + KD * T * 4
    rglru(nc, K, A)
    K.end_phase()
    rows1 = lambda i: K.h2_dram[TILES[i][0]:TILES[i][0] + TILES[i][1], :]
    project_and_norm(nc, K, A, 1, [K.y1T[:, k, :] for k in range(NB)], Place(nc, K.base), rows1)
    K.end_phase()
    route(nc, K, 1)
    K.end_phase()
    experts(nc, K, A, 1)
    K.end_phase()
    combine_and_norm(nc, K, A, 1)


def kernel(**inputs):
    import concourse.bacc as bacc
    from concourse.bass_utils import run_bass_kernel_spmd

    nc = bacc.Bacc("TRN2", target_bir_lowering=False, num_devices=1)
    arrays, A = {}, {}
    for name in INPUTS:
        a = np.ascontiguousarray(inputs[name])
        arrays[f"in_{name}"] = a
        A[name] = nc.dram_tensor(f"in_{name}", a.shape, mybir.dt.from_np(a.dtype), kind="ExternalInput").ap()
    out = nc.dram_tensor("out", (1, SEQ, D), F32, kind="ExternalOutput").ap()
    hybrid_block_kernel(nc, A, out)
    r = run_bass_kernel_spmd(nc, [arrays], core_ids=[0])
    return r.results[0]["out"]
```
